# Optimizing a Trainium2 kernel written in Bass

```python
import math
import jax, jax.numpy as jnp
from jax import lax
import numpy as np

D_MODEL = 1024
BATCH = 1
SEQ = 512
DEPTH = 2

N_BRANCH = 4
BRANCH_WIDTH = D_MODEL // 2
POOL_WINDOWS = (2, 4, 8, 16)
POOL_GROUPS = len(POOL_WINDOWS)
POOL_GROUP_DIM = BRANCH_WIDTH // POOL_GROUPS
HGRN_HEAD_DIM = 128
HGRN_HEADS = BRANCH_WIDTH // HGRN_HEAD_DIM
HGRN_CHUNK = 64
GMLP_CHUNK = 128
GMLP_GROUPS = 4
GMLP_GROUP_DIM = BRANCH_WIDTH // GMLP_GROUPS
FOX_HEAD_DIM = 128
FOX_HEADS = BRANCH_WIDTH // FOX_HEAD_DIM
FOX_BLOCK = 128
N_IN = BRANCH_WIDTH * (1 + 4 + 2 + 3) + FOX_HEADS
PEER_HEADS = 8
PEER_N_KEYS = 128
PEER_N_EXPERTS = PEER_N_KEYS * PEER_N_KEYS
PEER_TOPK = 16
PEER_QUERY_DIM = 256
PEER_HALF = PEER_QUERY_DIM // 2
PEER_BLOCK = 128
ALPHA = (2.0 * DEPTH) ** 0.25
BETA = (8.0 * DEPTH) ** -0.25
LN_EPS = 1e-5
RMS_EPS = 1e-6
NEG_BIG = -1e30

kernel_name = "hybrid_pool_hgrn2_gmlp_fox_peer_deepnorm"

def layer_norm(x, g, b):
    xf = x.astype(jnp.float32)
    mu = jnp.mean(xf, -1, keepdims=True)
    var = jnp.mean(jnp.square(xf - mu), -1, keepdims=True)
    return ((xf - mu) * lax.rsqrt(var + LN_EPS) * g + b).astype(x.dtype)

def rms_norm(x, g):
    xf = x.astype(jnp.float32)
    return xf * lax.rsqrt(jnp.mean(jnp.square(xf), -1, keepdims=True) + RMS_EPS) * g

def pool_mixer(p, pool_w, pool_scale):
    B, S, _ = p.shape
    pf = p.astype(jnp.float32)
    cs = jnp.cumsum(pf, axis=1)
    cs = jnp.concatenate([jnp.zeros_like(cs[:, :1]), cs], axis=1)
    t1 = jnp.arange(1, S + 1, dtype=jnp.float32)[None, :, None]
    outs = []
    for g, w in enumerate(POOL_WINDOWS):
        sl = slice(g * POOL_GROUP_DIM, (g + 1) * POOL_GROUP_DIM)
        cg = cs[..., sl]
        lo = jnp.pad(cg[:, :S + 1 - w], ((0, 0), (w - 1, 0), (0, 0)))
        mean = (cg[:, 1:] - lo) / jnp.minimum(t1, float(w))
        outs.append(mean - pf[..., sl])
    d = jnp.stack(outs, axis=2).astype(p.dtype)
    y = jnp.einsum('bsgc,gcd->bsgd', d, pool_w).reshape(B, S, BRANCH_WIDTH)
    return y * pool_scale

def hgrn2_mixer(q, f_raw, i, g, lb, norm_g):
    B, S, _ = q.shape
    H, Dh, C = HGRN_HEADS, HGRN_HEAD_DIM, HGRN_CHUNK
    n = S // C
    zf = f_raw.astype(jnp.float32)
    k = (1.0 - lb) * jax.nn.sigmoid(-zf)
    log_f = jnp.log1p(-k)

    def chunks(z):
        return z.astype(jnp.float32).reshape(B, n, C, H, Dh).transpose(1, 0, 3, 2, 4)

    mask = jnp.tril(jnp.ones((C, C), bool))[None, None, :, :, None]

    def step(state, inp):
        qc, kc, vc, lc = inp
        b = jnp.cumsum(lc, axis=2)
        o_inter = jnp.einsum('bhtk,bhkv->bhtv', qc * jnp.exp(b), state)
        diff = b[:, :, :, None, :] - b[:, :, None, :, :]
        decay = jnp.exp(jnp.where(mask, diff, NEG_BIG))
        a = jnp.einsum('bhtk,bhtsk,bhsk->bhts', qc, decay, kc)
        o = o_inter + jnp.einsum('bhts,bhsv->bhtv', a, vc)
        b_last = b[:, :, -1:, :]
        new_state = jnp.exp(b_last[:, :, 0, :, None]) * state + jnp.einsum(
            'bhsk,bhsv->bhkv', kc * jnp.exp(b_last - b), vc)
        return new_state, o

    s0 = jnp.zeros((B, H, Dh, Dh), jnp.float32)
    _, o = lax.scan(step, s0, (chunks(jax.nn.silu(q.astype(jnp.float32))), chunks(k), chunks(i), chunks(log_f)))
    o = o.transpose(1, 0, 3, 2, 4).reshape(B, S, H, Dh)
    o = rms_norm(o, norm_g).reshape(B, S, BRANCH_WIDTH)
    return (o * jax.nn.silu(g.astype(jnp.float32))).astype(q.dtype)

def gmlp_mixer(u, v, ln_g, ln_b, ws, bs):
    B, S, _ = u.shape
    n = S // GMLP_CHUNK
    u = jax.nn.gelu(u)
    v = layer_norm(jax.nn.gelu(v), ln_g, ln_b)
    vc = v.reshape(B, n, GMLP_CHUNK, GMLP_GROUPS, GMLP_GROUP_DIM)
    ws_causal = ws * jnp.tril(jnp.ones((GMLP_CHUNK, GMLP_CHUNK), ws.dtype))
    s = jnp.einsum('gts,bnsgc->bntgc', ws_causal, vc) + bs.T[None, None, :, :, None]
    return u * s.reshape(B, S, BRANCH_WIDTH)

def fox_mixer(q, k, v, f_logit):
    B, S, _ = q.shape
    H, Dh, Bq = FOX_HEADS, FOX_HEAD_DIM, FOX_BLOCK
    nb = S // Bq
    c = jnp.cumsum(jax.nn.log_sigmoid(f_logit.astype(jnp.float32)), axis=1).transpose(0, 2, 1)
    qh = q.reshape(B, S, H, Dh).transpose(0, 2, 1, 3) * (Dh ** -0.5)
    kh = k.reshape(B, S, H, Dh).transpose(0, 2, 1, 3)
    vh = v.reshape(B, S, H, Dh).transpose(0, 2, 1, 3)
    qb = qh.reshape(B, H, nb, Bq, Dh).transpose(2, 0, 1, 3, 4)
    cb = c.reshape(B, H, nb, Bq).transpose(2, 0, 1, 3)
    pos_k = jnp.arange(S)

    def block(args):
        qi, ci, blk = args
        pos_q = blk * Bq + jnp.arange(Bq)
        logits = jnp.einsum('bhtd,bhsd->bhts', qi.astype(jnp.float32), kh.astype(jnp.float32))
        logits = logits + ci[..., None] - c[:, :, None, :]
        logits = jnp.where(pos_q[:, None] >= pos_k[None, :], logits, NEG_BIG)
        p = jax.nn.softmax(logits, axis=-1)
        return jnp.einsum('bhts,bhsd->bhtd', p.astype(vh.dtype), vh)

    o = lax.map(block, (qb, cb, jnp.arange(nb)))
    return o.transpose(1, 0, 3, 2, 4).reshape(B, S, BRANCH_WIDTH)

def token_mixer_block(x, w_in, b_fox_f, pool_w, pool_scale, lb, hgrn_norm_g,
                      gmlp_ln_g, gmlp_ln_b, gmlp_ws, gmlp_bs, w_gate, b_gate, w_branch, w_out):
    B, S, D = x.shape
    W = BRANCH_WIDTH
    h = jnp.einsum('bsd,dn->bsn', x, w_in)
    splits = [W * j for j in range(1, 11)]
    (p_in, hq, hf, hi, hg, gu, gv, fq, fk, fv, ff) = jnp.split(h, splits, axis=-1)
    a = pool_mixer(p_in, pool_w, pool_scale)
    b = hgrn2_mixer(hq, hf, hi, hg, lb, hgrn_norm_g)
    c = gmlp_mixer(gu, gv, gmlp_ln_g, gmlp_ln_b, gmlp_ws, gmlp_bs)
    d = fox_mixer(fq, fk, fv, ff + b_fox_f)
    br = jnp.stack([a, b, c, d], axis=2)
    gates = jax.nn.sigmoid(jnp.einsum('bsd,dn->bsn', x, w_gate) + b_gate).reshape(B, S, N_BRANCH, D)
    merged = jnp.einsum('bsmw,mwd,bsmd->bsd', br, w_branch, gates)
    return jnp.einsum('bsd,de->bse', merged, w_out)

def peer_ffn(x, wq, keys, u_tab, v_tab):
    B, S, D = x.shape
    T = B * S
    xt = x.reshape(T, D)
    q = jnp.einsum('td,dn->tn', xt, wq).reshape(T, PEER_HEADS, 2, PEER_HALF).astype(jnp.float32)
    s1 = jnp.einsum('thd,hkd->thk', q[:, :, 0], keys[0].astype(jnp.float32))
    s2 = jnp.einsum('thd,hkd->thk', q[:, :, 1], keys[1].astype(jnp.float32))
    v1, i1 = lax.top_k(s1, PEER_TOPK)
    v2, i2 = lax.top_k(s2, PEER_TOPK)
    cand = (v1[..., :, None] + v2[..., None, :]).reshape(T, PEER_HEADS, PEER_TOPK * PEER_TOPK)
    cidx = (i1[..., :, None] * PEER_N_KEYS + i2[..., None, :]).reshape(T, PEER_HEADS, PEER_TOPK * PEER_TOPK)
    top_s, pos = lax.top_k(cand, PEER_TOPK)
    eidx = jnp.take_along_axis(cidx, pos, axis=-1)
    gate = jax.nn.softmax(top_s, axis=-1).astype(x.dtype)
    nblk = T // PEER_BLOCK

    def blk(args):
        xb, eb, gb = args
        hidden = jax.nn.gelu(jnp.einsum('td,thkd->thk', xb, u_tab[eb]))
        return jnp.einsum('thk,thkd->td', gb * hidden, v_tab[eb])

    y = lax.map(blk, (xt.reshape(nblk, PEER_BLOCK, D),
                      eidx.reshape(nblk, PEER_BLOCK, PEER_HEADS, PEER_TOPK),
                      gate.reshape(nblk, PEER_BLOCK, PEER_HEADS, PEER_TOPK)))
    return y.reshape(B, S, D)

def setup_inputs(seed: int = 0) -> dict:
    key = jax.random.key(seed)
    ks = jax.random.split(key, 24)
    f32 = jnp.float32
    L, D, W = DEPTH, D_MODEL, BRANCH_WIDTH

    def nrm(k, shape, scale):
        return jax.random.normal(k, shape, f32) * scale

    return {
        "x": nrm(ks[0], (BATCH, SEQ, D), 1.0),
        "w_in": nrm(ks[1], (L, D, N_IN), D ** -0.5),
        "b_fox_f": nrm(ks[2], (L, FOX_HEADS), 0.1),
        "pool_w": nrm(ks[3], (L, POOL_GROUPS, POOL_GROUP_DIM, POOL_GROUP_DIM), POOL_GROUP_DIM ** -0.5),
        "pool_scale": 1.0 + nrm(ks[4], (L, W), 0.02),
        "hgrn_lb_logits": nrm(ks[5], (L, W), 0.1),
        "hgrn_norm_g": 1.0 + nrm(ks[6], (L, HGRN_HEAD_DIM), 0.02),
        "gmlp_ln_g": 1.0 + nrm(ks[7], (L, W), 0.02),
        "gmlp_ln_b": nrm(ks[8], (L, W), 0.02),
        "gmlp_ws": nrm(ks[9], (L, GMLP_GROUPS, GMLP_CHUNK, GMLP_CHUNK), 0.02),
        "gmlp_bs": 1.0 + nrm(ks[10], (L, GMLP_GROUPS, GMLP_CHUNK), 0.01),
        "w_gate": nrm(ks[11], (L, D, N_BRANCH * D), D ** -0.5),
        "b_gate": nrm(ks[12], (L, N_BRANCH * D), 0.02),
        "w_branch": nrm(ks[13], (L, N_BRANCH, W, D), BETA * W ** -0.5),
        "w_out": nrm(ks[14], (L, D, D), BETA * D ** -0.5),
        "ln1_g": 1.0 + nrm(ks[15], (L, D), 0.02),
        "ln1_b": nrm(ks[16], (L, D), 0.02),
        "peer_wq": nrm(ks[17], (L, D, PEER_HEADS * PEER_QUERY_DIM), D ** -0.5),
        "peer_keys": nrm(ks[18], (L, 2, PEER_HEADS, PEER_N_KEYS, PEER_HALF), PEER_HALF ** -0.5),
        "peer_u": nrm(ks[19], (L, PEER_N_EXPERTS, D), D ** -0.5),
        "peer_v": nrm(ks[20], (L, PEER_N_EXPERTS, D), BETA),
        "ln2_g": 1.0 + nrm(ks[21], (L, D), 0.02),
        "ln2_b": nrm(ks[22], (L, D), 0.02),
    }

def reference(x, w_in, b_fox_f, pool_w, pool_scale, hgrn_lb_logits, hgrn_norm_g, gmlp_ln_g, gmlp_ln_b,
              gmlp_ws, gmlp_bs, w_gate, b_gate, w_branch, w_out, ln1_g, ln1_b, peer_wq, peer_keys,
              peer_u, peer_v, ln2_g, ln2_b):
    p_lb = jax.nn.softmax(hgrn_lb_logits.astype(jnp.float32), axis=0)
    lower_bounds = jnp.cumsum(p_lb, axis=0) - p_lb[0]
    for l in range(DEPTH):
        mix = token_mixer_block(x, w_in[l], b_fox_f[l], pool_w[l], pool_scale[l], lower_bounds[l],
                                hgrn_norm_g[l], gmlp_ln_g[l], gmlp_ln_b[l], gmlp_ws[l], gmlp_bs[l],
                                w_gate[l], b_gate[l], w_branch[l], w_out[l])
        x = layer_norm(ALPHA * x + mix, ln1_g[l], ln1_b[l])
        ffn = peer_ffn(x, peer_wq[l], peer_keys[l], peer_u[l], peer_v[l])
        x = layer_norm(ALPHA * x + ffn, ln2_g[l], ln2_b[l])
    return x


_drawn_inputs = setup_inputs


def setup_inputs(seed=0):
    import zlib

    import numpy as np

    out = dict(_drawn_inputs(seed))
    spreads = {}
    factors = {'b_fox_f': 3.092,
     'pool_scale': 3.573,
     'hgrn_lb_logits': 8.0,
     'hgrn_norm_g': 4.133,
     'gmlp_ln_g': 29.332,
     'gmlp_ln_b': 29.96,
     'gmlp_bs': 14.59,
     'b_gate': 4.354}
    for name, (base, spread) in spreads.items():
        noise = np.random.default_rng([zlib.crc32(name.encode()), seed]).standard_normal(out[name].shape)
        drawn = base * np.exp(spread * noise) if base else spread * noise
        out[name] = __import__('jax').numpy.asarray(drawn.astype(out[name].dtype))
    for name, factor in factors.items():
        out[name] = (out[name] * factor).astype(out[name].dtype)
    return out
```

```python
import math
from contextlib import ExitStack

import concourse.bass as bass
from concourse import mybir

F32 = mybir.dt.float32
U32 = mybir.dt.uint32
ALU = mybir.AluOpType
ACT = mybir.ActivationFunctionType
AX = mybir.AxisListType.X
ds = bass.ds

P = 128
D_MODEL = 1024
SEQ = 512
DEPTH = 2
KT = D_MODEL // P
NT = SEQ // P
W = D_MODEL // 2
WT = W // P
POOL_WINDOWS = (2, 4, 8, 16)
PEER_HEADS = 8
TOPK = 16
PAIRS = PEER_HEADS * TOPK
N_LISTS = 2 * PEER_HEADS
ALPHA = (2.0 * DEPTH) ** 0.25
LN_EPS = 1e-5
RMS_EPS = 1e-6
NEG_BIG = -1e30
LOWEST = -3.0e38
FOX_SCALE = float(P) ** -0.5
LEVELS = (64, 32, 16, 8)
DIAG = 8
EC = 4
NG = P // EC
TB = 64
NTB = SEQ // TB

T_POOL, T_HQ, T_HF, T_GU, T_FQ, T_FK = range(6)
N_HI, N_HG, N_GV, N_FV = range(4)
W_IN_ORDER = (0, 1, 2, 5, 7, 8, 3, 4, 6, 9)


def make_link(eng, sem, start=0):
    done = [0]

    def link(ins):
        done[0] += 1
        ins.then_inc(sem, 1)
        eng.wait_ge(sem, start + done[0])

    link.done = done
    return link


def build_program(nc, a):
    with ExitStack() as whole:
        sems = {}

        def sem(name):
            if name not in sems:
                sems[name] = whole.enter_context(nc.semaphore(name))
            return sems[name]

        def sb(ctx, name, shape, dt=F32):
            return ctx.enter_context(nc.sbuf_tensor(name, shape, dt))

        bank = [whole.enter_context(nc.psum_tensor(f"bank{i}", [P, 512], F32)) for i in range(8)]

        x_tok = sb(whole, "x_tok", [P, NT, D_MODEL])
        xT = sb(whole, "xT", [P, KT, SEQ])
        ident = sb(whole, "ident", [P, P])
        iota_row = sb(whole, "iota_row", [P, P])
        lvl_mask = sb(whole, "lvl_mask", [P, len(LEVELS) + 1, P])
        neg_mask = sb(whole, "neg_mask", [P, P])
        head_sel = sb(whole, "head_sel", [WT, WT, P])
        pool_rc = sb(whole, "pool_rc", [P, WT, 16])
        scan_keep = sb(whole, "scan_keep", [P, SEQ])
        one_minus_lb = sb(whole, "one_minus_lb", [P, DEPTH, WT])

        s_const = sem("const_done")
        s_chain_v = sem("dve_chain")
        s_chain_a = sem("act_chain")
        s_chain_p = sem("pool_chain")

        def norm_stage(tag, layer, summed, psum_halves, load_g, load_b, out_dram=None, weights=None):
            with ExitStack() as ctx:
                g_row = sb(ctx, f"{tag}_g", [P, D_MODEL])
                b_row = sb(ctx, f"{tag}_b", [P, D_MODEL])
                r = sb(ctx, f"{tag}_r", [P, 2, D_MODEL])
                stats = sb(ctx, f"{tag}_stats", [P, 2, 2, 6])
                mv = sb(ctx, f"{tag}_mv", [P, NT, 2])
                std = sb(ctx, f"{tag}_std", [P, NT])
                rstd = sb(ctx, f"{tag}_rstd", [P, NT])
                rows_in = sem(f"{tag}_rows_in")
                w_loaded = sem(f"{tag}_w_loaded")
                sum_ready = sem(f"{tag}_sum_ready")
                sum_used = sem(f"{tag}_sum_used")
                var_ready = sem(f"{tag}_var_ready")
                std_ready = sem(f"{tag}_std_ready")
                x_ready = sem(f"{tag}_x_ready")
                turned = sem(f"{tag}_turned")
                copied = sem(f"{tag}_copied")
                chain = sem(f"{tag}_chain")
                with nc.Block() as block:

                    @block.sync
                    def _(sp):
                        sp.dma_start(g_row[:], load_g).then_inc(rows_in, 16)
                        sp.dma_start(b_row[:], load_b).then_inc(rows_in, 16)
                        if weights:
                            sp.dma_start(weights[0][:], weights[1]).then_inc(w_loaded, 16)

                    @block.tensor
                    def _(pe):
                        def project(t):
                            for half in range(2):
                                if t >= 2:
                                    pe.wait_ge(sum_used, 2 * (t - 2) + half + 1)
                                for k in range(KT):
                                    mm = nc.tensor.matmul(bank[2 * (t % 2) + half][:], weights[2][:, k, t * P:(t + 1) * P],
                                                          weights[0][:, k, half * 512:(half + 1) * 512],
                                                          start=(k == 0), stop=(k == KT - 1))
                                mm.then_inc(sum_ready, 1)

                        def turn(t):
                            pe.wait_ge(x_ready, t + 1)
                            for half in range(2):
                                if t >= 2:
                                    pe.wait_ge(copied, 2 * (t - 2) + half + 1)
                                for q in range(4):
                                    k = 4 * half + q
                                    tr = nc.tensor.transpose(bank[4 + 2 * (t % 2) + half][:, q * P:(q + 1) * P],
                                                             x_tok[:, t, k * P:(k + 1) * P], ident[:])
                                tr.then_inc(turned, 1)

                        if weights:
                            pe.wait_ge(w_loaded, 16)
                            project(0)
                        for t in range(NT):
                            if weights and t + 1 < NT:
                                project(t + 1)
                            turn(t)

                    @block.vector
                    def _(dve):
                        link = make_link(dve, chain)
                        for t in range(NT):
                            rt = r[:, t % 2, :]
                            for half in range(2):
                                cols = slice(half * 512, (half + 1) * 512)
                                if weights:
                                    dve.wait_ge(sum_ready, 2 * t + half + 1)
                                    other = bank[2 * (t % 2) + half][:]
                                else:
                                    other = summed[:, t, cols]
                                ins = nc.vector.scalar_tensor_tensor(out=rt[:, cols], in0=x_tok[:, t, cols], scalar=ALPHA,
                                                                     in1=other, op0=ALU.mult, op1=ALU.add)
                                ins.then_inc(sum_used, 1)
                                dve.wait_ge(sum_used, 2 * t + half + 1)
                                link(nc.vector.bn_stats(stats[:, t % 2, half, :], rt[:, cols]))
                            link(nc.vector.bn_aggr(mv[:, t, :], stats[:, t % 2, :, :]))
                            link(nc.vector.tensor_scalar(rstd[:, t:t + 1], mv[:, t, 1:2], LN_EPS, None, ALU.add))
                            nc.vector.tensor_copy(std[:, t:t + 1], rstd[:, t:t + 1]).then_inc(var_ready, 1)
                            dve.wait_ge(std_ready, t + 1)
                            link(nc.vector.reciprocal(rstd[:, t:t + 1], std[:, t:t + 1]))
                            link(nc.vector.tensor_scalar(rt, rt, mv[:, t, 0:1], rstd[:, t:t + 1], ALU.subtract, ALU.mult))
                            if t == 0:
                                dve.wait_ge(rows_in, 32)
                            link(nc.vector.tensor_tensor(rt, rt, g_row[:], ALU.mult))
                            nc.vector.tensor_tensor(x_tok[:, t, :], rt, b_row[:], ALU.add).then_inc(x_ready, 1)

                    @block.scalar
                    def _(act):
                        def copy_out(t):
                            for half in range(2):
                                act.wait_ge(turned, 2 * t + half + 1)
                                nc.scalar.activation(xT[:, 4 * half:4 * half + 4, t * P:(t + 1) * P],
                                                     bank[4 + 2 * (t % 2) + half][:].rearrange("p (q n) -> p q n", q=4),
                                                     ACT.Copy).then_inc(copied, 1)
                        for t in range(NT):
                            act.wait_ge(var_ready, t + 1)
                            nc.scalar.activation(std[:, t:t + 1], std[:, t:t + 1], ACT.Sqrt).then_inc(std_ready, 1)
                            if t >= 1:
                                copy_out(t - 1)
                        copy_out(NT - 1)

        def project_stage(tag, w_dram, pairs_T, dst_T, pairs_N=0, dst_N=None, small=None):
            with ExitStack() as ctx:
                wbuf = sb(ctx, f"{tag}_w", [P, 2, KT, 512])
                loaded = [sem(f"{tag}_w_loaded{b}") for b in range(2)]
                mm_done = sem(f"{tag}_mm_done")
                kept_a = sem(f"{tag}_kept_a")
                kept_v = sem(f"{tag}_kept_v")
                small_in = sem(f"{tag}_small_in")
                with nc.Block() as block:

                    @block.sync
                    def _(sp):
                        if small:
                            sp.dma_start(small[0][:], small[1]).then_inc(small_in, 16)
                        with sp.Fori(0, pairs_T + pairs_N) as i:
                            for b in range(2):
                                sp.wait_ge(mm_done, 8 * i + 4 * b + 4)
                                sp.dma_start(wbuf[:, b], w_dram(2 * i + b)).then_inc(loaded[b], 16)

                    @block.tensor
                    def _(pe):
                        pe.sem_inc(mm_done, 8)

                        def pair(i, token_major):
                            for b in range(2):
                                pe.wait_ge(loaded[b], 16 * i + 16)
                                for q in range(4):
                                    n = 4 * b + q
                                    pe.wait_ge((kept_a, kept_v)[n % 2], 4 * i + n // 2 + 1)
                                    for k in range(KT):
                                        if token_major:
                                            mm = nc.tensor.matmul(bank[n][:], xT[:, k, q * P:(q + 1) * P], wbuf[:, b, k, :],
                                                                  start=(k == 0), stop=(k == KT - 1))
                                        else:
                                            mm = nc.tensor.matmul(bank[n][:], wbuf[:, b, k, q * P:(q + 1) * P], xT[:, k, :],
                                                                  start=(k == 0), stop=(k == KT - 1))
                                    mm.then_inc(mm_done, 1)

                        with pe.Fori(0, pairs_T) as i:
                            pair(i, False)
                        if pairs_N:
                            with pe.Fori(pairs_T, pairs_T + pairs_N) as i:
                                pair(i, True)
                        if small:
                            n_pairs = pairs_T + pairs_N
                            pe.wait_ge(small_in, 16)
                            pe.wait_ge(kept_a, 4 * n_pairs + 1)
                            for k in range(KT):
                                mm = nc.tensor.matmul(bank[0][0:WT, :], small[0][:, k, :], xT[:, k, :],
                                                      start=(k == 0), stop=(k == KT - 1))
                            mm.then_inc(mm_done, 1)

                    def keep(eng, copy, kept, parity):
                        eng.sem_inc(kept, 4)

                        def pair(i, dst, first):
                            for n in range(parity, 8, 2):
                                eng.wait_ge(mm_done, 8 * i + n + 9)
                                copy(dst[:, 2 * (i - first) + n // 4, n % 4, :], bank[n][:]).then_inc(kept, 1)

                        with eng.Fori(0, pairs_T) as i:
                            pair(i, dst_T, 0)
                        if pairs_N:
                            with eng.Fori(pairs_T, pairs_T + pairs_N) as i:
                                pair(i, dst_N, pairs_T)

                    @block.scalar
                    def _(act):
                        keep(act, lambda o, i: nc.scalar.activation(o, i, ACT.Copy), kept_a, 0)

                    @block.vector
                    def _(dve):
                        keep(dve, lambda o, i: nc.vector.tensor_copy(o, i), kept_v, 1)
                        if small:
                            dve.wait_ge(mm_done, 8 * (pairs_T + pairs_N) + 9)
                            nc.vector.tensor_copy(small[2][:], bank[0][0:WT, :]).then_inc(kept_v, 1)

        with ExitStack() as ctx:
            lbl = sb(ctx, "lb_logits", [P, DEPTH, WT])
            lb_work = sb(ctx, "lb_work", [P, 4, WT])
            lb_exp = sb(ctx, "lb_exp", [P, DEPTH, WT])
            x_in = sem("x_in")
            lb_in = sem("lb_in")
            turned0 = sem("turned0")
            copied0 = sem("copied0")
            lb_shift = sem("lb_shift")
            lb_expd = sem("lb_expd")
            rc_seed = sem("rc_seed")
            with nc.Block() as block:

                @block.sync
                def _(sp):
                    sp.dma_start(x_tok[:], a["x"].rearrange("o (t p) d -> p (o t) d", p=P)).then_inc(x_in, 16)
                    sp.dma_start(lbl[:], a["hgrn_lb_logits"]).then_inc(lb_in, 16)

                @block.gpsimd
                def _(pool):
                    link = make_link(pool, s_chain_p)
                    link(nc.gpsimd.memset(ident[:], 0.0))
                    nc.gpsimd.affine_select(out=ident[:], in_=ident[:], compare_op=ALU.not_equal, fill=1.0, base=0,
                                            pattern=[[-1, P]], channel_multiplier=1).then_inc(s_const, 1)
                    nc.gpsimd.iota(iota_row[:], pattern=[[1, P]], base=0, channel_multiplier=0,
                                   allow_small_or_imprecise_dtypes=True)
                    for g in range(WT):
                        ins = nc.gpsimd.iota(pool_rc[:, g, :], pattern=[[1, 16]], base=1, channel_multiplier=0,
                                             allow_small_or_imprecise_dtypes=True)
                    ins.then_inc(rc_seed, 1)
                    nc.gpsimd.memset(lvl_mask[:], 0.0)
                    nc.gpsimd.memset(scan_keep[:], 1.0)
                    link(nc.gpsimd.memset(head_sel[:], 1.0))
                    nc.gpsimd.memset(scan_keep[:].rearrange("p (t n) -> p t n", t=NT)[:, :, 0:1], 0.0)
                    for h in range(WT):
                        nc.gpsimd.affine_select(out=head_sel[:, h, :], in_=head_sel[:, h, :], compare_op=ALU.is_equal,
                                                fill=0.0, base=-h, pattern=[[0, P]], channel_multiplier=1)
                    link(nc.gpsimd.memset(neg_mask[:], 0.0))
                    nc.gpsimd.affine_select(out=neg_mask[:], in_=neg_mask[:], compare_op=ALU.is_ge, fill=NEG_BIG, base=0,
                                            pattern=[[-1, P]], channel_multiplier=1)
                    for i, h in enumerate(LEVELS):
                        v = lvl_mask[:, i, :].rearrange("p (n r) -> p n r", r=2 * h)
                        link(nc.gpsimd.memset(v[:, :, h:2 * h], 1.0))
                        link(nc.gpsimd.affine_select(out=v, in_=v, compare_op=ALU.is_ge, fill=0.0, base=0,
                                                     pattern=[[-2 * h, P // (2 * h)], [0, 2 * h]], channel_multiplier=1))
                        link(nc.gpsimd.affine_select(out=v, in_=v, compare_op=ALU.is_ge, fill=0.0, base=h - 1,
                                                     pattern=[[2 * h, P // (2 * h)], [0, 2 * h]], channel_multiplier=-1))
                    v = lvl_mask[:, len(LEVELS), :].rearrange("p (n r) -> p n r", r=DIAG)
                    link(nc.gpsimd.memset(v, 1.0))
                    link(nc.gpsimd.affine_select(out=v, in_=v, compare_op=ALU.is_ge, fill=0.0, base=0,
                                                 pattern=[[-DIAG, P // DIAG], [0, DIAG]], channel_multiplier=1))
                    nc.gpsimd.affine_select(out=v, in_=v, compare_op=ALU.is_ge, fill=0.0, base=0,
                                            pattern=[[DIAG, P // DIAG], [1, DIAG]], channel_multiplier=-1)

                @block.tensor
                def _(pe):
                    pe.wait_ge(s_const, 1)
                    pe.wait_ge(x_in, 16)
                    for t in range(NT):
                        for half in range(2):
                            for q in range(4):
                                k = 4 * half + q
                                tr = nc.tensor.transpose(bank[2 * t + half][:, q * P:(q + 1) * P],
                                                         x_tok[:, t, k * P:(k + 1) * P], ident[:])
                            tr.then_inc(turned0, 1)

                @block.vector
                def _(dve):
                    link = make_link(dve, s_chain_v)
                    dve.wait_ge(rc_seed, 1)
                    for g, w in enumerate(POOL_WINDOWS):
                        ins = nc.vector.tensor_scalar(pool_rc[:, g, :], pool_rc[:, g, :], float(w), None, ALU.min)
                    link(ins)
                    nc.vector.reciprocal(pool_rc[:], pool_rc[:])
                    dve.wait_ge(lb_in, 16)
                    link(nc.vector.tensor_copy(lb_work[:, 0, :], lbl[:, 0, :]))
                    for l in range(1, DEPTH):
                        link(nc.vector.tensor_tensor(lb_work[:, 0, :], lb_work[:, 0, :], lbl[:, l, :], ALU.max))
                    for l in range(DEPTH):
                        ins = nc.vector.tensor_tensor(lbl[:, l, :], lbl[:, l, :], lb_work[:, 0, :], ALU.subtract)
                    ins.then_inc(lb_shift, 1)
                    dve.wait_ge(lb_expd, 1)
                    link(nc.vector.tensor_copy(lb_work[:, 1, :], lb_exp[:, 0, :]))
                    for l in range(1, DEPTH):
                        link(nc.vector.tensor_tensor(lb_work[:, 1, :], lb_work[:, 1, :], lb_exp[:, l, :], ALU.add))
                    link(nc.vector.reciprocal(lb_work[:, 2, :], lb_work[:, 1, :]))
                    for l in range(DEPTH):
                        ins = nc.vector.tensor_tensor(lb_exp[:, l, :], lb_exp[:, l, :], lb_work[:, 2, :], ALU.mult)
                    link(ins)
                    link(nc.vector.tensor_copy(lb_work[:, 3, :], lb_exp[:, 0, :]))
                    for l in range(DEPTH):
                        if l:
                            link(nc.vector.tensor_tensor(lb_work[:, 3, :], lb_work[:, 3, :], lb_exp[:, l, :], ALU.add))
                        link(nc.vector.tensor_tensor(one_minus_lb[:, l, :], lb_work[:, 3, :], lb_exp[:, 0, :], ALU.subtract))
                        nc.vector.tensor_scalar(one_minus_lb[:, l, :], one_minus_lb[:, l, :], -1.0, 1.0, ALU.mult, ALU.add)

                @block.scalar
                def _(act):
                    act.wait_ge(lb_shift, 1)
                    nc.scalar.activation(lb_exp[:], lbl[:], ACT.Exp).then_inc(lb_expd, 1)
                    for t in range(NT):
                        for half in range(2):
                            act.wait_ge(turned0, 2 * t + half + 1)
                            nc.scalar.activation(xT[:, 4 * half:4 * half + 4, t * P:(t + 1) * P],
                                                 bank[2 * t + half][:].rearrange("p (q n) -> p q n", q=4), ACT.Copy)

        with nc.Fori(0, DEPTH) as layer:
            with ExitStack() as mix:
                brT = sb(mix, "brT", [P, 4, WT, SEQ])
                with ExitStack() as ctx:
                    projT = sb(ctx, "projT", [P, 6, 4, SEQ])
                    projN = sb(ctx, "projN", [P, 4, NT, W])
                    ffT = sb(ctx, "ffT", [WT, SEQ])
                    with ExitStack() as c2:
                        w_ff = sb(c2, "w_ff", [P, KT, WT])
                        project_stage("in", lambda n: a["w_in"][layer, n], 3, projT, 2, projN, (w_ff, a["w_ff"][layer], ffT))
                    mixer_stage(nc, a, layer, sb, sem, bank, brT, projT, projN, ffT, ident, lvl_mask, neg_mask, head_sel,
                                pool_rc, scan_keep, one_minus_lb)
                mergedT = sb(mix, "mergedT", [P, KT, SEQ])
                merge_stage(nc, a, layer, sb, sem, bank, brT, xT, mergedT)
                w_out = sb(mix, "w_out", [P, KT, D_MODEL])
                norm_stage("ln1", layer, None, True, a["ln1_g"][layer].partition_broadcast(P),
                           a["ln1_b"][layer].partition_broadcast(P), weights=(w_out, a["w_out"][layer], mergedT))
            with ExitStack() as ffn:
                rowT = sb(ffn, "rowT", [P, SEQ])
                colT = sb(ffn, "colT", [P, SEQ])
                gateT = sb(ffn, "gateT", [P, SEQ])
                with ExitStack() as ctx:
                    qT = sb(ctx, "qT", [P, 4, 4, SEQ])
                    project_stage("pq", lambda n: a["peer_wq"][layer, n], 2, qT)
                    route_stage(nc, a, layer, sb, sem, bank, qT, ident, iota_row, rowT, colT, gateT)
                spread_stage(nc, a, sb, sem, bank, iota_row, rowT, colT, gateT)
            with ExitStack() as ffn:
                y_sum = sb(ffn, "y_sum", [P, NT, D_MODEL])
                experts_stage(nc, a, layer, sb, sem, bank, xT, y_sum)
                norm_stage("ln2", layer, y_sum, False, a["ln2_g"][layer].partition_broadcast(P),
                           a["ln2_b"][layer].partition_broadcast(P))
            with nc.Block() as block:

                @block.gpsimd
                def _(pool):
                    for s in sems.values():
                        pool.sem_clear(s)

        stored = sem("stored")
        with nc.Block() as block:

            @block.sync
            def _(sp):
                sp.dma_start(a["out"].rearrange("o (t p) d -> p (o t) d", p=P), x_tok[:]).then_inc(stored, 16)
                sp.wait_ge(stored, 16)


def merge_stage(nc, a, layer, sb, sem, bank, brT, xT, mergedT):
    with ExitStack() as ctx:
        wg = sb(ctx, "wg", [P, 2, 4, KT, P])
        wb = sb(ctx, "wb", [P, 2, 4, WT, P])
        b_gate = sb(ctx, "b_gate", [P, KT, 4])
        gate = sb(ctx, "gate", [P, 4, SEQ])
        prod = sb(ctx, "prod", [P, 4, SEQ])
        loaded = [sem(f"mg_loaded{b}") for b in range(2)]
        bias_in = sem("mg_bias_in")
        gate_mm = sem("mg_gate_mm")
        br_mm = sem("mg_br_mm")
        gated = sem("mg_gated")
        prods = sem("mg_prods")
        chain = sem("mg_chain")
        with nc.Block() as block:

            @block.sync
            def _(sp):
                sp.dma_start(b_gate[:], a["b_gate"][layer]).then_inc(bias_in, 16)
                with sp.Fori(0, KT // 2) as i:
                    for b in range(2):
                        sp.wait_ge(br_mm, 8 * i + 4 * b + 4)
                        sp.dma_start(wg[:, b], a["w_gate"][layer, 2 * i + b]).then_inc(loaded[b], 16)
                        sp.dma_start(wb[:, b], a["w_branch"][layer, 2 * i + b]).then_inc(loaded[b], 16)

            @block.tensor
            def _(pe):
                pe.sem_inc(br_mm, 8)
                with pe.Fori(0, KT // 2) as i:
                    for b in range(2):
                        pe.wait_ge(loaded[b], 32 * i + 32)
                        for m in range(4):
                            pe.wait_ge(gated, 8 * i + 4 * b + m + 1)
                            for k in range(KT):
                                mm = nc.tensor.matmul(bank[m][:], wg[:, b, m, k, :], xT[:, k, :], start=(k == 0), stop=(k == KT - 1))
                            mm.then_inc(gate_mm, 1)
                            pe.wait_ge(prods, 8 * i + 4 * b + m + 1)
                            for k in range(WT):
                                mm = nc.tensor.matmul(bank[4 + m][:], wb[:, b, m, k, :], brT[:, m, k, :], start=(k == 0), stop=(k == WT - 1))
                            mm.then_inc(br_mm, 1)

            @block.scalar
            def _(act):
                act.sem_inc(gated, 4)
                act.wait_ge(bias_in, 16)
                with act.Fori(0, KT // 2) as i:
                    for b in range(2):
                        for m in range(4):
                            act.wait_ge(gate_mm, 8 * i + 4 * b + m + 1)
                            act.wait_ge(prods, 8 * i + 4 * b + m + 1)
                            nc.scalar.activation(gate[:, m, :], bank[m][:], ACT.Sigmoid,
                                                 bias=b_gate[:, ds(2 * i + b, 1), m]).then_inc(gated, 1)

            @block.vector
            def _(dve):
                dve.sem_inc(prods, 4)
                with dve.Fori(0, KT // 2) as i:
                    link = make_link(dve, chain, 4 * i)
                    for b in range(2):
                        for m in range(4):
                            dve.wait_ge(gated, 8 * i + 4 * b + m + 5)
                            dve.wait_ge(br_mm, 8 * i + 4 * b + m + 9)
                            nc.vector.tensor_tensor(prod[:, m, :], gate[:, m, :], bank[4 + m][:], ALU.mult).then_inc(prods, 1)
                        dve.wait_ge(prods, 8 * i + 4 * b + 8)
                        link(nc.vector.tensor_tensor(prod[:, 0:2, :], prod[:, 0:2, :], prod[:, 2:4, :], ALU.add))
                        link(nc.vector.tensor_tensor(mergedT[:, ds(2 * i + b, 1), :], prod[:, 0:1, :], prod[:, 1:2, :], ALU.add))
                    assert link.done[0] == 4


def route_stage(nc, a, layer, sb, sem, bank, qT, ident, iota_row, rowT, colT, gateT):
    H, K = PEER_HEADS, TOPK
    with ExitStack() as ctx:
        keys = sb(ctx, "keys", [P, N_LISTS, P])
        sc = sb(ctx, "sc", [P, N_LISTS, P])
        sc2 = sb(ctx, "sc2", [P, N_LISTS, P])
        best = sb(ctx, "best", [P, N_LISTS, K])
        best_ix = sb(ctx, "best_ix", [P, N_LISTS, K], U32)
        best_ixf = sb(ctx, "best_ixf", [P, N_LISTS, K])
        cand = sb(ctx, "cand", [P, H, K * K])
        cand2 = sb(ctx, "cand2", [P, H, K * K])
        top = sb(ctx, "top", [P, H, K])
        pos = sb(ctx, "pos", [P, H, K], U32)
        rank = sb(ctx, "rank", [P, 2, H * K], U32)
        rankf = sb(ctx, "rankf", [P, 2, H * K])
        hit = sb(ctx, "hit", [P, H * K, K])
        hit2 = sb(ctx, "hit2", [P, H * K, K])
        row = sb(ctx, "row", [P, PAIRS])
        col = sb(ctx, "col", [P, PAIRS])
        gate = sb(ctx, "pgate", [P, H, K])
        total = sb(ctx, "total", [P, H])
        keys_in = sem("rt_keys_in")
        scored = sem("rt_scored")
        sc_ready = sem("rt_sc_ready")
        sc_free = sem("rt_sc_free")
        shifted = sem("rt_shifted")
        expd = sem("rt_expd")
        routed = sem("rt_routed")
        turned = sem("rt_turned")
        taken = sem("rt_taken")
        chain = sem("rt_chain")
        with nc.Block() as block:

            @block.sync
            def _(sp):
                sp.dma_start(keys[:], a["peer_keys"][layer]).then_inc(keys_in, 16)

            @block.tensor
            def _(pe):
                def score(t):
                    for j in range(4):
                        if t:
                            pe.wait_ge(sc_ready, 4 * (t - 1) + j + 1)
                        for q in range(4):
                            n = 4 * j + q
                            mm = nc.tensor.matmul(bank[j][:, q * P:(q + 1) * P], qT[:, n // 4, n % 4, t * P:(t + 1) * P],
                                                  keys[:, n, :], start=True, stop=True)
                        mm.then_inc(scored, 1)

                def turn(t):
                    pe.wait_ge(routed, t + 1)
                    for j, src in enumerate((row, col, gate)):
                        if t:
                            pe.wait_ge(taken, 3 * (t - 1) + j + 1)
                        v = src[:] if j < 2 else src[:].rearrange("p h k -> p (h k)")
                        nc.tensor.transpose(bank[4 + j][:, 0:P], v, ident[:]).then_inc(turned, 1)

                pe.sem_inc(turned, 3)
                pe.wait_ge(keys_in, 16)
                score(0)
                for t in range(NT):
                    if t + 1 < NT:
                        score(t + 1)
                    turn(t)

            @block.scalar
            def _(act):
                def keep_scores(t):
                    if t:
                        act.wait_ge(sc_free, t)
                    for j in range(4):
                        act.wait_ge(scored, 4 * t + j + 1)
                        nc.scalar.activation(sc[:, 4 * j:4 * j + 4, :].rearrange("p q n -> p (q n)"), bank[j][:],
                                             ACT.Copy).then_inc(sc_ready, 1)

                keep_scores(0)
                for t in range(NT):
                    if t + 1 < NT:
                        keep_scores(t + 1)
                    act.wait_ge(shifted, t + 1)
                    nc.scalar.activation(gate[:], gate[:], ACT.Exp).then_inc(expd, 1)
                    for j, dst in enumerate((rowT, colT, gateT)):
                        act.wait_ge(turned, 3 * t + j + 4)
                        nc.scalar.activation(dst[:, t * P:(t + 1) * P], bank[4 + j][:, 0:P], ACT.Copy).then_inc(taken, 1)

            @block.vector
            def _(dve):
                V = nc.vector
                with dve.Fori(0, NT) as t:
                    dve.sem_clear(chain)
                    link = make_link(dve, chain)
                    dve.wait_ge(turned, 3 * t + 3)
                    link(V.memset(total[:], 0.0))
                    dve.wait_ge(sc_ready, 4 * t + 4)
                    link(V.memset(total[:], 0.0))
                    for n in range(N_LISTS):
                        ins = V.max(best[:, n, 0:8], sc[:, n, :])
                    link(ins)
                    for n in range(N_LISTS):
                        V.max_index(best_ix[:, n, 0:8], best[:, n, 0:8], sc[:, n, :])
                        ins = V.match_replace(sc2[:, n, :], best[:, n, 0:8], sc[:, n, :], LOWEST)
                    link(ins)
                    V.engine_nop().then_inc(sc_free, 1)
                    for n in range(N_LISTS):
                        ins = V.max(best[:, n, 8:16], sc2[:, n, :])
                    link(ins)
                    for n in range(N_LISTS):
                        ins = V.max_index(best_ix[:, n, 8:16], best[:, n, 8:16], sc2[:, n, :])
                    link(ins)
                    V.tensor_copy(best_ixf[:], best_ix[:])
                    pairs = best[:].rearrange("p (h two) k -> p h two k", two=2)
                    link(V.tensor_tensor(cand[:].rearrange("p h (i j) -> p h i j", i=K),
                                         pairs[:, :, 0, :].unsqueeze(3).to_broadcast([P, H, K, K]),
                                         pairs[:, :, 1, :].unsqueeze(2).to_broadcast([P, H, K, K]), ALU.add))
                    for h in range(H):
                        ins = V.max(top[:, h, 0:8], cand[:, h, :])
                    link(ins)
                    for h in range(H):
                        V.max_index(pos[:, h, 0:8], top[:, h, 0:8], cand[:, h, :])
                        ins = V.match_replace(cand2[:, h, :], top[:, h, 0:8], cand[:, h, :], LOWEST)
                    link(ins)
                    for h in range(H):
                        ins = V.max(top[:, h, 8:16], cand2[:, h, :])
                    link(ins)
                    for h in range(H):
                        ins = V.max_index(pos[:, h, 8:16], top[:, h, 8:16], cand2[:, h, :])
                    link(ins)
                    V.tensor_tensor(gate[:], top[:], top[:, :, 0:1].to_broadcast([P, H, K]), ALU.subtract).then_inc(shifted, 1)
                    pf = pos[:].rearrange("p h k -> p (h k)")
                    V.tensor_scalar(rank[:, 0, :], pf, 4, None, ALU.logical_shift_right)
                    link(V.tensor_scalar(rank[:, 1, :], pf, K - 1, None, ALU.bitwise_and))
                    link(V.tensor_copy(rankf[:], rank[:]))
                    lists = best_ixf[:].rearrange("p (h two) k -> p h two k", two=2)
                    for side, dst in enumerate((row, col)):
                        link(V.tensor_tensor(hit[:], rankf[:, side, :].unsqueeze(2).to_broadcast([P, H * K, K]),
                                             iota_row[:, 0:K].unsqueeze(1).to_broadcast([P, H * K, K]), ALU.is_equal))
                        link(V.tensor_tensor(hit2[:].rearrange("p (h k) j -> p h k j", h=H),
                                             hit[:].rearrange("p (h k) j -> p h k j", h=H),
                                             lists[:, :, side, :].unsqueeze(2).to_broadcast([P, H, K, K]), ALU.mult))
                        link(V.tensor_reduce(dst[:], hit2[:], AX, ALU.add))
                    dve.wait_ge(expd, t + 1)
                    link(V.tensor_reduce(total[:], gate[:], AX, ALU.add))
                    link(V.reciprocal(total[:], total[:]))
                    link(V.tensor_tensor(gate[:], gate[:], total[:].unsqueeze(2).to_broadcast([P, H, K]), ALU.mult))
                    V.engine_nop().then_inc(routed, 1)


def spread_stage(nc, a, sb, sem, bank, iota_row, rowT, colT, gateT):
    STEP = 16
    with ExitStack() as ctx:
        hot_row = sb(ctx, "hot_row", [P, STEP, P])
        hot_col = sb(ctx, "hot_col", [P, STEP, P])
        cols = sb(ctx, "cols", [P, 2, STEP])
        rows = sb(ctx, "rows", [P, 4, 4])
        stage = sb(ctx, "stage", [P, 2, P, TB])
        rows_hot = sem("sp_rows_hot")
        cols_hot = sem("sp_cols_hot")
        spread = sem("sp_spread")
        kept = sem("sp_kept")
        stored = [sem(f"sp_stored{b}") for b in range(2)]
        chain = sem("sp_chain")

        with nc.Block() as block:

            def steps(eng, body):
                with eng.Fori(0, NTB // 2) as m:
                    for b in range(2):
                        with eng.Fori(0, TB // STEP) as q:
                            body((2 * m + b) * (TB // STEP) + q, b, q, m)

            @block.gpsimd
            def _(pool):
                def body(n, b, q, m):
                    for g in range(4):
                        pool.wait_ge(spread, 4 * n + g + 1)
                        nc.gpsimd.tensor_copy(rows[:, g, :], rowT[:, ds(n * STEP + 4 * g, 4)])
                        pool.drain()
                        for s in range(4):
                            ins = nc.gpsimd.tensor_scalar(hot_row[:, 4 * g + s, :], iota_row[:], rows[:, g, s:s + 1], None, ALU.is_equal)
                        ins.then_inc(rows_hot, 1)
                steps(pool, body)

            @block.vector
            def _(dve):
                def body(n, b, q, m):
                    dve.wait_ge(cols_hot, 4 * n + 4)
                    nc.vector.tensor_copy(cols[:, 0, :], colT[:, ds(n * STEP, STEP)])
                    nc.vector.tensor_copy(cols[:, 1, :], gateT[:, ds(n * STEP, STEP)]).then_inc(chain, 1)
                    dve.wait_ge(chain, n + 1)
                    for g in range(4):
                        dve.wait_ge(spread, 4 * n + g + 1)
                        for s in range(4 * g, 4 * g + 4):
                            ins = nc.vector.tensor_scalar(hot_col[:, s, :], iota_row[:], cols[:, 0, s:s + 1], cols[:, 1, s:s + 1],
                                                          ALU.is_equal, ALU.mult)
                        ins.then_inc(cols_hot, 1)
                dve.sem_inc(cols_hot, 4)
                steps(dve, body)

            @block.tensor
            def _(pe):
                pe.sem_inc(spread, 4)

                def body(n, b, q, m):
                    for g in range(4):
                        pe.wait_ge(kept, 4 * n + g + 1)
                        pe.wait_ge(rows_hot, 4 * n + g + 1)
                        pe.wait_ge(cols_hot, 4 * n + g + 5)
                        for s in range(4):
                            mm = nc.tensor.matmul(bank[g][:, s * P:(s + 1) * P], hot_row[:, 4 * g + s, :], hot_col[:, 4 * g + s, :],
                                                  start=True, stop=True)
                        mm.then_inc(spread, 1)
                steps(pe, body)

            @block.scalar
            def _(act):
                act.sem_inc(kept, 4)
                act.sem_inc(stored[0], 16)
                act.sem_inc(stored[1], 16)

                def body(n, b, q, m):
                    act.wait_ge(stored[b], 16 * m + 16)
                    for g in range(4):
                        act.wait_ge(spread, 4 * n + g + 5)
                        nc.scalar.activation(stage[:, b, :, ds(q * STEP + 4 * g, 4)],
                                             bank[g][:].rearrange("p (t c) -> p c t", t=4), ACT.Copy).then_inc(kept, 1)
                steps(act, body)

            @block.sync
            def _(sp):
                per = 4 * TB // STEP
                with sp.Fori(0, NTB // 2) as m:
                    for b in range(2):
                        sp.wait_ge(kept, (2 * m + b) * per + per + 4)
                        sp.dma_start(a["gates"][:, 2 * m + b], stage[:, b]).then_inc(stored[b], 16)
                for b in range(2):
                    sp.wait_ge(stored[b], 16 * (NTB // 2) + 16)


def experts_stage(nc, a, layer, sb, sem, bank, xT, y_sum):
    with ExitStack() as ctx:
        u = sb(ctx, "u", [P, 2, EC, KT, P])
        v = sb(ctx, "v", [P, 2, EC, D_MODEL])
        G = sb(ctx, "G", [P, 2, NTB, EC, TB])
        hid = sb(ctx, "hid", [P, EC, SEQ])
        wgt = sb(ctx, "wgt", [P, 2, EC, SEQ])
        u_in = [sem(f"ex_u_in{b}") for b in range(2)]
        v_in = [sem(f"ex_v_in{b}") for b in range(2)]
        G_in = [sem(f"ex_G_in{b}") for b in range(2)]
        h_mm = sem("ex_h_mm")
        h_act = sem("ex_h_act")
        w_done = sem("ex_w_done")
        y_mm = sem("ex_y_mm")
        y_add = sem("ex_y_add")
        zeroed = sem("ex_zeroed")
        with nc.Block() as block:

            @block.sync
            def _(sp):
                with sp.Fori(0, NG // 2) as i:
                    for b in range(2):
                        n = 2 * i + b
                        sp.wait_ge(h_mm, 4 * n + 4)
                        sp.dma_start(u[:, b], a["peer_u"][layer, n]).then_inc(u_in[b], 16)
                        sp.wait_ge(w_done, 4 * n + 4)
                        sp.dma_start(G[:, b], a["gates"][:, :, ds(n * EC, EC), :]).then_inc(G_in[b], 16)
                        sp.wait_ge(y_mm, 8 * n + 8)
                        sp.dma_start(v[:, b], a["peer_v"][layer, :, ds(n * EC, EC), :]).then_inc(v_in[b], 16)

            def skewed(eng, first, second):
                first(0, 0, 0)
                with eng.Fori(0, NG // 2 - 1) as i:
                    first(2 * i + 1, i, 1)
                    second(2 * i, i, 0)
                    first(2 * i + 2, i + 1, 0)
                    second(2 * i + 1, i, 1)
                i = NG // 2 - 1
                first(2 * i + 1, i, 1)
                second(2 * i, i, 0)
                second(2 * i + 1, i, 1)

            @block.tensor
            def _(pe):
                pe.sem_inc(h_mm, 8)
                pe.sem_inc(y_mm, 16)

                def hidden(n, i, b):
                    pe.wait_ge(u_in[b], 16 * i + 16)
                    for c in range(EC):
                        pe.wait_ge(h_act, 4 * n + c + 1)
                        for k in range(KT):
                            mm = nc.tensor.matmul(bank[c][:], u[:, b, c, k, :], xT[:, k, :], start=(k == 0), stop=(k == KT - 1))
                        mm.then_inc(h_mm, 1)

                def output(n, i, b):
                    pe.wait_ge(v_in[b], 16 * i + 16)
                    pe.wait_ge(w_done, 4 * n + EC + 8)
                    for j in range(2 * NT):
                        t, half = j // 2, j % 2
                        pe.wait_ge(y_add, 8 * n + j + 5)
                        for c in range(EC):
                            mm = nc.tensor.matmul(bank[4 + j % 4][:], wgt[:, b, c, t * P:(t + 1) * P],
                                                  v[:, b, c, half * 512:(half + 1) * 512], start=(c == 0), stop=(c == EC - 1))
                        mm.then_inc(y_mm, 1)

                skewed(pe, hidden, output)

            @block.scalar
            def _(act):
                act.sem_inc(h_act, 4)

                def gelu(n, i, b):
                    for c in range(EC):
                        act.wait_ge(h_mm, 4 * n + c + 9)
                        act.wait_ge(w_done, 4 * n + c + 5)
                        nc.scalar.activation(hid[:, c, :], bank[c][:], ACT.Gelu_apprx_tanh).then_inc(h_act, 1)

                with act.Fori(0, NG // 2) as i:
                    for b in range(2):
                        gelu(2 * i + b, i, b)

            @block.vector
            def _(dve):
                nc.vector.memset(y_sum[:], 0.0).then_inc(zeroed, 1)
                dve.sem_inc(w_done, 8)
                dve.sem_inc(y_add, 8)
                dve.wait_ge(zeroed, 1)

                def weigh(n, i, b):
                    dve.wait_ge(G_in[b], 16 * i + 16)
                    dve.wait_ge(y_mm, 8 * n + 8)
                    for c in range(EC):
                        dve.wait_ge(h_act, 4 * n + c + 5)
                        nc.vector.tensor_tensor(wgt[:, b, c, :].rearrange("p (q t) -> p q t", t=TB),
                                                hid[:, c, :].rearrange("p (q t) -> p q t", t=TB),
                                                G[:, b, :, c, :], ALU.mult).then_inc(w_done, 1)

                def add(n, i, b):
                    for j in range(2 * NT):
                        t, half = j // 2, j % 2
                        part = y_sum[:, t, half * 512:(half + 1) * 512]
                        dve.wait_ge(y_mm, 8 * n + j + 17)
                        dve.wait_ge(y_add, 8 * n + j + 1)
                        nc.vector.tensor_tensor(part, part, bank[4 + j % 4][:], ALU.add).then_inc(y_add, 1)

                skewed(dve, weigh, add)


def mixer_stage(nc, a, layer, sb, sem, bank, brT, projT, projN, ffT, ident, lvl_mask, neg_mask, head_sel,
                pool_rc, scan_keep, one_minus_lb):
    V = nc.vector
    NL = len(LEVELS)
    with ExitStack() as ctx:
        tmp = [sb(ctx, f"tmp{i}", [P, WT, SEQ]) for i in range(2)]
        att = sb(ctx, "att", [P, NT, WT, P])
        state = sb(ctx, "state", [P, WT, P])
        decay = sb(ctx, "decay", [P, WT, NT])
        ss = sb(ctx, "ss", [P, NT, WT])
        rms = sb(ctx, "rms", [P, NT, WT])
        pool_w = sb(ctx, "pool_w", [P, WT, P])
        pool_scale = sb(ctx, "pool_scale", [P, WT])
        norm_g = sb(ctx, "norm_g", [P, 1])
        ws = sb(ctx, "ws", [P, WT, P])
        bs_row = sb(ctx, "bs_row", [P, WT, P])
        lng_row = sb(ctx, "lng_row", [P, W])
        lnb_row = sb(ctx, "lnb_row", [P, W])
        gstats = sb(ctx, "gstats", [P, NT, 6])
        gmv = sb(ctx, "gmv", [P, NT, 2])
        gstd = sb(ctx, "gstd", [P, NT])
        b_fox = sb(ctx, "b_fox", [WT, 1])
        fz = sb(ctx, "fz", [WT, 2, SEQ])
        fones = sb(ctx, "fones", [WT, 1])
        cum = sb(ctx, "cum", [WT, 2, SEQ])
        fmax = sb(ctx, "fmax", [P, 16])
        fsum = sb(ctx, "fsum", [P, 16])
        prob = sb(ctx, "prob", [P, 2, SEQ])
        probT = sb(ctx, "probT", [P, 2, SEQ])

        pin, q, k, gu, fq, fk = (projT[:, j] for j in (T_POOL, T_HQ, T_HF, T_GU, T_FQ, T_FK))
        val, hg, gv, fv = (projN[:, j] for j in (N_HI, N_HG, N_GV, N_FV))
        cumb = brT[:, 1]

        def flat(v):
            return v.rearrange("p h t -> p (h t)")

        params_in = {n: sem(f"mx_{n}_in") for n in ("poolw", "pools", "normg", "ws", "bs", "lng", "lnb", "bfox")}
        ws_masked = sem("mx_ws_masked")
        fones_done = sem("mx_fones_done")
        q_act, hg_act, gu_act, gv_act, sig_done, logf_done = (sem(f"mx_{n}") for n in ("q_act", "hg_act", "gu_act", "gv_act", "sig_done", "logf_done"))
        diff_ready, pool_mm, pool_kept = sem("mx_diff_ready"), sem("mx_pool_mm"), sem("mx_pool_kept")
        gvar, gsqrt, gnorm, gm_mm, gm_used = (sem(f"mx_{n}") for n in ("gvar", "gsqrt", "gnorm", "gm_mm", "gm_used"))
        k_ready, lvl_d, lvl_e, lvl_x, lvl_mm, att_done = (sem(f"mx_{n}") for n in ("k_ready", "lvl_d", "lvl_e", "lvl_x", "lvl_mm", "att_done"))
        kd_d, kd_e, kd_x, qin_x, kd_turned, kd_kept = (sem(f"mx_{n}") for n in ("kd_d", "kd_e", "kd_x", "qin_x", "kd_turned", "kd_kept"))
        o_mm, o_kept, ds_mm, s_upd, ss_ready, ss_sqrt, o_normed, o_turned = (
            sem(f"mx_{n}") for n in ("o_mm", "o_kept", "ds_mm", "s_upd", "ss_ready", "ss_sqrt", "o_normed", "o_turned"))
        fz_ready, fz_exp, c_ready, fq_ready = (sem(f"mx_{n}") for n in ("fz_ready", "fz_exp", "c_ready", "fq_ready"))
        fx_mm, fx_max, fx_exp, fx_p, fx_turned, fx_pt, fx_o, fx_kept = (
            sem(f"mx_{n}") for n in ("fx_mm", "fx_max", "fx_exp", "fx_p", "fx_turned", "fx_pt", "fx_o", "fx_kept"))
        chain = sem("mx_chain")
        chain_a = sem("mx_chain_a")

        with nc.Block() as block:

            @block.sync
            def _(sp):
                for name, dst, src in (
                        ("bfox", b_fox, a["b_fox_f"][layer]), ("poolw", pool_w, a["pool_w"][layer]),
                        ("pools", pool_scale, a["pool_scale"][layer]),
                        ("lng", lng_row, a["gmlp_ln_g"][layer].partition_broadcast(P)),
                        ("lnb", lnb_row, a["gmlp_ln_b"][layer].partition_broadcast(P)),
                        ("ws", ws, a["gmlp_ws"][layer]), ("normg", norm_g, a["hgrn_norm_g"][layer])):
                    sp.dma_start(dst[:], src).then_inc(params_in[name], 16)
                sp.dma_start(bs_row[:].rearrange("p g t -> p (g t)"),
                             a["gmlp_bs"][layer].partition_broadcast(P)).then_inc(params_in["bs"], 16)

            @block.gpsimd
            def _(pool):
                nc.gpsimd.memset(fones[:], 1.0).then_inc(fones_done, 1)
                pool.wait_ge(params_in["ws"], 16)
                nc.gpsimd.affine_select(out=ws[:], in_=ws[:], compare_op=ALU.is_ge, fill=0.0, base=0,
                                        pattern=[[0, WT], [1, P]], channel_multiplier=-1).then_inc(ws_masked, 1)

            @block.tensor
            def _(pe):
                pe.wait_ge(params_in["poolw"], 16)
                for g in range(WT):
                    pe.wait_ge(diff_ready, g + 1)
                    if g >= 2:
                        pe.wait_ge(pool_kept, g - 1)
                    nc.tensor.matmul(bank[6 + g % 2][:], pool_w[:, g, :], pin[:, g, :], start=True, stop=True).then_inc(pool_mm, 1)
                pe.wait_ge(ws_masked, 1)
                pe.wait_ge(gnorm, 1)
                for g in range(WT):
                    if g < 2:
                        pe.wait_ge(pool_kept, 3 + g)
                    else:
                        pe.wait_ge(gm_used, g - 1)
                    for t in range(NT):
                        mm = nc.tensor.matmul(bank[6 + g % 2][:, t * P:(t + 1) * P], gv[:, t, g * P:(g + 1) * P], ws[:, g, :],
                                              start=True, stop=True)
                    mm.then_inc(gm_mm, 1)
                for i in range(NL + 1):
                    pe.wait_ge(lvl_x, i + 1)
                    kk = tmp[i % 2] if i < NL else tmp[1]
                    qq = tmp[i % 2] if i < NL else tmp[0]
                    for t in range(NT):
                        if i:
                            pe.wait_ge(att_done, NT * (i - 1) + t + 1)
                        for h in range(WT):
                            mm = nc.tensor.matmul(bank[t][:, h * P:(h + 1) * P], kk[:, h, t * P:(t + 1) * P],
                                                  qq[:, h, t * P:(t + 1) * P], start=True, stop=True)
                        mm.then_inc(lvl_mm, 1)
                pe.wait_ge(kd_x, 1)
                for t in range(NT):
                    pe.wait_ge(att_done, NT * NL + t + 1)
                    for h in range(WT):
                        mm = nc.tensor.transpose(bank[t][:, h * P:(h + 1) * P], tmp[0][:, h, t * P:(t + 1) * P], ident[:])
                    mm.then_inc(kd_turned, 1)
                pe.wait_ge(kd_kept, NT)
                pe.wait_ge(qin_x, 1)
                for t in range(NT):
                    if t < NT - 1:
                        if t >= 2:
                            pe.wait_ge(s_upd, t - 1)
                        for h in range(WT):
                            mm = nc.tensor.matmul(bank[2 + t % 2][:, h * P:(h + 1) * P], tmp[1][:, t, h * P:(h + 1) * P],
                                                  val[:, t, h * P:(h + 1) * P], start=True, stop=True)
                        mm.then_inc(ds_mm, 1)
                    if t >= 2:
                        pe.wait_ge(o_kept, t - 1)
                    if t:
                        pe.wait_ge(s_upd, t)
                    for h in range(WT):
                        mm = nc.tensor.matmul(bank[t % 2][:, h * P:(h + 1) * P], att[:, t, h, :], val[:, t, h * P:(h + 1) * P],
                                              start=True, stop=(t == 0))
                        if t:
                            mm = nc.tensor.matmul(bank[t % 2][:, h * P:(h + 1) * P], q[:, h, t * P:(t + 1) * P], state[:, h, :],
                                                  start=False, stop=True)
                    mm.then_inc(o_mm, 1)
                pe.wait_ge(o_normed, 1)
                for t in range(NT):
                    for h in range(WT):
                        mm = nc.tensor.transpose(bank[t][:, h * P:(h + 1) * P], tmp[0][:, t, h * P:(h + 1) * P], ident[:])
                    mm.then_inc(o_turned, 1)
                pe.wait_ge(fq_ready, 1)
                pe.wait_ge(c_ready, 2)

                def logits(n):
                    h, t = divmod(n, NT)
                    cols = (t + 1) * P
                    b = bank[4 + n % 2]
                    if n >= 2:
                        pe.wait_ge(fx_exp, n - 1)
                    nc.tensor.matmul(b[:, 0:cols], fq[:, h, t * P:(t + 1) * P], fk[:, h, 0:cols], start=True, stop=False)
                    nc.tensor.matmul(b[:, 0:cols], cum[:, 0, t * P:(t + 1) * P], head_sel[:, h, 0:1].to_broadcast([WT, cols]), start=False, stop=False)
                    nc.tensor.matmul(b[:, 0:cols], head_sel[:, h, :], cum[:, 1, 0:cols], start=False, stop=False)
                    nc.tensor.matmul(b[:, t * P:cols], ident[:], neg_mask[:], start=False, stop=True).then_inc(fx_mm, 1)

                pe.wait_ge(gm_used, WT)
                logits(0)
                for n in range(WT * NT):
                    h, t = divmod(n, NT)
                    if n + 1 < WT * NT:
                        logits(n + 1)
                    pe.wait_ge(fx_p, n + 1)
                    if n:
                        pe.wait_ge(fx_pt, n)
                    for j in range(t + 1):
                        mm = nc.tensor.transpose(bank[6][:, j * P:(j + 1) * P], prob[:, n % 2, j * P:(j + 1) * P], ident[:])
                    mm.then_inc(fx_turned, 1)
                    if t == 0 and h:
                        pe.wait_ge(fx_kept, h)
                    pe.wait_ge(fx_pt, n + 1)
                    for j in range(t + 1):
                        mm = nc.tensor.matmul(bank[7][:, t * P:(t + 1) * P], fv[:, j, h * P:(h + 1) * P],
                                              probT[:, n % 2, j * P:(j + 1) * P], start=(j == 0), stop=(j == t))
                    mm.then_inc(fx_o, 1)

            @block.scalar
            def _(act):
                A = nc.scalar.activation
                link = make_link(act, chain_a)
                A(flat(q), flat(q), ACT.Silu).then_inc(q_act, 1)
                A(flat(hg), flat(hg), ACT.Silu).then_inc(hg_act, 1)
                A(flat(gv), flat(gv), ACT.Gelu_apprx_tanh).then_inc(gv_act, 1)
                A(flat(gu), flat(gu), ACT.Gelu_apprx_tanh).then_inc(gu_act, 1)
                act.wait_ge(gvar, 1)
                A(gstd[:], gstd[:], ACT.Sqrt).then_inc(gsqrt, 1)
                A(flat(k), flat(k), ACT.Sigmoid, scale=-1.0).then_inc(sig_done, 1)
                act.wait_ge(params_in["pools"], 16)
                for g in range(WT):
                    act.wait_ge(pool_mm, g + 1)
                    A(brT[:, 0, g, :], bank[6 + g % 2][:], ACT.Copy, scale=pool_scale[:, g:g + 1]).then_inc(pool_kept, 1)
                act.wait_ge(k_ready, 1)
                A(flat(tmp[0]), flat(k), ACT.Ln, bias=1.0, scale=-1.0).then_inc(logf_done, 1)
                act.wait_ge(fz_ready, 1)
                link(A(fz[:, 1, :], fz[:, 1, :], ACT.Exp))
                A(fz[:, 1, :], fz[:, 1, :], ACT.Ln, bias=1.0).then_inc(fz_exp, 1)
                for i in range(NL):
                    act.wait_ge(lvl_d, i + 1)
                    A(flat(tmp[i % 2]), flat(tmp[i % 2]), ACT.Exp).then_inc(lvl_e, 1)
                act.wait_ge(lvl_d, NL + 1)
                link(A(flat(tmp[1]), flat(tmp[0]), ACT.Exp, scale=-1.0))
                A(flat(tmp[0]), flat(tmp[0]), ACT.Exp).then_inc(lvl_e, 1)
                act.wait_ge(kd_d, 1)
                A(flat(tmp[0]), flat(tmp[0]), ACT.Exp).then_inc(kd_e, 1)
                link(A(decay[:], cumb.rearrange("p h (t n) -> p h t n", n=P)[:, :, :, P - 1], ACT.Exp))
                A(flat(cumb), flat(cumb), ACT.Exp).then_inc(kd_e, 1)
                for t in range(NT):
                    act.wait_ge(kd_turned, t + 1)
                    A(tmp[1][:, t, :], bank[t][:], ACT.Copy).then_inc(kd_kept, 1)
                for t in range(NT):
                    act.wait_ge(o_mm, t + 1)
                    A(tmp[0][:, t, :], bank[t % 2][:], ACT.Copy).then_inc(o_kept, 1)
                act.wait_ge(ss_ready, 1)
                A(rms[:], ss[:], ACT.Sqrt).then_inc(ss_sqrt, 1)
                act.wait_ge(params_in["normg"], 16)
                for t in range(NT):
                    act.wait_ge(o_turned, t + 1)
                    A(brT[:, 1, :, t * P:(t + 1) * P], bank[t][:].rearrange("p (h n) -> p h n", h=WT), ACT.Copy,
                      scale=norm_g[:, 0:1])
                for n in range(WT * NT):
                    h, t = divmod(n, NT)
                    cols = (t + 1) * P
                    act.wait_ge(fx_max, n + 1)
                    if n >= 2:
                        act.wait_ge(fx_turned, n - 1)
                    A(prob[:, n % 2, 0:cols], bank[4 + n % 2][:, 0:cols], ACT.Exp, bias=fmax[:, n:n + 1],
                      accum_out=fsum[:, n:n + 1]).then_inc(fx_exp, 1)
                    act.wait_ge(fx_turned, n + 1)
                    if n >= 2:
                        act.wait_ge(fx_o, n - 1)
                    A(probT[:, n % 2, 0:cols], bank[6][:, 0:cols], ACT.Copy).then_inc(fx_pt, 1)
                    if t == NT - 1:
                        act.wait_ge(fx_o, n + 1)
                        A(brT[:, 3, h, :], bank[7][:], ACT.Copy).then_inc(fx_kept, 1)

            @block.vector
            def _(dve):
                link = make_link(dve, chain)
                src = pin
                for i, w in enumerate(POOL_WINDOWS):
                    dst, sh = tmp[i % 2][:], w // 2
                    V.tensor_tensor(dst[:, i:, sh:], src[:, i:, sh:], src[:, i:, 0:SEQ - sh], ALU.add)
                    link(V.tensor_copy(dst[:, i:, 0:sh], src[:, i:, 0:sh]))
                    link(V.tensor_tensor(prob[:, 0, 0:16], dst[:, i, 0:16], pool_rc[:, i, :], ALU.mult))
                    link(V.tensor_tensor(brT[:, 0, i, 0:16], prob[:, 0, 0:16], pin[:, i, 0:16], ALU.subtract))
                    link(V.scalar_tensor_tensor(out=brT[:, 0, i, 16:], in0=dst[:, i, 16:], scalar=1.0 / w,
                                                in1=pin[:, i, 16:], op0=ALU.mult, op1=ALU.subtract))
                    src = dst
                for g in range(WT):
                    V.tensor_copy(pin[:, g, :], brT[:, 0, g, :]).then_inc(diff_ready, 1)
                dve.wait_ge(params_in["bfox"], 16)
                link(V.tensor_scalar(fz[:, 0, :], ffT[:], b_fox[:, 0:1], None, ALU.add))
                link(V.tensor_scalar(fz[:, 1, :], fz[:, 0, :], -1.0, None, ALU.mult))
                V.tensor_tensor(fz[:, 1, :], fz[:, 0, :], fz[:, 1, :], ALU.min).then_inc(fz_ready, 1)
                V.tensor_scalar(flat(fq), flat(fq), FOX_SCALE, None, ALU.mult).then_inc(fq_ready, 1)
                dve.wait_ge(gv_act, 1)
                for t in range(NT):
                    ins = V.bn_stats(gstats[:, t, :], gv[:, t, :])
                link(ins)
                for t in range(NT):
                    ins = V.bn_aggr(gmv[:, t, :], gstats[:, t, :])
                link(ins)
                V.tensor_scalar(gstd[:], gmv[:, :, 1], LN_EPS, None, ALU.add).then_inc(gvar, 1)
                dve.wait_ge(gsqrt, 1)
                link(V.reciprocal(gstd[:], gstd[:]))
                for t in range(NT):
                    ins = V.tensor_scalar(gv[:, t, :], gv[:, t, :], gmv[:, t, 0:1], gstd[:, t:t + 1], ALU.subtract, ALU.mult)
                link(ins)
                dve.wait_ge(params_in["lng"], 16)
                link(V.tensor_tensor(gv, gv, lng_row[:].unsqueeze(1).to_broadcast([P, NT, W]), ALU.mult))
                dve.wait_ge(params_in["lnb"], 16)
                V.tensor_tensor(gv, gv, lnb_row[:].unsqueeze(1).to_broadcast([P, NT, W]), ALU.add).then_inc(gnorm, 1)
                dve.wait_ge(sig_done, 1)
                for h in range(WT):
                    ins = V.tensor_scalar(k[:, h, :], k[:, h, :], one_minus_lb[:, ds(layer, 1), h], None, ALU.mult)
                ins.then_inc(k_ready, 1)
                dve.wait_ge(logf_done, 1)
                for h in range(WT):
                    ins = V.tensor_tensor_scan(cumb[:, h, :], scan_keep[:], tmp[0][:, h, :], 0.0, ALU.mult, ALU.add)
                link(ins)
                dve.wait_ge(fz_exp, 1)
                dve.wait_ge(fones_done, 1)
                link(V.tensor_scalar(fz[:, 0, :], fz[:, 0, :], 0.0, None, ALU.min))
                link(V.tensor_tensor(fz[:, 0, :], fz[:, 0, :], fz[:, 1, :], ALU.subtract))
                V.tensor_tensor_scan(cum[:, 0, :], fones[:].to_broadcast([WT, SEQ]), fz[:, 0, :], 0.0, ALU.mult, ALU.add).then_inc(c_ready, 1)
                dve.wait_ge(c_ready, 1)
                V.tensor_scalar(cum[:, 1, :], cum[:, 0, :], -1.0, None, ALU.mult).then_inc(c_ready, 1)
                dve.wait_ge(params_in["bs"], 16)
                dve.wait_ge(gu_act, 1)
                for g in range(WT):
                    dve.wait_ge(gm_mm, g + 1)
                    out = brT[:, 2, g, :].rearrange("p (t n) -> p t n", t=NT)
                    V.tensor_tensor(out, bank[6 + g % 2][:].rearrange("p (t n) -> p t n", t=NT),
                                    bs_row[:, g:g + 1, :].to_broadcast([P, NT, P]), ALU.add).then_inc(gm_used, 1)
                    dve.wait_ge(gm_used, g + 1)
                    V.tensor_tensor(brT[:, 2, g, :], brT[:, 2, g, :], gu[:, g, :], ALU.mult)
                link(V.memset(att[:], 0.0))

                def blocks(v, r):
                    return v.rearrange("p h (n two r) -> p (h n) two r", two=2, r=r)

                def exponents(i):
                    h = LEVELS[i]
                    n = WT * SEQ // (2 * h)
                    if i >= 2:
                        dve.wait_ge(lvl_mm, NT * (i - 1))
                    x, b = blocks(tmp[i % 2][:], h), blocks(cumb, h)
                    anchor = b[:, :, 0, h - 1:h].to_broadcast([P, n, h])
                    V.tensor_tensor(x[:, :, 0, :], anchor, b[:, :, 0, :], ALU.subtract)
                    V.tensor_tensor(x[:, :, 1, :], b[:, :, 1, :], anchor, ALU.subtract).then_inc(lvl_d, 1)

                def factors(i):
                    h = LEVELS[i]
                    dve.wait_ge(lvl_e, i + 1)
                    if i == 0:
                        dve.wait_ge(q_act, 1)
                    x = blocks(tmp[i % 2][:], h)
                    V.tensor_tensor(x[:, :, 0, :], x[:, :, 0, :], blocks(k, h)[:, :, 0, :], ALU.mult)
                    V.tensor_tensor(x[:, :, 1, :], x[:, :, 1, :], blocks(q, h)[:, :, 1, :], ALU.mult).then_inc(lvl_x, 1)

                def weights(i):
                    for t in range(NT):
                        dve.wait_ge(lvl_mm, NT * i + t + 1)
                        if i:
                            dve.wait_ge(att_done, NT * (i - 1) + t + 1)
                        V.copy_predicated(att[:, t], lvl_mask[:, i:i + 1, :].bitcast(U32).to_broadcast([P, WT, P]),
                                          bank[t][:].rearrange("p (h n) -> p h n", h=WT)).then_inc(att_done, 1)

                exponents(0)
                for i in range(NL):
                    if i + 1 < NL:
                        exponents(i + 1)
                    factors(i)
                    weights(i)
                dve.wait_ge(lvl_mm, NT * NL)
                d4 = "p h (n r) -> p (h n) r"
                n8 = WT * SEQ // DIAG
                b8 = cumb.rearrange(d4, r=DIAG)
                V.tensor_tensor(tmp[0][:].rearrange(d4, r=DIAG), b8,
                                b8[:, :, DIAG // 2 - 1:DIAG // 2].to_broadcast([P, n8, DIAG]), ALU.subtract).then_inc(lvl_d, 1)
                dve.wait_ge(lvl_e, NL + 1)
                V.tensor_tensor(tmp[0][:], tmp[0][:], q, ALU.mult)
                V.tensor_tensor(tmp[1][:], tmp[1][:], k, ALU.mult).then_inc(lvl_x, 1)
                weights(NL)
                bt = cumb.rearrange("p h (t n) -> p (h t) n", n=P)
                V.tensor_tensor(tmp[0][:].rearrange("p h (t n) -> p (h t) n", n=P),
                                bt[:, :, P - 1:P].to_broadcast([P, WT * NT, P]), bt, ALU.subtract).then_inc(kd_d, 1)
                dve.wait_ge(kd_e, 1)
                V.tensor_tensor(tmp[0][:], tmp[0][:], k, ALU.mult).then_inc(kd_x, 1)
                dve.wait_ge(kd_e, 2)
                V.tensor_tensor(q, q, cumb, ALU.mult).then_inc(qin_x, 1)
                for t in range(NT - 1):
                    dve.wait_ge(ds_mm, t + 1)
                    dve.wait_ge(o_mm, t + 1)
                    if t == 0:
                        V.tensor_copy(flat(state), bank[2][:]).then_inc(s_upd, 1)
                        continue
                    dve.wait_ge(s_upd, t)
                    for h in range(WT):
                        ins = V.scalar_tensor_tensor(out=state[:, h, :], in0=state[:, h, :], scalar=decay[:, h, t:t + 1],
                                                     in1=bank[2 + t % 2][:, h * P:(h + 1) * P], op0=ALU.mult, op1=ALU.add)
                    ins.then_inc(s_upd, 1)
                dve.wait_ge(o_kept, NT)
                sq = cumb
                link(V.tensor_tensor(sq, tmp[0][:], tmp[0][:], ALU.mult))
                link(V.tensor_reduce(ss[:], sq.rearrange("p t (h n) -> p t h n", h=WT), AX, ALU.add))
                V.tensor_scalar(ss[:], ss[:], 1.0 / P, RMS_EPS, ALU.mult, ALU.add).then_inc(ss_ready, 1)
                dve.wait_ge(ss_sqrt, 1)
                link(V.reciprocal(rms[:], rms[:]))
                o4 = tmp[0][:].rearrange("p t (h n) -> p (t h) n", h=WT)
                link(V.tensor_tensor(o4, o4, rms[:].rearrange("p t h -> p (t h)").unsqueeze(2).to_broadcast([P, NT * WT, P]), ALU.mult))
                dve.wait_ge(hg_act, 1)
                V.tensor_tensor(tmp[0][:], tmp[0][:], hg, ALU.mult).then_inc(o_normed, 1)
                for n in range(WT * NT + 1):
                    if n < WT * NT:
                        cols = (n % NT + 1) * P
                        dve.wait_ge(fx_mm, n + 1)
                        V.tensor_reduce(fmax[:, n:n + 1], bank[4 + n % 2][:, 0:cols], AX, ALU.max, negate=True).then_inc(fx_max, 1)
                    if n:
                        m = n - 1
                        cols = (m % NT + 1) * P
                        dve.wait_ge(fx_exp, m + 1)
                        link(V.reciprocal(fsum[:, m:m + 1], fsum[:, m:m + 1]))
                        V.tensor_scalar(prob[:, m % 2, 0:cols], prob[:, m % 2, 0:cols], fsum[:, m:m + 1], None,
                                        ALU.mult).then_inc(fx_p, 1)


def _layout(x, shape, order):
    import numpy as np
    return np.ascontiguousarray(np.asarray(x).reshape(shape).transpose(order))


def kernel(**inputs):
    import numpy as np
    import concourse.bacc as bacc
    from concourse.bass_utils import run_bass_kernel_spmd

    L = DEPTH
    i = {n: np.asarray(x) for n, x in inputs.items()}
    w_in = i["w_in"]
    blocks = w_in[:, :, :10 * W].reshape(L, KT, P, 10, W)[:, :, :, list(W_IN_ORDER), :]
    arrays = {
        "x": np.ascontiguousarray(i["x"]),
        "hgrn_lb_logits": _layout(i["hgrn_lb_logits"], (L, WT, P), (2, 0, 1)),
        "w_in": np.ascontiguousarray(blocks.transpose(0, 3, 2, 1, 4)),
        "w_ff": _layout(w_in[:, :, 10 * W:], (L, KT, P, WT), (0, 2, 1, 3)),
        "b_fox_f": _layout(i["b_fox_f"], (L, WT, 1), (0, 1, 2)),
        "pool_w": _layout(i["pool_w"], (L, WT, P, P), (0, 2, 1, 3)),
        "pool_scale": _layout(i["pool_scale"], (L, WT, P), (0, 2, 1)),
        "hgrn_norm_g": _layout(i["hgrn_norm_g"], (L, P, 1), (0, 1, 2)),
        "gmlp_ln_g": np.ascontiguousarray(i["gmlp_ln_g"]),
        "gmlp_ln_b": np.ascontiguousarray(i["gmlp_ln_b"]),
        "gmlp_ws": _layout(i["gmlp_ws"], (L, WT, P, P), (0, 3, 1, 2)),
        "gmlp_bs": _layout(i["gmlp_bs"], (L, WT * P), (0, 1)),
        "w_gate": _layout(i["w_gate"], (L, KT, P, 4, KT, P), (0, 4, 2, 3, 1, 5)),
        "b_gate": _layout(i["b_gate"], (L, 4, KT, P), (0, 3, 2, 1)),
        "w_branch": _layout(i["w_branch"], (L, 4, WT, P, KT, P), (0, 4, 3, 1, 2, 5)),
        "w_out": _layout(i["w_out"], (L, KT, P, D_MODEL), (0, 2, 1, 3)),
        "peer_wq": _layout(i["peer_wq"], (L, KT, P, 4, 512), (0, 3, 2, 1, 4)),
        "peer_keys": _layout(i["peer_keys"], (L, 2, PEER_HEADS, P, P), (0, 4, 2, 1, 3)).reshape(L, P, N_LISTS, P),
        "peer_u": _layout(i["peer_u"], (L, P, NG, EC, KT, P), (0, 2, 5, 3, 4, 1)),
        "peer_v": _layout(i["peer_v"], (L, P, P, D_MODEL), (0, 1, 2, 3)),
    }
    for n in ("ln1_g", "ln1_b", "ln2_g", "ln2_b"):
        arrays[n] = np.ascontiguousarray(i[n])

    nc = bacc.Bacc("TRN2", target_bir_lowering=False, num_devices=1)
    a = {n: nc.dram_tensor(f"{n}_dram", x.shape, mybir.dt.from_np(x.dtype), kind="ExternalInput").ap() for n, x in arrays.items()}
    a["gates"] = nc.dram_tensor("gates_scratch", (P, NTB, P, TB), F32, kind="Internal").ap()
    a["out"] = nc.dram_tensor("out_dram", (1, SEQ, D_MODEL), F32, kind="ExternalOutput").ap()
    build_program(nc, a)
    r = run_bass_kernel_spmd(nc, [{f"{n}_dram": x for n, x in arrays.items()}], core_ids=[0])
    return r.results[0]["out_dram"]
```

```python
import math
from contextlib import ExitStack

import concourse.bass as bass
from concourse import mybir

F32 = mybir.dt.float32
F32R = mybir.dt.float32r
U32 = mybir.dt.uint32
ALU = mybir.AluOpType
ACT = mybir.ActivationFunctionType
AX = mybir.AxisListType.X
ds = bass.ds

P = 128
D_MODEL = 1024
SEQ = 512
DEPTH = 2
KT = D_MODEL // P
NT = SEQ // P
W = D_MODEL // 2
WT = W // P
POOL_WINDOWS = (2, 4, 8, 16)
PEER_HEADS = 8
TOPK = 16
PAIRS = PEER_HEADS * TOPK
N_LISTS = 2 * PEER_HEADS
ALPHA = (2.0 * DEPTH) ** 0.25
LN_EPS = 1e-5
RMS_EPS = 1e-6
NEG_BIG = -1e30
LOWEST = -3.0e38
FOX_SCALE = float(P) ** -0.5
LEVELS = (64, 32, 16, 8)
DIAG = 8
EC = 4
NG = P // EC
TB = 64
NTB = SEQ // TB

T_POOL, T_HQ, T_GU, T_FQ, T_HF, T_FK = range(6)
N_HI, N_HG, N_GV, N_FV = range(4)
W_IN_ORDER = (0, 1, 5, 7, 2, 8, 3, 4, 6, 9)


def make_link(eng, sem, start=0):
    done = [0]

    def link(ins):
        done[0] += 1
        ins.then_inc(sem, 1)
        eng.wait_ge(sem, start + done[0])

    link.done = done
    return link


def as_f32(v):
    return v.bitcast(F32)


def matmul_split(nc, out, lhsT, rhs, first, last):
    (lh, ll), (rh, rl) = lhsT, rhs
    nc.tensor.matmul(out, lh, rl, start=first, stop=False)
    nc.tensor.matmul(out, lh, rh, start=False, stop=False)
    return nc.tensor.matmul(out, ll, rh, start=False, stop=last)


def build_program(nc, a):
    with ExitStack() as whole:
        sems = {}

        def sem(name):
            if name not in sems:
                sems[name] = whole.enter_context(nc.semaphore(name))
            return sems[name]

        def sb(ctx, name, shape, dt=F32):
            return ctx.enter_context(nc.sbuf_tensor(name, shape, dt))

        bank = [whole.enter_context(nc.psum_tensor(f"bank{i}", [P, 512], F32)) for i in range(8)]

        xh = sb(whole, "xT_high", [P, KT, SEQ], F32R)
        xl = sb(whole, "xT_low", [P, KT, SEQ], F32R)
        ident = sb(whole, "ident", [P, P])
        iota_row = sb(whole, "iota_row", [P, P])
        lvl_mask = sb(whole, "lvl_mask", [P, len(LEVELS) + 1, P])
        neg_mask = sb(whole, "neg_mask", [P, P])
        head_sel = sb(whole, "head_sel", [WT, WT, P])
        pool_rc = sb(whole, "pool_rc", [P, WT, 16])
        scan_keep = sb(whole, "scan_keep", [P, SEQ])
        one_minus_lb = sb(whole, "one_minus_lb", [P, DEPTH, WT])

        s_const = sem("const_done")
        s_chain_v = sem("dve_chain")
        s_chain_a = sem("act_chain")
        s_chain_p = sem("pool_chain")

        def clear(prefix=""):
            with nc.Block() as block:

                @block.gpsimd
                def _(pool):
                    for name, s in sems.items():
                        if name.startswith(prefix):
                            pool.sem_clear(s)

        def norm_stage(tag, x_tok, load_g, load_b, out_proj=None):
            x_dram = a["out"].rearrange("o (t p) d -> p (o t) d", p=P)
            with ExitStack() as ctx:
                g_row = sb(ctx, f"{tag}_g", [P, D_MODEL])
                b_row = sb(ctx, f"{tag}_b", [P, D_MODEL])
                r = sb(ctx, f"{tag}_r", [P, 2, D_MODEL])
                stats = sb(ctx, f"{tag}_stats", [P, 2, 2, 6])
                mv = sb(ctx, f"{tag}_mv", [P, NT, 2])
                std = sb(ctx, f"{tag}_std", [P, NT])
                rstd = sb(ctx, f"{tag}_rstd", [P, NT])
                rows_in = sem(f"ln_rows_in")
                x_in, x_out = sem(f"ln_x_in"), sem(f"ln_x_out")
                sum_ready = sem(f"ln_sum_ready")
                sum_used = sem(f"ln_sum_used")
                var_ready = sem(f"ln_var_ready")
                std_ready = sem(f"ln_std_ready")
                x_ready = sem(f"ln_x_ready")
                turned = sem(f"ln_turned")
                high_done = sem(f"ln_high_done")
                low_done = sem(f"ln_low_done")
                chain = sem(f"ln_chain")
                w_in = [sem(f"ln_w_in{j}") for j in range(4)]
                w_high = sem(f"ln_w_high")
                w_low = sem(f"ln_w_low")
                if out_proj:
                    w_dram, merged = out_proj
                    w_raw = sb(ctx, "wo_raw", [P, 4, D_MODEL])
                    wh = sb(ctx, "wo_high", [P, KT, D_MODEL], F32R)
                    wl = sb(ctx, "wo_low", [P, KT, D_MODEL], F32R)
                    mh = sb(ctx, "merged_high", [P, KT, SEQ], F32R)
                    ml = sb(ctx, "merged_low", [P, KT, SEQ], F32R)
                with nc.Block() as block:

                    @block.sync
                    def _(sp):
                        if out_proj:
                            for j in range(4):
                                if j >= 2:
                                    sp.wait_ge(w_low, 2 * j - 2)
                                sp.dma_start(w_raw[:, j % 2 * 2:j % 2 * 2 + 2, :], w_dram[:, 2 * j:2 * j + 2, :]).then_inc(w_in[j], 16)
                            sp.dma_start(x_tok[:], x_dram).then_inc(x_in, 16)
                        sp.dma_start(g_row[:], load_g).then_inc(rows_in, 16)
                        sp.dma_start(b_row[:], load_b).then_inc(rows_in, 16)
                        if not out_proj:
                            for t in range(NT):
                                sp.wait_ge(x_ready, t + 1)
                                sp.dma_start(x_dram[:, t], x_tok[:, t]).then_inc(x_out, 16)
                            sp.wait_ge(x_out, 16 * NT)

                    @block.tensor
                    def _(pe):
                        def project(pair):
                            for k in range(KT):
                                if pair == 0:
                                    pe.wait_ge(w_low, k + 1)
                                for j in range(4):
                                    t, half = 2 * pair + j // 2, j % 2
                                    tok, cols = slice(t * P, (t + 1) * P), slice(half * 512, (half + 1) * 512)
                                    mm = matmul_split(nc, bank[4 * pair + j][:], (mh[:, k, tok], ml[:, k, tok]),
                                                      (wh[:, k, cols], wl[:, k, cols]), k == 0, k == KT - 1)
                            mm.then_inc(sum_ready, 1)

                        def turn(t):
                            pe.wait_ge(x_ready, t + 1)
                            for half in range(2):
                                if t >= 2:
                                    pe.wait_ge(low_done, 2 * (t - 2) + half + 1)
                                for q in range(4):
                                    k = 4 * half + q
                                    tr = nc.tensor.transpose(bank[2 * (t % 2) + half][:, q * P:(q + 1) * P],
                                                             x_tok[:, t, k * P:(k + 1) * P], ident[:])
                                tr.then_inc(turned, 1)

                        if out_proj:
                            project(0)
                            project(1)
                            pe.wait_ge(sum_used, 4)
                        for t in range(NT):
                            turn(t)

                    @block.vector
                    def _(dve):
                        link = make_link(dve, chain)

                        def low(t):
                            for half in range(2):
                                dve.wait_ge(high_done, 2 * t + half + 1)
                                s = (slice(None), slice(4 * half, 4 * half + 4), slice(t * P, (t + 1) * P))
                                nc.vector.tensor_tensor(xl[s], bank[2 * (t % 2) + half][:].rearrange("p (q n) -> p q n", q=4),
                                                        as_f32(xh[s]), ALU.subtract).then_inc(low_done, 1)

                        if out_proj:
                            for k in range(KT):
                                dve.wait_ge(w_high, k + 1)
                                nc.vector.tensor_tensor(ml[:, k, :], merged[:, k, :], as_f32(mh[:, k, :]), ALU.subtract)
                                nc.vector.tensor_tensor(wl[:, k, :], w_raw[:, k % 4, :], as_f32(wh[:, k, :]),
                                                        ALU.subtract).then_inc(w_low, 1)
                        for t in range(NT):
                            rt = r[:, t % 2, :]
                            for half in range(2):
                                cols = slice(half * 512, (half + 1) * 512)
                                if out_proj and t + half == 0:
                                    dve.wait_ge(x_in, 16)
                                if out_proj:
                                    dve.wait_ge(sum_ready, t // 2 + 1)
                                    nc.vector.scalar_tensor_tensor(out=x_tok[:, t, cols], in0=x_tok[:, t, cols], scalar=ALPHA,
                                                                   in1=bank[2 * t + half][:], op0=ALU.mult,
                                                                   op1=ALU.add).then_inc(sum_used, 1)
                                    dve.wait_ge(sum_used, 2 * t + half + 1)
                                link(nc.vector.bn_stats(stats[:, t % 2, half, :], x_tok[:, t, cols]))
                            link(nc.vector.bn_aggr(mv[:, t, :], stats[:, t % 2, :, :]))
                            nc.vector.tensor_scalar(std[:, t:t + 1], mv[:, t, 1:2], LN_EPS, None, ALU.add).then_inc(var_ready, 1)
                            if t:
                                low(t - 1)
                            dve.wait_ge(std_ready, t + 1)
                            link(nc.vector.reciprocal(rstd[:, t:t + 1], std[:, t:t + 1]))
                            link(nc.vector.tensor_scalar(rt, x_tok[:, t, :], mv[:, t, 0:1], rstd[:, t:t + 1], ALU.subtract, ALU.mult))
                            if t == 0:
                                dve.wait_ge(rows_in, 32)
                            link(nc.vector.tensor_tensor(rt, rt, g_row[:], ALU.mult))
                            nc.vector.tensor_tensor(x_tok[:, t, :], rt, b_row[:], ALU.add).then_inc(x_ready, 1)
                        low(NT - 1)

                    @block.scalar
                    def _(act):
                        def high(t):
                            for half in range(2):
                                act.wait_ge(turned, 2 * t + half + 1)
                                nc.scalar.activation(xh[:, 4 * half:4 * half + 4, t * P:(t + 1) * P],
                                                     bank[2 * (t % 2) + half][:].rearrange("p (q n) -> p q n", q=4),
                                                     ACT.Copy).then_inc(high_done, 1)
                        if out_proj:
                            for k in range(KT):
                                nc.scalar.activation(mh[:, k, :], merged[:, k, :], ACT.Copy)
                                act.wait_ge(w_in[k // 2], 16)
                                nc.scalar.activation(wh[:, k, :], w_raw[:, k % 4, :], ACT.Copy).then_inc(w_high, 1)
                        for t in range(NT):
                            act.wait_ge(var_ready, t + 1)
                            nc.scalar.activation(std[:, t:t + 1], std[:, t:t + 1], ACT.Sqrt).then_inc(std_ready, 1)
                            if t >= 1:
                                high(t - 1)
                        high(NT - 1)

        def project_stage(tag, w_dram, pairs_T, dst_T, pairs_N=0, dst_N=None, small=None):
            with ExitStack() as ctx:
                raw = sb(ctx, f"{tag}_raw", [P, 2, KT // 2, 512])
                wh = sb(ctx, f"{tag}_wh", [P, 2, KT, 512], F32R)
                wl = sb(ctx, f"{tag}_wl", [P, 2, KT, 512], F32R)
                loaded = [sem(f"pj_w_loaded{r}") for r in range(2)]
                w_high = sem(f"pj_w_high")
                w_low = sem(f"pj_w_low")
                mm_done = sem(f"pj_mm_done")
                kept_a = sem(f"pj_kept_a")
                kept_v = sem(f"pj_kept_v")
                small_in = sem(f"pj_small_in")
                small_h = sem(f"pj_small_h")
                small_l = sem(f"pj_small_l")
                n_pairs = pairs_T + pairs_N
                if small:
                    sh = sb(ctx, f"{tag}_sh", [P, KT, WT], F32R)
                    sl = sb(ctx, f"{tag}_sl", [P, KT, WT], F32R)
                with nc.Block() as block:

                    @block.sync
                    def _(sp):
                        with sp.Fori(0, n_pairs) as i:
                            for b in range(2):
                                for r in range(2):
                                    sp.wait_ge(w_low, 4 * i + 2 * b + r + 1)
                                    sp.dma_start(raw[:, r], w_dram(2 * i + b)[:, 4 * r:4 * r + 4, :]).then_inc(loaded[r], 16)
                        if small:
                            sp.dma_start(small[0][:], small[1]).then_inc(small_in, 16)

                    @block.tensor
                    def _(pe):
                        pe.sem_inc(mm_done, 8)

                        def pair(i, token_major):
                            for b in range(2):
                                for q in range(4):
                                    n = 4 * b + q
                                    cols = slice(q * P, (q + 1) * P)
                                    pe.wait_ge((kept_a, kept_v)[n % 2], 4 * i + n // 2 + 1)
                                    for k in range(KT):
                                        if q == 0 and k % 4 == 0:
                                            pe.wait_ge(w_low, 4 * i + 2 * b + k // 4 + 3)
                                        x2 = (xh[:, k, cols], xl[:, k, cols]) if token_major else (xh[:, k, :], xl[:, k, :])
                                        w2 = ((wh[:, b, k, :], wl[:, b, k, :]) if token_major else
                                              (wh[:, b, k, cols], wl[:, b, k, cols]))
                                        lhsT, rhs = (x2, w2) if token_major else (w2, x2)
                                        mm = matmul_split(nc, bank[n][:], lhsT, rhs, k == 0, k == KT - 1)
                                    mm.then_inc(mm_done, 1)

                        with pe.Fori(0, pairs_T) as i:
                            pair(i, False)
                        if pairs_N:
                            with pe.Fori(pairs_T, n_pairs) as i:
                                pair(i, True)
                        if small:
                            pe.wait_ge(small_l, 1)
                            pe.wait_ge(kept_a, 4 * n_pairs + 1)
                            for k in range(KT):
                                mm = matmul_split(nc, bank[0][0:WT, :], (sh[:, k, :], sl[:, k, :]), (xh[:, k, :], xl[:, k, :]),
                                                  k == 0, k == KT - 1)
                            mm.then_inc(mm_done, 1)

                    def split_and_keep(eng, split, copy, kept, parity):
                        eng.sem_inc(kept, 4)

                        def out(i, b, dst, first):
                            for n in range(4 * b + parity, 4 * b + 4, 2):
                                eng.wait_ge(mm_done, 8 * i + n + 9)
                                copy(dst[:, 2 * (i - first) + n // 4, n % 4, :], bank[n][:]).then_inc(kept, 1)

                        split(0, 0)
                        if pairs_N:
                            with eng.Fori(0, pairs_T) as i:
                                split(i, 1)
                                out(i, 0, dst_T, 0)
                                split(i + 1, 0)
                                out(i, 1, dst_T, 0)
                            if pairs_N > 1:
                                with eng.Fori(pairs_T, n_pairs - 1) as i:
                                    split(i, 1)
                                    out(i, 0, dst_N, pairs_T)
                                    split(i + 1, 0)
                                    out(i, 1, dst_N, pairs_T)
                            dst, first = dst_N, pairs_T
                        else:
                            with eng.Fori(0, pairs_T - 1) as i:
                                split(i, 1)
                                out(i, 0, dst_T, 0)
                                split(i + 1, 0)
                                out(i, 1, dst_T, 0)
                            dst, first = dst_T, 0
                        i = n_pairs - 1
                        split(i, 1)
                        out(i, 0, dst, first)
                        out(i, 1, dst, first)

                    @block.scalar
                    def _(act):
                        def high(i, b):
                            act.wait_ge(mm_done, 8 * i + 4 * b + 4)
                            for r in range(2):
                                act.wait_ge(loaded[r], 32 * i + 16 * b + 16)
                                nc.scalar.activation(wh[:, b, 4 * r:4 * r + 4, :], raw[:, r], ACT.Copy).then_inc(w_high, 1)

                        split_and_keep(act, high, lambda o, i: nc.scalar.activation(o, i, ACT.Copy), kept_a, 0)
                        if small:
                            act.wait_ge(small_in, 16)
                            nc.scalar.activation(sh[:], small[0][:], ACT.Copy).then_inc(small_h, 1)

                    @block.vector
                    def _(dve):
                        dve.sem_inc(w_low, 2)

                        def low(i, b):
                            for r in range(2):
                                dve.wait_ge(w_high, 4 * i + 2 * b + r + 1)
                                nc.vector.tensor_tensor(wl[:, b, 4 * r:4 * r + 4, :], raw[:, r], as_f32(wh[:, b, 4 * r:4 * r + 4, :]),
                                                        ALU.subtract).then_inc(w_low, 1)

                        split_and_keep(dve, low, lambda o, i: nc.vector.tensor_copy(o, i), kept_v, 1)
                        if small:
                            dve.wait_ge(small_h, 1)
                            nc.vector.tensor_tensor(sl[:], small[0][:], as_f32(sh[:]), ALU.subtract).then_inc(small_l, 1)
                            dve.wait_ge(mm_done, 8 * n_pairs + 9)
                            nc.vector.tensor_copy(small[2][:], bank[0][0:WT, :]).then_inc(kept_v, 1)

        with ExitStack() as ctx:
            x_tok = sb(ctx, "x_first", [P, NT, D_MODEL])
            x_out0 = sem("x_out0")
            lbl = sb(ctx, "lb_logits", [P, DEPTH, WT])
            lb_work = sb(ctx, "lb_work", [P, 4, WT])
            lb_exp = sb(ctx, "lb_exp", [P, DEPTH, WT])
            x_in = sem("x_in")
            lb_in = sem("lb_in")
            turned0 = sem("turned0")
            copied0 = sem("copied0")
            lb_shift = sem("lb_shift")
            lb_expd = sem("lb_expd")
            rc_seed = sem("rc_seed")
            with nc.Block() as block:

                @block.sync
                def _(sp):
                    sp.dma_start(x_tok[:], a["x"].rearrange("o (t p) d -> p (o t) d", p=P)).then_inc(x_in, 16)
                    sp.dma_start(lbl[:], a["hgrn_lb_logits"]).then_inc(lb_in, 16)
                    sp.wait_ge(x_in, 16)
                    sp.dma_start(a["out"].rearrange("o (t p) d -> p (o t) d", p=P), x_tok[:]).then_inc(x_out0, 16)
                    sp.wait_ge(x_out0, 16)

                @block.gpsimd
                def _(pool):
                    link = make_link(pool, s_chain_p)
                    link(nc.gpsimd.memset(ident[:], 0.0))
                    nc.gpsimd.affine_select(out=ident[:], in_=ident[:], compare_op=ALU.not_equal, fill=1.0, base=0,
                                            pattern=[[-1, P]], channel_multiplier=1).then_inc(s_const, 1)
                    nc.gpsimd.iota(iota_row[:], pattern=[[1, P]], base=0, channel_multiplier=0,
                                   allow_small_or_imprecise_dtypes=True)
                    for g in range(WT):
                        ins = nc.gpsimd.iota(pool_rc[:, g, :], pattern=[[1, 16]], base=1, channel_multiplier=0,
                                             allow_small_or_imprecise_dtypes=True)
                    ins.then_inc(rc_seed, 1)
                    nc.gpsimd.memset(lvl_mask[:], 0.0)
                    nc.gpsimd.memset(scan_keep[:], 1.0)
                    link(nc.gpsimd.memset(head_sel[:], 1.0))
                    nc.gpsimd.memset(scan_keep[:].rearrange("p (t n) -> p t n", t=NT)[:, :, 0:1], 0.0)
                    for h in range(WT):
                        nc.gpsimd.affine_select(out=head_sel[:, h, :], in_=head_sel[:, h, :], compare_op=ALU.is_equal,
                                                fill=0.0, base=-h, pattern=[[0, P]], channel_multiplier=1)
                    link(nc.gpsimd.memset(neg_mask[:], 0.0))
                    nc.gpsimd.affine_select(out=neg_mask[:], in_=neg_mask[:], compare_op=ALU.is_ge, fill=NEG_BIG, base=0,
                                            pattern=[[-1, P]], channel_multiplier=1)
                    for i, h in enumerate(LEVELS):
                        v = lvl_mask[:, i, :].rearrange("p (n r) -> p n r", r=2 * h)
                        link(nc.gpsimd.memset(v[:, :, h:2 * h], 1.0))
                        link(nc.gpsimd.affine_select(out=v, in_=v, compare_op=ALU.is_ge, fill=0.0, base=0,
                                                     pattern=[[-2 * h, P // (2 * h)], [0, 2 * h]], channel_multiplier=1))
                        link(nc.gpsimd.affine_select(out=v, in_=v, compare_op=ALU.is_ge, fill=0.0, base=h - 1,
                                                     pattern=[[2 * h, P // (2 * h)], [0, 2 * h]], channel_multiplier=-1))
                    v = lvl_mask[:, len(LEVELS), :].rearrange("p (n r) -> p n r", r=DIAG)
                    link(nc.gpsimd.memset(v, 1.0))
                    link(nc.gpsimd.affine_select(out=v, in_=v, compare_op=ALU.is_ge, fill=0.0, base=0,
                                                 pattern=[[-DIAG, P // DIAG], [0, DIAG]], channel_multiplier=1))
                    nc.gpsimd.affine_select(out=v, in_=v, compare_op=ALU.is_ge, fill=0.0, base=0,
                                            pattern=[[DIAG, P // DIAG], [1, DIAG]], channel_multiplier=-1)

                @block.tensor
                def _(pe):
                    pe.wait_ge(s_const, 1)
                    pe.wait_ge(x_in, 16)
                    for t in range(NT):
                        for half in range(2):
                            for q in range(4):
                                k = 4 * half + q
                                tr = nc.tensor.transpose(bank[2 * t + half][:, q * P:(q + 1) * P],
                                                         x_tok[:, t, k * P:(k + 1) * P], ident[:])
                            tr.then_inc(turned0, 1)

                @block.vector
                def _(dve):
                    link = make_link(dve, s_chain_v)
                    dve.wait_ge(rc_seed, 1)
                    for g, w in enumerate(POOL_WINDOWS):
                        ins = nc.vector.tensor_scalar(pool_rc[:, g, :], pool_rc[:, g, :], float(w), None, ALU.min)
                    link(ins)
                    nc.vector.reciprocal(pool_rc[:], pool_rc[:])
                    dve.wait_ge(lb_in, 16)
                    link(nc.vector.tensor_copy(lb_work[:, 0, :], lbl[:, 0, :]))
                    for l in range(1, DEPTH):
                        link(nc.vector.tensor_tensor(lb_work[:, 0, :], lb_work[:, 0, :], lbl[:, l, :], ALU.max))
                    for l in range(DEPTH):
                        ins = nc.vector.tensor_tensor(lbl[:, l, :], lbl[:, l, :], lb_work[:, 0, :], ALU.subtract)
                    ins.then_inc(lb_shift, 1)
                    dve.wait_ge(lb_expd, 1)
                    link(nc.vector.tensor_copy(lb_work[:, 1, :], lb_exp[:, 0, :]))
                    for l in range(1, DEPTH):
                        link(nc.vector.tensor_tensor(lb_work[:, 1, :], lb_work[:, 1, :], lb_exp[:, l, :], ALU.add))
                    link(nc.vector.reciprocal(lb_work[:, 2, :], lb_work[:, 1, :]))
                    for l in range(DEPTH):
                        ins = nc.vector.tensor_tensor(lb_exp[:, l, :], lb_exp[:, l, :], lb_work[:, 2, :], ALU.mult)
                    link(ins)
                    link(nc.vector.tensor_copy(lb_work[:, 3, :], lb_exp[:, 0, :]))
                    for l in range(DEPTH):
                        if l:
                            link(nc.vector.tensor_tensor(lb_work[:, 3, :], lb_work[:, 3, :], lb_exp[:, l, :], ALU.add))
                        link(nc.vector.tensor_tensor(one_minus_lb[:, l, :], lb_work[:, 3, :], lb_exp[:, 0, :], ALU.subtract))
                        nc.vector.tensor_scalar(one_minus_lb[:, l, :], one_minus_lb[:, l, :], -1.0, 1.0, ALU.mult, ALU.add)
                    for n in range(2 * NT):
                        s = (slice(None), slice(4 * (n % 2), 4 * (n % 2) + 4), slice(n // 2 * P, (n // 2 + 1) * P))
                        dve.wait_ge(copied0, n + 1)
                        nc.vector.tensor_tensor(xl[s], bank[n][:].rearrange("p (q n) -> p q n", q=4), as_f32(xh[s]), ALU.subtract)

                @block.scalar
                def _(act):
                    act.wait_ge(lb_shift, 1)
                    nc.scalar.activation(lb_exp[:], lbl[:], ACT.Exp).then_inc(lb_expd, 1)
                    for n in range(2 * NT):
                        t, half = n // 2, n % 2
                        act.wait_ge(turned0, n + 1)
                        nc.scalar.activation(xh[:, 4 * half:4 * half + 4, t * P:(t + 1) * P],
                                             bank[n][:].rearrange("p (q n) -> p q n", q=4), ACT.Copy).then_inc(copied0, 1)

        with nc.Fori(0, DEPTH) as layer:
            with ExitStack() as upper:
                with ExitStack() as mix:
                    projT = sb(mix, "projT", [P, 6, 4, SEQ])
                    with ExitStack() as ctx:
                        projN = sb(ctx, "projN", [P, 4, NT, W])
                        ffT = sb(ctx, "ffT", [WT, SEQ])
                        with ExitStack() as c2:
                            w_ff = sb(c2, "w_ff", [P, KT, WT])
                            project_stage("in", lambda n: a["w_in"][layer, n], 3, projT, 2, projN, (w_ff, a["w_ff"][layer], ffT))
                        mixer_stage(nc, a, layer, sb, sem, bank, projT, projN, ffT, ident, lvl_mask, neg_mask, head_sel,
                                    pool_rc, scan_keep, one_minus_lb)
                    x_tok = upper.enter_context(nc.sbuf_tensor("x_tok", [P, NT, D_MODEL], F32, side="right"))
                    merging = ExitStack()
                    merged = merging.enter_context(nc.sbuf_tensor("merged", [P, KT, SEQ], F32, side="right"))
                    merge_stage(nc, a, layer, sb, sem, bank, projT, xh, xl, merged)
                norm_stage("ln1", x_tok, a["ln1_g"][layer].partition_broadcast(P), a["ln1_b"][layer].partition_broadcast(P),
                           out_proj=(a["w_out"][layer], merged))
                merging.close()
                with ExitStack() as ffn:
                    rowT = sb(ffn, "rowT", [P, SEQ])
                    colT = sb(ffn, "colT", [P, SEQ])
                    gateT = sb(ffn, "gateT", [P, SEQ])
                    with ExitStack() as ctx:
                        qT = sb(ctx, "qT", [P, 4, 4, SEQ])
                        clear("pj_")
                        project_stage("pq", lambda n: a["peer_wq"][layer, n], 2, qT)
                        route_stage(nc, a, layer, sb, sem, bank, qT, ident, iota_row, rowT, colT, gateT)
                    spread_stage(nc, a, sb, sem, bank, iota_row, rowT, colT, gateT)
                experts_stage(nc, a, layer, sb, sem, bank, xh, xl, x_tok)
                clear("ln_")
                norm_stage("ln2", x_tok, a["ln2_g"][layer].partition_broadcast(P), a["ln2_b"][layer].partition_broadcast(P))
            clear()


def merge_stage(nc, a, layer, sb, sem, bank, projT, xh, xl, merged):
    KW = KT + WT
    with ExitStack() as ctx:
        brh = sb(ctx, "brh", [P, 2, WT, SEQ], F32R)
        brl = sb(ctx, "brl", [P, 2, WT, SEQ], F32R)
        raw = sb(ctx, "mg_raw", [P, 2, KW, P])
        wh = sb(ctx, "mg_wh", [P, 2, KW, P], F32R)
        wl = sb(ctx, "mg_wl", [P, 2, KW, P], F32R)
        b_gate = sb(ctx, "b_gate", [P, KT, 4])
        gate = sb(ctx, "gate", [P, 2, SEQ])
        prod = sb(ctx, "prod", [P, 2, SEQ])
        loaded = [sem(f"mg_loaded{b}") for b in range(2)]
        bias_in = sem("mg_bias_in")
        br_high, br_low = sem("mg_br_high"), sem("mg_br_low")
        w_high = sem("mg_w_high")
        w_low = sem("mg_w_low")
        gate_mm = sem("mg_gate_mm")
        br_mm = sem("mg_br_mm")
        gated = sem("mg_gated")
        prods = sem("mg_prods")
        added = sem("mg_added")

        def units(eng, m, body):
            with eng.Fori(0, KT // 2) as i:
                for b in range(2):
                    body(KT * m + 2 * i + b, 2 * i + b, b)

        with nc.Block() as block:

            @block.sync
            def _(sp):
                sp.dma_start(b_gate[:], a["b_gate"][layer]).then_inc(bias_in, 16)
                for m in range(4):
                    def load(n, dt, b):
                        sp.wait_ge(w_low, n + 1)
                        sp.dma_start(raw[:, b], a["w_merge"][layer, m, dt]).then_inc(loaded[b], 16)
                    units(sp, m, load)

            @block.tensor
            def _(pe):
                pe.sem_inc(br_mm, 2)
                for m in range(4):
                    pe.wait_ge(br_low, m + 1)

                    def multiply(n, dt, b):
                        pe.wait_ge(gated, n + 1)
                        pe.wait_ge(w_low, n + 3)
                        for k in range(KT):
                            mm = matmul_split(nc, bank[b][:], (wh[:, b, k, :], wl[:, b, k, :]), (xh[:, k, :], xl[:, k, :]),
                                              k == 0, k == KT - 1)
                        mm.then_inc(gate_mm, 1)
                        pe.wait_ge(prods, n + 1)
                        for k in range(WT):
                            mm = matmul_split(nc, bank[2 + b][:], (wh[:, b, KT + k, :], wl[:, b, KT + k, :]),
                                              (brh[:, m % 2, k, :], brl[:, m % 2, k, :]), k == 0, k == WT - 1)
                        mm.then_inc(br_mm, 1)
                    units(pe, m, multiply)

            @block.scalar
            def _(act):
                act.sem_inc(gated, 2)

                def split_branch(m):
                    if m >= 2:
                        act.wait_ge(br_mm, KT * (m - 1) + 2)
                    nc.scalar.activation(brh[:, m % 2], projT[:, m], ACT.Copy).then_inc(br_high, 1)

                def high(n, b):
                    act.wait_ge(br_mm, n + 1)
                    act.wait_ge(loaded[b], 16 * (n // 2) + 16 if isinstance(n, int) else 8 * (n - b) + 16)
                    nc.scalar.activation(wh[:, b], raw[:, b], ACT.Copy).then_inc(w_high, 1)

                split_branch(0)
                act.wait_ge(bias_in, 16)
                high(0, 0)
                high(1, 1)
                for m in range(4):
                    if m < 3:
                        split_branch(m + 1)

                    def sigmoids(n, dt, b, last=False):
                        act.wait_ge(gate_mm, n + 1)
                        act.wait_ge(prods, n + 1)
                        nc.scalar.activation(gate[:, b, :], bank[b][:], ACT.Sigmoid, bias=b_gate[:, ds(dt, 1), m]).then_inc(gated, 1)
                        if not last:
                            high(n + 2, b)

                    if m < 3:
                        units(act, m, sigmoids)
                    else:
                        with act.Fori(0, KT // 2 - 1) as i:
                            for b in range(2):
                                sigmoids(KT * m + 2 * i + b, 2 * i + b, b)
                        for b in range(2):
                            sigmoids(KT * m + KT - 2 + b, KT - 2 + b, b, last=True)

            @block.vector
            def _(dve):
                V = nc.vector
                dve.sem_inc(w_low, 2)
                dve.sem_inc(prods, 2)
                dve.sem_inc(added, 2)

                def split_branch(m):
                    dve.wait_ge(br_high, m + 1)
                    V.tensor_tensor(brl[:, m % 2], projT[:, m], as_f32(brh[:, m % 2]), ALU.subtract).then_inc(br_low, 1)

                def low(n, b):
                    dve.wait_ge(w_high, n + 1)
                    V.tensor_tensor(wl[:, b], raw[:, b], as_f32(wh[:, b]), ALU.subtract).then_inc(w_low, 1)

                split_branch(0)
                low(0, 0)
                low(1, 1)
                for m in range(4):
                    if m < 3:
                        split_branch(m + 1)

                    def products(n, dt, b, last=False):
                        dve.wait_ge(gated, n + 3)
                        dve.wait_ge(br_mm, n + 3)
                        dve.wait_ge(added, n + 1)
                        if m == 0:
                            V.tensor_tensor(merged[:, ds(dt, 1), :], gate[:, b:b + 1, :], bank[2 + b][:].unsqueeze(1), ALU.mult).then_inc(prods, 1)
                            V.engine_nop().then_inc(added, 1)
                        else:
                            V.tensor_tensor(prod[:, b, :], gate[:, b, :], bank[2 + b][:], ALU.mult).then_inc(prods, 1)
                            dve.wait_ge(prods, n + 3)
                            V.tensor_tensor(merged[:, ds(dt, 1), :], merged[:, ds(dt, 1), :], prod[:, b:b + 1, :], ALU.add).then_inc(added, 1)
                        if not last:
                            low(n + 2, b)

                    if m < 3:
                        units(dve, m, products)
                    else:
                        with dve.Fori(0, KT // 2 - 1) as i:
                            for b in range(2):
                                products(KT * m + 2 * i + b, 2 * i + b, b)
                        for b in range(2):
                            products(KT * m + KT - 2 + b, KT - 2 + b, b, last=True)


def route_stage(nc, a, layer, sb, sem, bank, qT, ident, iota_row, rowT, colT, gateT):
    H, K = PEER_HEADS, TOPK
    with ExitStack() as ctx:
        keys = sb(ctx, "keys", [P, N_LISTS, P])
        sc = sb(ctx, "sc", [P, N_LISTS, P])
        sc2 = sb(ctx, "sc2", [P, N_LISTS, P])
        best = sb(ctx, "best", [P, N_LISTS, K])
        best_ix = sb(ctx, "best_ix", [P, N_LISTS, K], U32)
        best_ixf = sb(ctx, "best_ixf", [P, N_LISTS, K])
        cand = sb(ctx, "cand", [P, H, K * K])
        cand2 = sb(ctx, "cand2", [P, H, K * K])
        top = sb(ctx, "top", [P, H, K])
        pos = sb(ctx, "pos", [P, H, K], U32)
        rank = sb(ctx, "rank", [P, 2, H * K], U32)
        rankf = sb(ctx, "rankf", [P, 2, H * K])
        hit = sb(ctx, "hit", [P, H * K, K])
        hit2 = sb(ctx, "hit2", [P, H * K, K])
        row = sb(ctx, "row", [P, PAIRS])
        col = sb(ctx, "col", [P, PAIRS])
        gate = sb(ctx, "pgate", [P, H, K])
        total = sb(ctx, "total", [P, H])
        keys_in = sem("rt_keys_in")
        scored = sem("rt_scored")
        sc_ready = sem("rt_sc_ready")
        sc_free = sem("rt_sc_free")
        shifted = sem("rt_shifted")
        expd = sem("rt_expd")
        routed = sem("rt_routed")
        turned = sem("rt_turned")
        taken = sem("rt_taken")
        chain = sem("rt_chain")
        with nc.Block() as block:

            @block.sync
            def _(sp):
                sp.dma_start(keys[:], a["peer_keys"][layer]).then_inc(keys_in, 16)

            @block.tensor
            def _(pe):
                def score(t):
                    for j in range(4):
                        if t:
                            pe.wait_ge(sc_ready, 4 * (t - 1) + j + 1)
                        for q in range(4):
                            n = 4 * j + q
                            mm = nc.tensor.matmul(bank[j][:, q * P:(q + 1) * P], qT[:, n // 4, n % 4, t * P:(t + 1) * P],
                                                  keys[:, n, :], start=True, stop=True)
                        mm.then_inc(scored, 1)

                def turn(t):
                    pe.wait_ge(routed, t + 1)
                    for j, src in enumerate((row, col, gate)):
                        if t:
                            pe.wait_ge(taken, 3 * (t - 1) + j + 1)
                        v = src[:] if j < 2 else src[:].rearrange("p h k -> p (h k)")
                        nc.tensor.transpose(bank[4 + j][:, 0:P], v, ident[:]).then_inc(turned, 1)

                pe.sem_inc(turned, 3)
                pe.wait_ge(keys_in, 16)
                score(0)
                for t in range(NT):
                    if t + 1 < NT:
                        score(t + 1)
                    turn(t)

            @block.scalar
            def _(act):
                def keep_scores(t):
                    if t:
                        act.wait_ge(sc_free, t)
                    for j in range(4):
                        act.wait_ge(scored, 4 * t + j + 1)
                        nc.scalar.activation(sc[:, 4 * j:4 * j + 4, :].rearrange("p q n -> p (q n)"), bank[j][:],
                                             ACT.Copy).then_inc(sc_ready, 1)

                keep_scores(0)
                for t in range(NT):
                    if t + 1 < NT:
                        keep_scores(t + 1)
                    act.wait_ge(shifted, t + 1)
                    nc.scalar.activation(gate[:], gate[:], ACT.Exp).then_inc(expd, 1)
                    for j, dst in enumerate((rowT, colT, gateT)):
                        act.wait_ge(turned, 3 * t + j + 4)
                        nc.scalar.activation(dst[:, t * P:(t + 1) * P], bank[4 + j][:, 0:P], ACT.Copy).then_inc(taken, 1)

            @block.vector
            def _(dve):
                V = nc.vector
                with dve.Fori(0, NT) as t:
                    dve.sem_clear(chain)
                    link = make_link(dve, chain)
                    dve.wait_ge(turned, 3 * t + 3)
                    link(V.memset(total[:], 0.0))
                    dve.wait_ge(sc_ready, 4 * t + 4)
                    link(V.memset(total[:], 0.0))
                    for n in range(N_LISTS):
                        ins = V.max(best[:, n, 0:8], sc[:, n, :])
                    link(ins)
                    for n in range(N_LISTS):
                        V.max_index(best_ix[:, n, 0:8], best[:, n, 0:8], sc[:, n, :])
                        ins = V.match_replace(sc2[:, n, :], best[:, n, 0:8], sc[:, n, :], LOWEST)
                    link(ins)
                    V.engine_nop().then_inc(sc_free, 1)
                    for n in range(N_LISTS):
                        ins = V.max(best[:, n, 8:16], sc2[:, n, :])
                    link(ins)
                    for n in range(N_LISTS):
                        ins = V.max_index(best_ix[:, n, 8:16], best[:, n, 8:16], sc2[:, n, :])
                    link(ins)
                    V.tensor_copy(best_ixf[:], best_ix[:])
                    pairs = best[:].rearrange("p (h two) k -> p h two k", two=2)
                    link(V.tensor_tensor(cand[:].rearrange("p h (i j) -> p h i j", i=K),
                                         pairs[:, :, 0, :].unsqueeze(3).to_broadcast([P, H, K, K]),
                                         pairs[:, :, 1, :].unsqueeze(2).to_broadcast([P, H, K, K]), ALU.add))
                    for h in range(H):
                        ins = V.max(top[:, h, 0:8], cand[:, h, :])
                    link(ins)
                    for h in range(H):
                        V.max_index(pos[:, h, 0:8], top[:, h, 0:8], cand[:, h, :])
                        ins = V.match_replace(cand2[:, h, :], top[:, h, 0:8], cand[:, h, :], LOWEST)
                    link(ins)
                    for h in range(H):
                        ins = V.max(top[:, h, 8:16], cand2[:, h, :])
                    link(ins)
                    for h in range(H):
                        ins = V.max_index(pos[:, h, 8:16], top[:, h, 8:16], cand2[:, h, :])
                    link(ins)
                    V.tensor_tensor(gate[:], top[:], top[:, :, 0:1].to_broadcast([P, H, K]), ALU.subtract).then_inc(shifted, 1)
                    pf = pos[:].rearrange("p h k -> p (h k)")
                    V.tensor_scalar(rank[:, 0, :], pf, 4, None, ALU.logical_shift_right)
                    link(V.tensor_scalar(rank[:, 1, :], pf, K - 1, None, ALU.bitwise_and))
                    link(V.tensor_copy(rankf[:], rank[:]))
                    lists = best_ixf[:].rearrange("p (h two) k -> p h two k", two=2)
                    for side, dst in enumerate((row, col)):
                        link(V.tensor_tensor(hit[:], rankf[:, side, :].unsqueeze(2).to_broadcast([P, H * K, K]),
                                             iota_row[:, 0:K].unsqueeze(1).to_broadcast([P, H * K, K]), ALU.is_equal))
                        link(V.tensor_tensor(hit2[:].rearrange("p (h k) j -> p h k j", h=H),
                                             hit[:].rearrange("p (h k) j -> p h k j", h=H),
                                             lists[:, :, side, :].unsqueeze(2).to_broadcast([P, H, K, K]), ALU.mult))
                        link(V.tensor_reduce(dst[:], hit2[:], AX, ALU.add))
                    dve.wait_ge(expd, t + 1)
                    link(V.tensor_reduce(total[:], gate[:], AX, ALU.add))
                    link(V.reciprocal(total[:], total[:]))
                    link(V.tensor_tensor(gate[:], gate[:], total[:].unsqueeze(2).to_broadcast([P, H, K]), ALU.mult))
                    V.engine_nop().then_inc(routed, 1)


def spread_stage(nc, a, sb, sem, bank, iota_row, rowT, colT, gateT):
    STEP = 16
    with ExitStack() as ctx:
        hot_row = sb(ctx, "hot_row", [P, STEP, P])
        hot_col = sb(ctx, "hot_col", [P, STEP, P])
        cols = sb(ctx, "cols", [P, 2, STEP])
        rows = sb(ctx, "rows", [P, 4, 4])
        stage = sb(ctx, "stage", [P, 2, P, TB])
        rows_hot = sem("sp_rows_hot")
        cols_hot = sem("sp_cols_hot")
        spread = sem("sp_spread")
        kept = sem("sp_kept")
        stored = [sem(f"sp_stored{b}") for b in range(2)]
        chain = sem("sp_chain")

        with nc.Block() as block:

            def steps(eng, body):
                with eng.Fori(0, NTB // 2) as m:
                    for b in range(2):
                        with eng.Fori(0, TB // STEP) as q:
                            body((2 * m + b) * (TB // STEP) + q, b, q, m)

            @block.gpsimd
            def _(pool):
                def body(n, b, q, m):
                    for g in range(4):
                        pool.wait_ge(spread, 4 * n + g + 1)
                        nc.gpsimd.tensor_copy(rows[:, g, :], rowT[:, ds(n * STEP + 4 * g, 4)])
                        pool.drain()
                        for s in range(4):
                            ins = nc.gpsimd.tensor_scalar(hot_row[:, 4 * g + s, :], iota_row[:], rows[:, g, s:s + 1], None, ALU.is_equal)
                        ins.then_inc(rows_hot, 1)
                steps(pool, body)

            @block.vector
            def _(dve):
                def body(n, b, q, m):
                    dve.wait_ge(cols_hot, 4 * n + 4)
                    nc.vector.tensor_copy(cols[:, 0, :], colT[:, ds(n * STEP, STEP)])
                    nc.vector.tensor_copy(cols[:, 1, :], gateT[:, ds(n * STEP, STEP)]).then_inc(chain, 1)
                    dve.wait_ge(chain, n + 1)
                    for g in range(4):
                        dve.wait_ge(spread, 4 * n + g + 1)
                        for s in range(4 * g, 4 * g + 4):
                            ins = nc.vector.tensor_scalar(hot_col[:, s, :], iota_row[:], cols[:, 0, s:s + 1], cols[:, 1, s:s + 1],
                                                          ALU.is_equal, ALU.mult)
                        ins.then_inc(cols_hot, 1)
                dve.sem_inc(cols_hot, 4)
                steps(dve, body)

            @block.tensor
            def _(pe):
                pe.sem_inc(spread, 4)

                def body(n, b, q, m):
                    for g in range(4):
                        pe.wait_ge(kept, 4 * n + g + 1)
                        pe.wait_ge(rows_hot, 4 * n + g + 1)
                        pe.wait_ge(cols_hot, 4 * n + g + 5)
                        for s in range(4):
                            mm = nc.tensor.matmul(bank[g][:, s * P:(s + 1) * P], hot_row[:, 4 * g + s, :], hot_col[:, 4 * g + s, :],
                                                  start=True, stop=True)
                        mm.then_inc(spread, 1)
                steps(pe, body)

            @block.scalar
            def _(act):
                act.sem_inc(kept, 4)
                act.sem_inc(stored[0], 16)
                act.sem_inc(stored[1], 16)

                def body(n, b, q, m):
                    act.wait_ge(stored[b], 16 * m + 16)
                    for g in range(4):
                        act.wait_ge(spread, 4 * n + g + 5)
                        nc.scalar.activation(stage[:, b, :, ds(q * STEP + 4 * g, 4)],
                                             bank[g][:].rearrange("p (t c) -> p c t", t=4), ACT.Copy).then_inc(kept, 1)
                steps(act, body)

            @block.sync
            def _(sp):
                per = 4 * TB // STEP
                with sp.Fori(0, NTB // 2) as m:
                    for b in range(2):
                        sp.wait_ge(kept, (2 * m + b) * per + per + 4)
                        sp.dma_start(a["gates"][:, 2 * m + b], stage[:, b]).then_inc(stored[b], 16)
                for b in range(2):
                    sp.wait_ge(stored[b], 16 * (NTB // 2) + 16)


def experts_stage(nc, a, layer, sb, sem, bank, xh, xl, x_tok):
    V, A = nc.vector, nc.scalar.activation
    H = EC // 2
    with ExitStack() as ctx:
        ur = sb(ctx, "u_raw", [P, EC, KT, P])
        uh = sb(ctx, "u_high", [P, EC, KT, P], F32R)
        ul = sb(ctx, "u_low", [P, EC, KT, P], F32R)
        vr = sb(ctx, "v_raw", [P, EC, D_MODEL])
        vh = sb(ctx, "v_high", [P, EC, D_MODEL], F32R)
        vl = sb(ctx, "v_low", [P, EC, D_MODEL], F32R)
        G = sb(ctx, "G", [P, NTB, EC, TB])
        hid = sb(ctx, "hid", [P, EC, SEQ])
        wh = sb(ctx, "w_high", [P, 2, EC, SEQ], F32R)
        wl = sb(ctx, "w_low", [P, 2, EC, SEQ], F32R)
        u_in = [sem(f"ex_u_in{r}") for r in range(2)]
        v_in, G_in = sem("ex_v_in"), sem("ex_G_in")
        u_high = sem("ex_u_high")
        u_low = sem("ex_u_low")
        v_high = sem("ex_v_high")
        v_low = sem("ex_v_low")
        h_mm = sem("ex_h_mm")
        h_act = sem("ex_h_act")
        w_mul = sem("ex_w_mul")
        w_high = sem("ex_w_high")
        w_low = sem("ex_w_low")
        y_mm = sem("ex_y_mm")
        y_add = sem("ex_y_add")
        scaled = sem("ex_scaled")

        def in_pairs(eng, body, last):
            with eng.Fori(0, NG // 2 - 1) as i:
                for b in range(2):
                    body(2 * i + b, b)
            for b in range(2):
                last(NG - 2 + b, b)

        with nc.Block() as block:

            @block.sync
            def _(sp):
                with sp.Fori(0, NG) as n:
                    for r in range(2):
                        sp.wait_ge(u_low, EC * n + H * r + H)
                        sp.dma_start(ur[:, H * r:H * r + H], a["peer_u"][layer, n, :, H * r:H * r + H]).then_inc(u_in[r], 16)
                    sp.wait_ge(w_mul, EC * n + EC)
                    sp.dma_start(G[:], a["gates"][:, :, ds(n * EC, EC), :]).then_inc(G_in, 16)
                    sp.wait_ge(v_low, EC * n + EC)
                    sp.dma_start(vr[:], a["peer_v"][layer, :, ds(n * EC, EC), :]).then_inc(v_in, 16)

            @block.tensor
            def _(pe):
                pe.sem_inc(h_mm, 4)
                pe.sem_inc(y_mm, 16)

                def hidden(n):
                    for c in range(EC):
                        pe.wait_ge(h_act, EC * n + c + 1)
                        pe.wait_ge(u_low, EC * n + c + 5)
                        for k in range(KT):
                            mm = matmul_split(nc, bank[c][:], (uh[:, c, k, :], ul[:, c, k, :]), (xh[:, k, :], xl[:, k, :]),
                                              k == 0, k == KT - 1)
                        mm.then_inc(h_mm, 1)

                def output(n, b):
                    pe.wait_ge(v_low, EC * n + EC + 4)
                    pe.wait_ge(w_low, EC * n + EC + 4)
                    for j in range(2 * NT):
                        tok, cols = slice(j // 2 * P, (j // 2 + 1) * P), slice(j % 2 * 512, (j % 2 + 1) * 512)
                        pe.wait_ge(y_add, 8 * n + j + 5)
                        for c in range(EC):
                            mm = matmul_split(nc, bank[4 + j % 4][:], (wh[:, b, c, tok], wl[:, b, c, tok]),
                                              (vh[:, c, cols], vl[:, c, cols]), c == 0, c == EC - 1)
                        mm.then_inc(y_mm, 1)

                hidden(0)
                with pe.Fori(0, NG // 2 - 1) as i:
                    hidden(2 * i + 1)
                    output(2 * i, 0)
                    hidden(2 * i + 2)
                    output(2 * i + 1, 1)
                hidden(NG - 1)
                output(NG - 2, 0)
                output(NG - 1, 1)

            @block.scalar
            def _(act):
                act.sem_inc(h_act, 4)

                def split_u(n, c):
                    act.wait_ge(u_in[c // H], 16 * n + 16)
                    act.wait_ge(h_mm, EC * n + c + 1)
                    A(uh[:, c], ur[:, c], ACT.Copy).then_inc(u_high, 1)

                def group(n, b, last=False):
                    for c in range(EC):
                        act.wait_ge(h_mm, EC * n + c + 5)
                        act.wait_ge(w_low, EC * n + c + 1)
                        A(hid[:, c, :], bank[c][:], ACT.Gelu_apprx_tanh).then_inc(h_act, 1)
                        if not last:
                            split_u(n + 1, c)
                        if c == 0:
                            act.wait_ge(y_mm, 8 * n + 8)
                        act.wait_ge(w_mul, EC * n + c + 5)
                        A(wh[:, b, c, :], hid[:, c, :], ACT.Copy).then_inc(w_high, 1)
                    act.wait_ge(v_in, 16 * n + 16)
                    act.wait_ge(y_mm, 8 * n + 16)
                    for c in range(EC):
                        A(vh[:, c, :], vr[:, c, :], ACT.Copy).then_inc(v_high, 1)

                for c in range(EC):
                    split_u(0, c)
                in_pairs(act, group, lambda n, b: group(n, b, last=(b == 1)))

            @block.vector
            def _(dve):
                dve.sem_inc(u_low, 4)
                dve.sem_inc(v_low, 4)
                dve.sem_inc(w_mul, 4)
                dve.sem_inc(w_low, 4)
                dve.sem_inc(y_add, 8)
                V.tensor_scalar(x_tok[:], x_tok[:], ALPHA, None, ALU.mult).then_inc(scaled, 1)
                dve.wait_ge(scaled, 1)

                def split_u(n, c):
                    dve.wait_ge(u_high, EC * n + c + 1)
                    V.tensor_tensor(ul[:, c], ur[:, c], as_f32(uh[:, c]), ALU.subtract).then_inc(u_low, 1)

                def weigh(n, b, last=False):
                    dve.wait_ge(G_in, 16 * n + 16)
                    for c in range(EC):
                        h = hid[:, c, :]
                        dve.wait_ge(h_act, EC * n + c + 5)
                        V.tensor_tensor(h.rearrange("p (q t) -> p q t", t=TB), h.rearrange("p (q t) -> p q t", t=TB),
                                        G[:, :, c, :], ALU.mult).then_inc(w_mul, 1)
                        if not last:
                            split_u(n + 1, c)
                        dve.wait_ge(w_high, EC * n + c + 1)
                        V.tensor_tensor(wl[:, b, c, :], h, as_f32(wh[:, b, c, :]), ALU.subtract).then_inc(w_low, 1)

                def add(n):
                    for j in range(2 * NT):
                        part = x_tok[:, j // 2, j % 2 * 512:(j % 2 + 1) * 512]
                        dve.wait_ge(y_mm, 8 * n + j + 17)
                        dve.wait_ge(y_add, 8 * n + j + 1)
                        V.tensor_tensor(part, part, bank[4 + j % 4][:], ALU.add).then_inc(y_add, 1)

                def split_v(n):
                    for c in range(EC):
                        dve.wait_ge(v_high, EC * n + c + 1)
                        V.tensor_tensor(vl[:, c, :], vr[:, c, :], as_f32(vh[:, c, :]), ALU.subtract).then_inc(v_low, 1)

                for c in range(EC):
                    split_u(0, c)
                weigh(0, 0)
                split_v(0)
                with dve.Fori(0, NG // 2 - 1) as i:
                    weigh(2 * i + 1, 1)
                    add(2 * i)
                    split_v(2 * i + 1)
                    weigh(2 * i + 2, 0)
                    add(2 * i + 1)
                    split_v(2 * i + 2)
                weigh(NG - 1, 1, last=True)
                add(NG - 2)
                split_v(NG - 1)
                add(NG - 1)


def mixer_stage(nc, a, layer, sb, sem, bank, projT, projN, ffT, ident, lvl_mask, neg_mask, head_sel,
                pool_rc, scan_keep, one_minus_lb):
    V = nc.vector
    NL = len(LEVELS)
    with ExitStack() as ctx:
        tmp = [sb(ctx, f"tmp{i}", [P, WT, SEQ]) for i in range(2)]
        att = sb(ctx, "att", [P, NT, WT, P])
        state = sb(ctx, "state", [P, WT, P])
        decay = sb(ctx, "decay", [P, WT, NT])
        ss = sb(ctx, "ss", [P, NT, WT])
        rms = sb(ctx, "rms", [P, NT, WT])
        pool_w = sb(ctx, "pool_w", [P, WT, P])
        pool_scale = sb(ctx, "pool_scale", [P, WT])
        norm_g = sb(ctx, "norm_g", [P, 1])
        ws = sb(ctx, "ws", [P, WT, P])
        bs_row = sb(ctx, "bs_row", [P, WT, P])
        lng_row = sb(ctx, "lng_row", [P, W])
        lnb_row = sb(ctx, "lnb_row", [P, W])
        gstats = sb(ctx, "gstats", [P, NT, 6])
        gmv = sb(ctx, "gmv", [P, NT, 2])
        gstd = sb(ctx, "gstd", [P, NT])
        b_fox = sb(ctx, "b_fox", [WT, 1])
        fz = sb(ctx, "fz", [WT, 2, SEQ])
        fones = sb(ctx, "fones", [WT, 1])
        cum = sb(ctx, "cum", [WT, 2, SEQ])
        fmax = sb(ctx, "fmax", [P, 16])
        fsum = sb(ctx, "fsum", [P, 16])
        prob = sb(ctx, "prob", [P, 2, SEQ])
        probT = sb(ctx, "probT", [P, 2, SEQ])

        pin, q, k, gu, fq, fk = (projT[:, j] for j in (T_POOL, T_HQ, T_HF, T_GU, T_FQ, T_FK))
        val, hg, gv, fv = (projN[:, j] for j in (N_HI, N_HG, N_GV, N_FV))
        cumb = sb(ctx, "cumb", [P, WT, SEQ])[:]

        def flat(v):
            return v.rearrange("p h t -> p (h t)")

        params_in = {n: sem(f"mx_{n}_in") for n in ("poolw", "pools", "normg", "ws", "bs", "lng", "lnb", "bfox")}
        ws_masked = sem("mx_ws_masked")
        fones_done = sem("mx_fones_done")
        q_act, hg_act, gu_act, gv_act, sig_done, logf_done = (sem(f"mx_{n}") for n in ("q_act", "hg_act", "gu_act", "gv_act", "sig_done", "logf_done"))
        diff_ready, pool_mm, pool_kept = sem("mx_diff_ready"), sem("mx_pool_mm"), sem("mx_pool_kept")
        gvar, gsqrt, gnorm, gm_mm, gm_used = (sem(f"mx_{n}") for n in ("gvar", "gsqrt", "gnorm", "gm_mm", "gm_used"))
        k_ready, lvl_d, lvl_e, lvl_x, lvl_mm, att_done = (sem(f"mx_{n}") for n in ("k_ready", "lvl_d", "lvl_e", "lvl_x", "lvl_mm", "att_done"))
        kd_d, kd_e, kd_x, qin_x, kd_turned, kd_kept = (sem(f"mx_{n}") for n in ("kd_d", "kd_e", "kd_x", "qin_x", "kd_turned", "kd_kept"))
        o_mm, o_kept, ds_mm, s_upd, ss_ready, ss_sqrt, o_normed, o_turned = (
            sem(f"mx_{n}") for n in ("o_mm", "o_kept", "ds_mm", "s_upd", "ss_ready", "ss_sqrt", "o_normed", "o_turned"))
        fz_ready, fz_exp, c_ready, fq_ready = (sem(f"mx_{n}") for n in ("fz_ready", "fz_exp", "c_ready", "fq_ready"))
        fx_mm, fx_max, fx_exp, fx_p, fx_turned, fx_pt, fx_o, fx_kept = (
            sem(f"mx_{n}") for n in ("fx_mm", "fx_max", "fx_exp", "fx_p", "fx_turned", "fx_pt", "fx_o", "fx_kept"))
        chain = sem("mx_chain")
        chain_a = sem("mx_chain_a")

        with nc.Block() as block:

            @block.sync
            def _(sp):
                for name, dst, src in (
                        ("bfox", b_fox, a["b_fox_f"][layer]), ("poolw", pool_w, a["pool_w"][layer]),
                        ("pools", pool_scale, a["pool_scale"][layer]),
                        ("lng", lng_row, a["gmlp_ln_g"][layer].partition_broadcast(P)),
                        ("lnb", lnb_row, a["gmlp_ln_b"][layer].partition_broadcast(P)),
                        ("ws", ws, a["gmlp_ws"][layer]), ("normg", norm_g, a["hgrn_norm_g"][layer])):
                    sp.dma_start(dst[:], src).then_inc(params_in[name], 16)
                sp.dma_start(bs_row[:].rearrange("p g t -> p (g t)"),
                             a["gmlp_bs"][layer].partition_broadcast(P)).then_inc(params_in["bs"], 16)

            @block.gpsimd
            def _(pool):
                nc.gpsimd.memset(fones[:], 1.0).then_inc(fones_done, 1)
                pool.wait_ge(params_in["ws"], 16)
                nc.gpsimd.affine_select(out=ws[:], in_=ws[:], compare_op=ALU.is_ge, fill=0.0, base=0,
                                        pattern=[[0, WT], [1, P]], channel_multiplier=-1).then_inc(ws_masked, 1)

            @block.tensor
            def _(pe):
                pe.wait_ge(params_in["poolw"], 16)
                for g in range(WT):
                    pe.wait_ge(diff_ready, g + 1)
                    if g >= 2:
                        pe.wait_ge(pool_kept, g - 1)
                    nc.tensor.matmul(bank[6 + g % 2][:], pool_w[:, g, :], pin[:, g, :], start=True, stop=True).then_inc(pool_mm, 1)
                pe.wait_ge(ws_masked, 1)
                pe.wait_ge(gnorm, 1)
                for g in range(WT):
                    if g < 2:
                        pe.wait_ge(pool_kept, 3 + g)
                    else:
                        pe.wait_ge(gm_used, g - 1)
                    for t in range(NT):
                        mm = nc.tensor.matmul(bank[6 + g % 2][:, t * P:(t + 1) * P], gv[:, t, g * P:(g + 1) * P], ws[:, g, :],
                                              start=True, stop=True)
                    mm.then_inc(gm_mm, 1)
                for i in range(NL + 1):
                    pe.wait_ge(lvl_x, i + 1)
                    kk = tmp[i % 2] if i < NL else tmp[1]
                    qq = tmp[i % 2] if i < NL else tmp[0]
                    for t in range(NT):
                        if i:
                            pe.wait_ge(att_done, NT * (i - 1) + t + 1)
                        for h in range(WT):
                            mm = nc.tensor.matmul(bank[t][:, h * P:(h + 1) * P], kk[:, h, t * P:(t + 1) * P],
                                                  qq[:, h, t * P:(t + 1) * P], start=True, stop=True)
                        mm.then_inc(lvl_mm, 1)
                pe.wait_ge(kd_x, 1)
                for t in range(NT):
                    pe.wait_ge(att_done, NT * NL + t + 1)
                    for h in range(WT):
                        mm = nc.tensor.transpose(bank[t][:, h * P:(h + 1) * P], tmp[0][:, h, t * P:(t + 1) * P], ident[:])
                    mm.then_inc(kd_turned, 1)
                pe.wait_ge(kd_kept, NT)
                pe.wait_ge(qin_x, 1)
                for t in range(NT):
                    if t < NT - 1:
                        if t >= 2:
                            pe.wait_ge(s_upd, t - 1)
                        for h in range(WT):
                            mm = nc.tensor.matmul(bank[2 + t % 2][:, h * P:(h + 1) * P], tmp[1][:, t, h * P:(h + 1) * P],
                                                  val[:, t, h * P:(h + 1) * P], start=True, stop=True)
                        mm.then_inc(ds_mm, 1)
                    if t >= 2:
                        pe.wait_ge(o_kept, t - 1)
                    if t:
                        pe.wait_ge(s_upd, t)
                    for h in range(WT):
                        mm = nc.tensor.matmul(bank[t % 2][:, h * P:(h + 1) * P], att[:, t, h, :], val[:, t, h * P:(h + 1) * P],
                                              start=True, stop=(t == 0))
                        if t:
                            mm = nc.tensor.matmul(bank[t % 2][:, h * P:(h + 1) * P], q[:, h, t * P:(t + 1) * P], state[:, h, :],
                                                  start=False, stop=True)
                    mm.then_inc(o_mm, 1)
                pe.wait_ge(o_normed, 1)
                for t in range(NT):
                    for h in range(WT):
                        mm = nc.tensor.transpose(bank[t][:, h * P:(h + 1) * P], tmp[0][:, t, h * P:(h + 1) * P], ident[:])
                    mm.then_inc(o_turned, 1)
                pe.wait_ge(fq_ready, 1)
                pe.wait_ge(c_ready, 2)

                def logits(n):
                    h, t = divmod(n, NT)
                    cols = (t + 1) * P
                    b = bank[4 + n % 2]
                    if n >= 2:
                        pe.wait_ge(fx_exp, n - 1)
                    nc.tensor.matmul(b[:, 0:cols], fq[:, h, t * P:(t + 1) * P], fk[:, h, 0:cols], start=True, stop=False)
                    nc.tensor.matmul(b[:, 0:cols], cum[:, 0, t * P:(t + 1) * P], head_sel[:, h, 0:1].to_broadcast([WT, cols]), start=False, stop=False)
                    nc.tensor.matmul(b[:, 0:cols], head_sel[:, h, :], cum[:, 1, 0:cols], start=False, stop=False)
                    nc.tensor.matmul(b[:, t * P:cols], ident[:], neg_mask[:], start=False, stop=True).then_inc(fx_mm, 1)

                pe.wait_ge(gm_used, WT)
                logits(0)
                for n in range(WT * NT):
                    h, t = divmod(n, NT)
                    if n + 1 < WT * NT:
                        logits(n + 1)
                    pe.wait_ge(fx_p, n + 1)
                    if n:
                        pe.wait_ge(fx_pt, n)
                    for j in range(t + 1):
                        mm = nc.tensor.transpose(bank[6][:, j * P:(j + 1) * P], prob[:, n % 2, j * P:(j + 1) * P], ident[:])
                    mm.then_inc(fx_turned, 1)
                    if t == 0 and h:
                        pe.wait_ge(fx_kept, h)
                    pe.wait_ge(fx_pt, n + 1)
                    for j in range(t + 1):
                        mm = nc.tensor.matmul(bank[7][:, t * P:(t + 1) * P], fv[:, j, h * P:(h + 1) * P],
                                              probT[:, n % 2, j * P:(j + 1) * P], start=(j == 0), stop=(j == t))
                    mm.then_inc(fx_o, 1)

            @block.scalar
            def _(act):
                A = nc.scalar.activation
                link = make_link(act, chain_a)
                A(flat(q), flat(q), ACT.Silu).then_inc(q_act, 1)
                A(flat(hg), flat(hg), ACT.Silu).then_inc(hg_act, 1)
                A(flat(gv), flat(gv), ACT.Gelu_apprx_tanh).then_inc(gv_act, 1)
                A(flat(gu), flat(gu), ACT.Gelu_apprx_tanh).then_inc(gu_act, 1)
                act.wait_ge(gvar, 1)
                A(gstd[:], gstd[:], ACT.Sqrt).then_inc(gsqrt, 1)
                A(flat(k), flat(k), ACT.Sigmoid, scale=-1.0).then_inc(sig_done, 1)
                act.wait_ge(params_in["pools"], 16)
                for g in range(WT):
                    act.wait_ge(pool_mm, g + 1)
                    A(pin[:, g, :], bank[6 + g % 2][:], ACT.Copy, scale=pool_scale[:, g:g + 1]).then_inc(pool_kept, 1)
                act.wait_ge(k_ready, 1)
                A(flat(tmp[0]), flat(k), ACT.Ln, bias=1.0, scale=-1.0).then_inc(logf_done, 1)
                act.wait_ge(fz_ready, 1)
                link(A(fz[:, 1, :], fz[:, 1, :], ACT.Exp))
                A(fz[:, 1, :], fz[:, 1, :], ACT.Ln, bias=1.0).then_inc(fz_exp, 1)
                for i in range(NL):
                    act.wait_ge(lvl_d, i + 1)
                    A(flat(tmp[i % 2]), flat(tmp[i % 2]), ACT.Exp).then_inc(lvl_e, 1)
                act.wait_ge(lvl_d, NL + 1)
                link(A(flat(tmp[1]), flat(tmp[0]), ACT.Exp, scale=-1.0))
                A(flat(tmp[0]), flat(tmp[0]), ACT.Exp).then_inc(lvl_e, 1)
                act.wait_ge(kd_d, 1)
                A(flat(tmp[0]), flat(tmp[0]), ACT.Exp).then_inc(kd_e, 1)
                link(A(decay[:], cumb.rearrange("p h (t n) -> p h t n", n=P)[:, :, :, P - 1], ACT.Exp))
                A(flat(cumb), flat(cumb), ACT.Exp).then_inc(kd_e, 1)
                for t in range(NT):
                    act.wait_ge(kd_turned, t + 1)
                    A(tmp[1][:, t, :], bank[t][:], ACT.Copy).then_inc(kd_kept, 1)
                for t in range(NT):
                    act.wait_ge(o_mm, t + 1)
                    A(tmp[0][:, t, :], bank[t % 2][:], ACT.Copy).then_inc(o_kept, 1)
                act.wait_ge(ss_ready, 1)
                A(rms[:], ss[:], ACT.Sqrt).then_inc(ss_sqrt, 1)
                act.wait_ge(params_in["normg"], 16)
                for t in range(NT):
                    act.wait_ge(o_turned, t + 1)
                    A(q[:, :, t * P:(t + 1) * P], bank[t][:].rearrange("p (h n) -> p h n", h=WT), ACT.Copy,
                      scale=norm_g[:, 0:1])
                for n in range(WT * NT):
                    h, t = divmod(n, NT)
                    cols = (t + 1) * P
                    act.wait_ge(fx_max, n + 1)
                    if n >= 2:
                        act.wait_ge(fx_turned, n - 1)
                    A(prob[:, n % 2, 0:cols], bank[4 + n % 2][:, 0:cols], ACT.Exp, bias=fmax[:, n:n + 1],
                      accum_out=fsum[:, n:n + 1]).then_inc(fx_exp, 1)
                    act.wait_ge(fx_turned, n + 1)
                    if n >= 2:
                        act.wait_ge(fx_o, n - 1)
                    A(probT[:, n % 2, 0:cols], bank[6][:, 0:cols], ACT.Copy).then_inc(fx_pt, 1)
                    if t == NT - 1:
                        act.wait_ge(fx_o, n + 1)
                        A(fq[:, h, :], bank[7][:], ACT.Copy).then_inc(fx_kept, 1)

            @block.vector
            def _(dve):
                link = make_link(dve, chain)
                src = pin
                for i, w in enumerate(POOL_WINDOWS):
                    dst, sh = tmp[i % 2][:], w // 2
                    V.tensor_tensor(dst[:, i:, sh:], src[:, i:, sh:], src[:, i:, 0:SEQ - sh], ALU.add)
                    link(V.tensor_copy(dst[:, i:, 0:sh], src[:, i:, 0:sh]))
                    link(V.tensor_tensor(prob[:, 0, 0:16], dst[:, i, 0:16], pool_rc[:, i, :], ALU.mult))
                    V.tensor_tensor(pin[:, i, 0:16], prob[:, 0, 0:16], pin[:, i, 0:16], ALU.subtract)
                    V.scalar_tensor_tensor(out=pin[:, i, 16:], in0=dst[:, i, 16:], scalar=1.0 / w,
                                           in1=pin[:, i, 16:], op0=ALU.mult, op1=ALU.subtract).then_inc(diff_ready, 1)
                    dve.wait_ge(diff_ready, i + 1)
                    src = dst
                dve.wait_ge(params_in["bfox"], 16)
                link(V.tensor_scalar(fz[:, 0, :], ffT[:], b_fox[:, 0:1], None, ALU.add))
                link(V.tensor_scalar(fz[:, 1, :], fz[:, 0, :], -1.0, None, ALU.mult))
                V.tensor_tensor(fz[:, 1, :], fz[:, 0, :], fz[:, 1, :], ALU.min).then_inc(fz_ready, 1)
                V.tensor_scalar(flat(fq), flat(fq), FOX_SCALE, None, ALU.mult).then_inc(fq_ready, 1)
                dve.wait_ge(gv_act, 1)
                for t in range(NT):
                    ins = V.bn_stats(gstats[:, t, :], gv[:, t, :])
                link(ins)
                for t in range(NT):
                    ins = V.bn_aggr(gmv[:, t, :], gstats[:, t, :])
                link(ins)
                V.tensor_scalar(gstd[:], gmv[:, :, 1], LN_EPS, None, ALU.add).then_inc(gvar, 1)
                dve.wait_ge(gsqrt, 1)
                link(V.reciprocal(gstd[:], gstd[:]))
                for t in range(NT):
                    ins = V.tensor_scalar(gv[:, t, :], gv[:, t, :], gmv[:, t, 0:1], gstd[:, t:t + 1], ALU.subtract, ALU.mult)
                link(ins)
                dve.wait_ge(params_in["lng"], 16)
                link(V.tensor_tensor(gv, gv, lng_row[:].unsqueeze(1).to_broadcast([P, NT, W]), ALU.mult))
                dve.wait_ge(params_in["lnb"], 16)
                V.tensor_tensor(gv, gv, lnb_row[:].unsqueeze(1).to_broadcast([P, NT, W]), ALU.add).then_inc(gnorm, 1)
                dve.wait_ge(sig_done, 1)
                for h in range(WT):
                    ins = V.tensor_scalar(k[:, h, :], k[:, h, :], one_minus_lb[:, ds(layer, 1), h], None, ALU.mult)
                ins.then_inc(k_ready, 1)
                dve.wait_ge(logf_done, 1)
                for h in range(WT):
                    ins = V.tensor_tensor_scan(cumb[:, h, :], scan_keep[:], tmp[0][:, h, :], 0.0, ALU.mult, ALU.add)
                link(ins)
                dve.wait_ge(fz_exp, 1)
                dve.wait_ge(fones_done, 1)
                link(V.tensor_scalar(fz[:, 0, :], fz[:, 0, :], 0.0, None, ALU.min))
                link(V.tensor_tensor(fz[:, 0, :], fz[:, 0, :], fz[:, 1, :], ALU.subtract))
                V.tensor_tensor_scan(cum[:, 0, :], fones[:].to_broadcast([WT, SEQ]), fz[:, 0, :], 0.0, ALU.mult, ALU.add).then_inc(c_ready, 1)
                dve.wait_ge(c_ready, 1)
                V.tensor_scalar(cum[:, 1, :], cum[:, 0, :], -1.0, None, ALU.mult).then_inc(c_ready, 1)
                dve.wait_ge(params_in["bs"], 16)
                dve.wait_ge(gu_act, 1)
                for g in range(WT):
                    dve.wait_ge(gm_mm, g + 1)
                    V.tensor_tensor(prob[:, g % 2, :].rearrange("p (t n) -> p t n", t=NT), bank[6 + g % 2][:].rearrange("p (t n) -> p t n", t=NT),
                                    bs_row[:, g:g + 1, :].to_broadcast([P, NT, P]), ALU.add).then_inc(gm_used, 1)
                    dve.wait_ge(gm_used, g + 1)
                    V.tensor_tensor(gu[:, g, :], prob[:, g % 2, :], gu[:, g, :], ALU.mult)
                link(V.memset(att[:], 0.0))

                def blocks(v, r):
                    return v.rearrange("p h (n two r) -> p (h n) two r", two=2, r=r)

                def exponents(i):
                    h = LEVELS[i]
                    n = WT * SEQ // (2 * h)
                    if i >= 2:
                        dve.wait_ge(lvl_mm, NT * (i - 1))
                    x, b = blocks(tmp[i % 2][:], h), blocks(cumb, h)
                    anchor = b[:, :, 0, h - 1:h].to_broadcast([P, n, h])
                    V.tensor_tensor(x[:, :, 0, :], anchor, b[:, :, 0, :], ALU.subtract)
                    V.tensor_tensor(x[:, :, 1, :], b[:, :, 1, :], anchor, ALU.subtract).then_inc(lvl_d, 1)

                def factors(i):
                    h = LEVELS[i]
                    dve.wait_ge(lvl_e, i + 1)
                    if i == 0:
                        dve.wait_ge(q_act, 1)
                    x = blocks(tmp[i % 2][:], h)
                    V.tensor_tensor(x[:, :, 0, :], x[:, :, 0, :], blocks(k, h)[:, :, 0, :], ALU.mult)
                    V.tensor_tensor(x[:, :, 1, :], x[:, :, 1, :], blocks(q, h)[:, :, 1, :], ALU.mult).then_inc(lvl_x, 1)

                def weights(i):
                    for t in range(NT):
                        dve.wait_ge(lvl_mm, NT * i + t + 1)
                        if i:
                            dve.wait_ge(att_done, NT * (i - 1) + t + 1)
                        V.copy_predicated(att[:, t], lvl_mask[:, i:i + 1, :].bitcast(U32).to_broadcast([P, WT, P]),
                                          bank[t][:].rearrange("p (h n) -> p h n", h=WT)).then_inc(att_done, 1)

                exponents(0)
                for i in range(NL):
                    if i + 1 < NL:
                        exponents(i + 1)
                    factors(i)
                    weights(i)
                dve.wait_ge(lvl_mm, NT * NL)
                d4 = "p h (n r) -> p (h n) r"
                n8 = WT * SEQ // DIAG
                b8 = cumb.rearrange(d4, r=DIAG)
                V.tensor_tensor(tmp[0][:].rearrange(d4, r=DIAG), b8,
                                b8[:, :, DIAG // 2 - 1:DIAG // 2].to_broadcast([P, n8, DIAG]), ALU.subtract).then_inc(lvl_d, 1)
                dve.wait_ge(lvl_e, NL + 1)
                V.tensor_tensor(tmp[0][:], tmp[0][:], q, ALU.mult)
                V.tensor_tensor(tmp[1][:], tmp[1][:], k, ALU.mult).then_inc(lvl_x, 1)
                weights(NL)
                bt = cumb.rearrange("p h (t n) -> p (h t) n", n=P)
                V.tensor_tensor(tmp[0][:].rearrange("p h (t n) -> p (h t) n", n=P),
                                bt[:, :, P - 1:P].to_broadcast([P, WT * NT, P]), bt, ALU.subtract).then_inc(kd_d, 1)
                dve.wait_ge(kd_e, 1)
                V.tensor_tensor(tmp[0][:], tmp[0][:], k, ALU.mult).then_inc(kd_x, 1)
                dve.wait_ge(kd_e, 2)
                V.tensor_tensor(q, q, cumb, ALU.mult).then_inc(qin_x, 1)
                for t in range(NT - 1):
                    dve.wait_ge(ds_mm, t + 1)
                    dve.wait_ge(o_mm, t + 1)
                    if t == 0:
                        V.tensor_copy(flat(state), bank[2][:]).then_inc(s_upd, 1)
                        continue
                    dve.wait_ge(s_upd, t)
                    for h in range(WT):
                        ins = V.scalar_tensor_tensor(out=state[:, h, :], in0=state[:, h, :], scalar=decay[:, h, t:t + 1],
                                                     in1=bank[2 + t % 2][:, h * P:(h + 1) * P], op0=ALU.mult, op1=ALU.add)
                    ins.then_inc(s_upd, 1)
                dve.wait_ge(o_kept, NT)
                sq = cumb
                link(V.tensor_tensor(sq, tmp[0][:], tmp[0][:], ALU.mult))
                link(V.tensor_reduce(ss[:], sq.rearrange("p t (h n) -> p t h n", h=WT), AX, ALU.add))
                V.tensor_scalar(ss[:], ss[:], 1.0 / P, RMS_EPS, ALU.mult, ALU.add).then_inc(ss_ready, 1)
                dve.wait_ge(ss_sqrt, 1)
                link(V.reciprocal(rms[:], rms[:]))
                o4 = tmp[0][:].rearrange("p t (h n) -> p (t h) n", h=WT)
                link(V.tensor_tensor(o4, o4, rms[:].rearrange("p t h -> p (t h)").unsqueeze(2).to_broadcast([P, NT * WT, P]), ALU.mult))
                dve.wait_ge(hg_act, 1)
                V.tensor_tensor(tmp[0][:], tmp[0][:], hg, ALU.mult).then_inc(o_normed, 1)
                for n in range(WT * NT + 1):
                    if n < WT * NT:
                        cols = (n % NT + 1) * P
                        dve.wait_ge(fx_mm, n + 1)
                        V.tensor_reduce(fmax[:, n:n + 1], bank[4 + n % 2][:, 0:cols], AX, ALU.max, negate=True).then_inc(fx_max, 1)
                    if n:
                        m = n - 1
                        cols = (m % NT + 1) * P
                        dve.wait_ge(fx_exp, m + 1)
                        link(V.reciprocal(fsum[:, m:m + 1], fsum[:, m:m + 1]))
                        V.tensor_scalar(prob[:, m % 2, 0:cols], prob[:, m % 2, 0:cols], fsum[:, m:m + 1], None,
                                        ALU.mult).then_inc(fx_p, 1)


def _layout(x, shape, order):
    import numpy as np
    return np.ascontiguousarray(np.asarray(x).reshape(shape).transpose(order))


def kernel(**inputs):
    import numpy as np
    import concourse.bacc as bacc
    from concourse.bass_utils import run_bass_kernel_spmd

    L = DEPTH
    i = {n: np.asarray(x) for n, x in inputs.items()}
    w_in = i["w_in"]
    blocks = w_in[:, :, :10 * W].reshape(L, KT, P, 10, W)[:, :, :, list(W_IN_ORDER), :]
    arrays = {
        "x": np.ascontiguousarray(i["x"]),
        "hgrn_lb_logits": _layout(i["hgrn_lb_logits"], (L, WT, P), (2, 0, 1)),
        "w_in": np.ascontiguousarray(blocks.transpose(0, 3, 2, 1, 4)),
        "w_ff": _layout(w_in[:, :, 10 * W:], (L, KT, P, WT), (0, 2, 1, 3)),
        "b_fox_f": _layout(i["b_fox_f"], (L, WT, 1), (0, 1, 2)),
        "pool_w": _layout(i["pool_w"], (L, WT, P, P), (0, 2, 1, 3)),
        "pool_scale": _layout(i["pool_scale"], (L, WT, P), (0, 2, 1)),
        "hgrn_norm_g": _layout(i["hgrn_norm_g"], (L, P, 1), (0, 1, 2)),
        "gmlp_ln_g": np.ascontiguousarray(i["gmlp_ln_g"]),
        "gmlp_ln_b": np.ascontiguousarray(i["gmlp_ln_b"]),
        "gmlp_ws": _layout(i["gmlp_ws"], (L, WT, P, P), (0, 3, 1, 2)),
        "gmlp_bs": _layout(i["gmlp_bs"], (L, WT * P), (0, 1)),
        "b_gate": _layout(i["b_gate"], (L, 4, KT, P), (0, 3, 2, 1)),
        "w_merge": np.ascontiguousarray(np.concatenate(
            [i["w_gate"].reshape(L, KT, P, 4, KT, P).transpose(0, 3, 4, 2, 1, 5),
             i["w_branch"].reshape(L, 4, WT, P, KT, P).transpose(0, 1, 4, 3, 2, 5)], axis=4)),
        "w_out": _layout(i["w_out"], (L, KT, P, D_MODEL), (0, 2, 1, 3)),
        "peer_wq": _layout(i["peer_wq"], (L, KT, P, 4, 512), (0, 3, 2, 1, 4)),
        "peer_keys": _layout(i["peer_keys"], (L, 2, PEER_HEADS, P, P), (0, 4, 2, 1, 3)).reshape(L, P, N_LISTS, P),
        "peer_u": _layout(i["peer_u"], (L, P, NG, EC, KT, P), (0, 2, 5, 3, 4, 1)),
        "peer_v": _layout(i["peer_v"], (L, P, P, D_MODEL), (0, 1, 2, 3)),
    }
    for n in ("ln1_g", "ln1_b", "ln2_g", "ln2_b"):
        arrays[n] = np.ascontiguousarray(i[n])

    nc = bacc.Bacc("TRN2", target_bir_lowering=False, num_devices=1)
    a = {n: nc.dram_tensor(f"{n}_dram", x.shape, mybir.dt.from_np(x.dtype), kind="ExternalInput").ap() for n, x in arrays.items()}
    a["gates"] = nc.dram_tensor("gates_scratch", (P, NTB, P, TB), F32, kind="Internal").ap()
    a["out"] = nc.dram_tensor("out_dram", (1, SEQ, D_MODEL), F32, kind="ExternalOutput").ap()
    build_program(nc, a)
    r = run_bass_kernel_spmd(nc, [{f"{n}_dram": x for n, x in arrays.items()}], core_ids=[0])
    return r.results[0]["out_dram"]
```

```python
import math
from contextlib import ExitStack

import concourse.bass as bass
from concourse import mybir

F32 = mybir.dt.float32
F32R = mybir.dt.float32r
U32 = mybir.dt.uint32
ALU = mybir.AluOpType
ACT = mybir.ActivationFunctionType
AX = mybir.AxisListType.X
ds = bass.ds

P = 128
D_MODEL = 1024
SEQ = 512
DEPTH = 2
KT = D_MODEL // P
NT = SEQ // P
W = D_MODEL // 2
WT = W // P
POOL_WINDOWS = (2, 4, 8, 16)
PEER_HEADS = 8
TOPK = 16
PAIRS = PEER_HEADS * TOPK
N_LISTS = 2 * PEER_HEADS
ALPHA = (2.0 * DEPTH) ** 0.25
LN_EPS = 1e-5
RMS_EPS = 1e-6
NEG_BIG = -1e30
LOWEST = -3.0e38
FOX_SCALE = float(P) ** -0.5
LEVELS = (64, 32, 16, 8)
DIAG = 8
EC = 4
NG = P // EC
TB = 64
NTB = SEQ // TB
AHEAD_ROUTE = 10
AHEAD_SPREAD = NTB // 2
NG_AHEAD = AHEAD_ROUTE + AHEAD_SPREAD
NG_FULL = NG - NG_AHEAD
GATES_AHEAD = 6

T_POOL, T_HQ, T_GU, T_FQ, T_HF, T_FK = range(6)
N_HI, N_HG, N_GV, N_FV = range(4)
W_IN_ORDER = (0, 1, 5, 7, 2, 8, 3, 4, 6, 9)


def make_link(eng, sem, start=0):
    done = [0]

    def link(ins):
        done[0] += 1
        ins.then_inc(sem, 1)
        eng.wait_ge(sem, start + done[0])

    link.done = done
    return link


def as_f32(v):
    return v.bitcast(F32)


def matmul_split(nc, out, lhsT, rhs, first, last):
    (lh, ll), (rh, rl) = lhsT, rhs
    nc.tensor.matmul(out, lh, rl, start=first, stop=False)
    nc.tensor.matmul(out, lh, rh, start=False, stop=False)
    return nc.tensor.matmul(out, ll, rh, start=False, stop=last)


def build_program(nc, a):
    with ExitStack() as whole:
        sems = {}

        def sem(name):
            if name not in sems:
                sems[name] = whole.enter_context(nc.semaphore(name))
            return sems[name]

        def sb(ctx, name, shape, dt=F32):
            return ctx.enter_context(nc.sbuf_tensor(name, shape, dt))

        bank = [whole.enter_context(nc.psum_tensor(f"bank{i}", [P, 512], F32)) for i in range(8)]

        xh = sb(whole, "xT_high", [P, KT, SEQ], F32R)
        xl = sb(whole, "xT_low", [P, KT, SEQ], F32R)
        ident = sb(whole, "ident", [P, P])
        iota_row = sb(whole, "iota_row", [P, P])
        lvl_mask = sb(whole, "lvl_mask", [P, len(LEVELS) + 1, P])
        neg_mask = sb(whole, "neg_mask", [P, P])
        head_sel = sb(whole, "head_sel", [WT, WT, P])
        pool_rc = sb(whole, "pool_rc", [P, WT, 16])
        scan_keep = sb(whole, "scan_keep", [P, SEQ])
        one_minus_lb = sb(whole, "one_minus_lb", [P, DEPTH, WT])

        s_const = sem("const_done")
        s_chain_v = sem("dve_chain")
        s_chain_a = sem("act_chain")
        s_chain_p = sem("pool_chain")

        def clear(prefix=""):
            with nc.Block() as block:

                @block.gpsimd
                def _(pool):
                    for name, s in sems.items():
                        if name.startswith(prefix):
                            pool.sem_clear(s)

        def norm_stage(tag, x_tok, load_g, load_b, out_proj=None):
            x_dram = a["out"].rearrange("o (t p) d -> p (o t) d", p=P)
            with ExitStack() as ctx:
                g_row = sb(ctx, f"{tag}_g", [P, D_MODEL])
                b_row = sb(ctx, f"{tag}_b", [P, D_MODEL])
                r = sb(ctx, f"{tag}_r", [P, 2, D_MODEL])
                stats = sb(ctx, f"{tag}_stats", [P, 2, 2, 6])
                mv = sb(ctx, f"{tag}_mv", [P, NT, 2])
                std = sb(ctx, f"{tag}_std", [P, NT])
                rstd = sb(ctx, f"{tag}_rstd", [P, NT])
                rows_in = sem("ln_rows_in")
                x_in, x_out = sem("ln_x_in"), sem("ln_x_out")
                sum_ready = sem("ln_sum_ready")
                sum_used = sem("ln_sum_used")
                var_ready = sem("ln_var_ready")
                std_ready = sem("ln_std_ready")
                x_ready = sem("ln_x_ready")
                turned = sem("ln_turned")
                high_done = sem("ln_high_done")
                low_done = sem("ln_low_done")
                chain = sem("ln_chain")
                w_in = [sem(f"ln_w_in{j}") for j in range(4)]
                w_high = sem("ln_w_high")
                w_low = sem("ln_w_low")
                if out_proj:
                    w_dram, merged = out_proj
                    w_raw = sb(ctx, "wo_raw", [P, 4, D_MODEL])
                    wh = sb(ctx, "wo_high", [P, KT, D_MODEL], F32R)
                    wl = sb(ctx, "wo_low", [P, KT, D_MODEL], F32R)
                    mh = sb(ctx, "merged_high", [P, KT, SEQ], F32R)
                    ml = sb(ctx, "merged_low", [P, KT, SEQ], F32R)
                with nc.Block() as block:

                    @block.sync
                    def _(sp):
                        if out_proj:
                            for j in range(4):
                                if j >= 2:
                                    sp.wait_ge(w_low, 2 * j - 2)
                                sp.dma_start(w_raw[:, j % 2 * 2:j % 2 * 2 + 2, :], w_dram[:, 2 * j:2 * j + 2, :]).then_inc(w_in[j], 16)
                            sp.dma_start(x_tok[:], x_dram).then_inc(x_in, 16)
                        sp.dma_start(g_row[:], load_g).then_inc(rows_in, 16)
                        sp.dma_start(b_row[:], load_b).then_inc(rows_in, 16)
                        if not out_proj:
                            for t in range(NT):
                                sp.wait_ge(x_ready, t + 1)
                                sp.dma_start(x_dram[:, t], x_tok[:, t]).then_inc(x_out, 16)
                            sp.wait_ge(x_out, 16 * NT)

                    @block.tensor
                    def _(pe):
                        def project(first, tiles):
                            for k in range(KT):
                                if first == 0:
                                    pe.wait_ge(w_low, k + 1)
                                for j in range(2 * tiles):
                                    t, half = first + j // 2, j % 2
                                    tok, cols = slice(t * P, (t + 1) * P), slice(half * 512, (half + 1) * 512)
                                    mm = matmul_split(nc, bank[2 * t + half][:], (mh[:, k, tok], ml[:, k, tok]),
                                                      (wh[:, k, cols], wl[:, k, cols]), k == 0, k == KT - 1)
                            mm.then_inc(sum_ready, tiles)

                        def turn(t):
                            pe.wait_ge(x_ready, t + 1)
                            for half in range(2):
                                if t >= 2:
                                    pe.wait_ge(low_done, 2 * (t - 2) + half + 1)
                                for q in range(4):
                                    k = 4 * half + q
                                    tr = nc.tensor.transpose(bank[2 * (t % 2) + half][:, q * P:(q + 1) * P],
                                                             x_tok[:, t, k * P:(k + 1) * P], ident[:])
                                tr.then_inc(turned, 1)

                        if out_proj:
                            project(0, 2)
                            for t in range(2, NT):
                                project(t, 1)
                            pe.wait_ge(sum_used, 4)
                        for t in range(NT):
                            turn(t)

                    @block.vector
                    def _(dve):
                        link = make_link(dve, chain)

                        def low(t):
                            for half in range(2):
                                dve.wait_ge(high_done, 2 * t + half + 1)
                                s = (slice(None), slice(4 * half, 4 * half + 4), slice(t * P, (t + 1) * P))
                                nc.vector.tensor_tensor(xl[s], bank[2 * (t % 2) + half][:].rearrange("p (q n) -> p q n", q=4),
                                                        as_f32(xh[s]), ALU.subtract).then_inc(low_done, 1)

                        if out_proj:
                            for k in range(KT):
                                dve.wait_ge(w_high, k + 1)
                                nc.vector.tensor_tensor(ml[:, k, :], merged[:, k, :], as_f32(mh[:, k, :]), ALU.subtract)
                                nc.vector.tensor_tensor(wl[:, k, :], w_raw[:, k % 4, :], as_f32(wh[:, k, :]),
                                                        ALU.subtract).then_inc(w_low, 1)
                        for t in range(NT):
                            rt = r[:, t % 2, :]
                            for half in range(2):
                                cols = slice(half * 512, (half + 1) * 512)
                                if out_proj and t + half == 0:
                                    dve.wait_ge(x_in, 16)
                                if out_proj:
                                    dve.wait_ge(sum_ready, t + 1)
                                    nc.vector.scalar_tensor_tensor(out=x_tok[:, t, cols], in0=x_tok[:, t, cols], scalar=ALPHA,
                                                                   in1=bank[2 * t + half][:], op0=ALU.mult,
                                                                   op1=ALU.add).then_inc(sum_used, 1)
                                    dve.wait_ge(sum_used, 2 * t + half + 1)
                                link(nc.vector.bn_stats(stats[:, t % 2, half, :], x_tok[:, t, cols]))
                            link(nc.vector.bn_aggr(mv[:, t, :], stats[:, t % 2, :, :]))
                            nc.vector.tensor_scalar(std[:, t:t + 1], mv[:, t, 1:2], LN_EPS, None, ALU.add).then_inc(var_ready, 1)
                            if t:
                                low(t - 1)
                            dve.wait_ge(std_ready, t + 1)
                            link(nc.vector.reciprocal(rstd[:, t:t + 1], std[:, t:t + 1]))
                            link(nc.vector.tensor_scalar(rt, x_tok[:, t, :], mv[:, t, 0:1], rstd[:, t:t + 1], ALU.subtract, ALU.mult))
                            if t == 0:
                                dve.wait_ge(rows_in, 32)
                            link(nc.vector.tensor_tensor(rt, rt, g_row[:], ALU.mult))
                            nc.vector.tensor_tensor(x_tok[:, t, :], rt, b_row[:], ALU.add).then_inc(x_ready, 1)
                        low(NT - 1)

                    @block.scalar
                    def _(act):
                        def high(t):
                            for half in range(2):
                                act.wait_ge(turned, 2 * t + half + 1)
                                nc.scalar.activation(xh[:, 4 * half:4 * half + 4, t * P:(t + 1) * P],
                                                     bank[2 * (t % 2) + half][:].rearrange("p (q n) -> p q n", q=4),
                                                     ACT.Copy).then_inc(high_done, 1)
                        if out_proj:
                            for k in range(KT):
                                nc.scalar.activation(mh[:, k, :], merged[:, k, :], ACT.Copy)
                                act.wait_ge(w_in[k // 2], 16)
                                nc.scalar.activation(wh[:, k, :], w_raw[:, k % 4, :], ACT.Copy).then_inc(w_high, 1)
                        for t in range(NT):
                            act.wait_ge(var_ready, t + 1)
                            nc.scalar.activation(std[:, t:t + 1], std[:, t:t + 1], ACT.Sqrt).then_inc(std_ready, 1)
                            if t >= 1:
                                high(t - 1)
                        high(NT - 1)

        def project_stage(tag, w_dram, pairs_T, dst_T, pairs_N=0, dst_N=None, small=None, load_next=None):
            with ExitStack() as ctx:
                raw = sb(ctx, f"{tag}_raw", [P, 2, KT // 2, 512])
                wh = sb(ctx, f"{tag}_wh", [P, 2, KT, 512], F32R)
                wl = sb(ctx, f"{tag}_wl", [P, 2, KT, 512], F32R)
                loaded = [sem(f"pj_w_loaded{r}") for r in range(2)]
                w_high = sem("pj_w_high")
                w_low = sem("pj_w_low")
                mm_done = sem("pj_mm_done")
                kept_a = sem("pj_kept_a")
                kept_v = sem("pj_kept_v")
                small_in = sem("pj_small_in")
                small_h = sem("pj_small_h")
                small_l = sem("pj_small_l")
                n_pairs = pairs_T + pairs_N
                if small:
                    sh = sb(ctx, f"{tag}_sh", [P, KT, WT], F32R)
                    sl = sb(ctx, f"{tag}_sl", [P, KT, WT], F32R)
                with nc.Block() as block:

                    @block.sync
                    def _(sp):
                        with sp.Fori(0, n_pairs) as i:
                            for b in range(2):
                                for r in range(2):
                                    sp.wait_ge(w_low, 4 * i + 2 * b + r + 1)
                                    sp.dma_start(raw[:, r], w_dram(2 * i + b)[:, 4 * r:4 * r + 4, :]).then_inc(loaded[r], 16)
                        if small:
                            sp.dma_start(small[0][:], small[1]).then_inc(small_in, 16)
                        if load_next:
                            load_next(sp)

                    @block.tensor
                    def _(pe):
                        pe.sem_inc(mm_done, 8)

                        def pair(i, token_major):
                            for b in range(2):
                                for q in range(4):
                                    n = 4 * b + q
                                    cols = slice(q * P, (q + 1) * P)
                                    pe.wait_ge((kept_a, kept_v)[n % 2], 4 * i + n // 2 + 1)
                                    for k in range(KT):
                                        if q == 0 and k % 4 == 0:
                                            pe.wait_ge(w_low, 4 * i + 2 * b + k // 4 + 3)
                                        x2 = (xh[:, k, cols], xl[:, k, cols]) if token_major else (xh[:, k, :], xl[:, k, :])
                                        w2 = ((wh[:, b, k, :], wl[:, b, k, :]) if token_major else
                                              (wh[:, b, k, cols], wl[:, b, k, cols]))
                                        lhsT, rhs = (x2, w2) if token_major else (w2, x2)
                                        mm = matmul_split(nc, bank[n][:], lhsT, rhs, k == 0, k == KT - 1)
                                    mm.then_inc(mm_done, 1)

                        with pe.Fori(0, pairs_T) as i:
                            pair(i, False)
                        if pairs_N:
                            with pe.Fori(pairs_T, n_pairs) as i:
                                pair(i, True)
                        if small:
                            pe.wait_ge(small_l, 1)
                            pe.wait_ge(kept_a, 4 * n_pairs + 1)
                            for k in range(KT):
                                mm = matmul_split(nc, bank[0][0:WT, :], (sh[:, k, :], sl[:, k, :]), (xh[:, k, :], xl[:, k, :]),
                                                  k == 0, k == KT - 1)
                            mm.then_inc(mm_done, 1)

                    def split_and_keep(eng, split, copy, kept, parity):
                        eng.sem_inc(kept, 4)

                        def out(i, b, dst, first):
                            for n in range(4 * b + parity, 4 * b + 4, 2):
                                eng.wait_ge(mm_done, 8 * i + n + 9)
                                copy(dst[:, 2 * (i - first) + n // 4, n % 4, :], bank[n][:]).then_inc(kept, 1)

                        split(0, 0)
                        if pairs_N:
                            with eng.Fori(0, pairs_T) as i:
                                split(i, 1)
                                out(i, 0, dst_T, 0)
                                split(i + 1, 0)
                                out(i, 1, dst_T, 0)
                            if pairs_N > 1:
                                with eng.Fori(pairs_T, n_pairs - 1) as i:
                                    split(i, 1)
                                    out(i, 0, dst_N, pairs_T)
                                    split(i + 1, 0)
                                    out(i, 1, dst_N, pairs_T)
                            dst, first = dst_N, pairs_T
                        else:
                            with eng.Fori(0, pairs_T - 1) as i:
                                split(i, 1)
                                out(i, 0, dst_T, 0)
                                split(i + 1, 0)
                                out(i, 1, dst_T, 0)
                            dst, first = dst_T, 0
                        i = n_pairs - 1
                        split(i, 1)
                        out(i, 0, dst, first)
                        out(i, 1, dst, first)

                    @block.scalar
                    def _(act):
                        def high(i, b):
                            act.wait_ge(mm_done, 8 * i + 4 * b + 4)
                            for r in range(2):
                                act.wait_ge(loaded[r], 32 * i + 16 * b + 16)
                                nc.scalar.activation(wh[:, b, 4 * r:4 * r + 4, :], raw[:, r], ACT.Copy).then_inc(w_high, 1)

                        split_and_keep(act, high, lambda o, i: nc.scalar.activation(o, i, ACT.Copy), kept_a, 0)
                        if small:
                            act.wait_ge(small_in, 16)
                            nc.scalar.activation(sh[:], small[0][:], ACT.Copy).then_inc(small_h, 1)

                    @block.vector
                    def _(dve):
                        dve.sem_inc(w_low, 2)

                        def low(i, b):
                            for r in range(2):
                                dve.wait_ge(w_high, 4 * i + 2 * b + r + 1)
                                nc.vector.tensor_tensor(wl[:, b, 4 * r:4 * r + 4, :], raw[:, r], as_f32(wh[:, b, 4 * r:4 * r + 4, :]),
                                                        ALU.subtract).then_inc(w_low, 1)

                        split_and_keep(dve, low, lambda o, i: nc.vector.tensor_copy(o, i), kept_v, 1)
                        if small:
                            dve.wait_ge(small_h, 1)
                            nc.vector.tensor_tensor(sl[:], small[0][:], as_f32(sh[:]), ALU.subtract).then_inc(small_l, 1)
                            dve.wait_ge(mm_done, 8 * n_pairs + 9)
                            nc.vector.tensor_copy(small[2][:], bank[0][0:WT, :]).then_inc(kept_v, 1)

        with ExitStack() as ctx:
            x_tok = sb(ctx, "x_first", [P, NT, D_MODEL])
            x_out0 = sem("ln_x_out")
            lbl = sb(ctx, "lb_logits", [P, DEPTH, WT])
            lb_work = sb(ctx, "lb_work", [P, 4, WT])
            lb_exp = sb(ctx, "lb_exp", [P, DEPTH, WT])
            x_in = sem("ln_x_in")
            lb_in = sem("lb_in")
            turned0 = sem("ln_turned")
            copied0 = sem("ln_high_done")
            lb_shift = sem("lb_shift")
            lb_expd = sem("lb_expd")
            rc_seed = sem("rc_seed")
            with nc.Block() as block:

                @block.sync
                def _(sp):
                    sp.dma_start(x_tok[:], a["x"].rearrange("o (t p) d -> p (o t) d", p=P)).then_inc(x_in, 16)
                    sp.dma_start(lbl[:], a["hgrn_lb_logits"]).then_inc(lb_in, 16)
                    sp.wait_ge(x_in, 16)
                    sp.dma_start(a["out"].rearrange("o (t p) d -> p (o t) d", p=P), x_tok[:]).then_inc(x_out0, 16)
                    sp.wait_ge(x_out0, 16)

                @block.gpsimd
                def _(pool):
                    link = make_link(pool, s_chain_p)
                    link(nc.gpsimd.memset(ident[:], 0.0))
                    nc.gpsimd.affine_select(out=ident[:], in_=ident[:], compare_op=ALU.not_equal, fill=1.0, base=0,
                                            pattern=[[-1, P]], channel_multiplier=1).then_inc(s_const, 1)
                    nc.gpsimd.iota(iota_row[:], pattern=[[1, P]], base=0, channel_multiplier=0,
                                   allow_small_or_imprecise_dtypes=True)
                    for g in range(WT):
                        ins = nc.gpsimd.iota(pool_rc[:, g, :], pattern=[[1, 16]], base=1, channel_multiplier=0,
                                             allow_small_or_imprecise_dtypes=True)
                    ins.then_inc(rc_seed, 1)
                    nc.gpsimd.memset(lvl_mask[:], 0.0)
                    nc.gpsimd.memset(scan_keep[:], 1.0)
                    link(nc.gpsimd.memset(head_sel[:], 1.0))
                    nc.gpsimd.memset(scan_keep[:].rearrange("p (t n) -> p t n", t=NT)[:, :, 0:1], 0.0)
                    for h in range(WT):
                        nc.gpsimd.affine_select(out=head_sel[:, h, :], in_=head_sel[:, h, :], compare_op=ALU.is_equal,
                                                fill=0.0, base=-h, pattern=[[0, P]], channel_multiplier=1)
                    link(nc.gpsimd.memset(neg_mask[:], 0.0))
                    nc.gpsimd.affine_select(out=neg_mask[:], in_=neg_mask[:], compare_op=ALU.is_ge, fill=NEG_BIG, base=0,
                                            pattern=[[-1, P]], channel_multiplier=1)
                    for i, h in enumerate(LEVELS):
                        v = lvl_mask[:, i, :].rearrange("p (n r) -> p n r", r=2 * h)
                        link(nc.gpsimd.memset(v[:, :, h:2 * h], 1.0))
                        link(nc.gpsimd.affine_select(out=v, in_=v, compare_op=ALU.is_ge, fill=0.0, base=0,
                                                     pattern=[[-2 * h, P // (2 * h)], [0, 2 * h]], channel_multiplier=1))
                        link(nc.gpsimd.affine_select(out=v, in_=v, compare_op=ALU.is_ge, fill=0.0, base=h - 1,
                                                     pattern=[[2 * h, P // (2 * h)], [0, 2 * h]], channel_multiplier=-1))
                    v = lvl_mask[:, len(LEVELS), :].rearrange("p (n r) -> p n r", r=DIAG)
                    link(nc.gpsimd.memset(v, 1.0))
                    link(nc.gpsimd.affine_select(out=v, in_=v, compare_op=ALU.is_ge, fill=0.0, base=0,
                                                 pattern=[[-DIAG, P // DIAG], [0, DIAG]], channel_multiplier=1))
                    nc.gpsimd.affine_select(out=v, in_=v, compare_op=ALU.is_ge, fill=0.0, base=0,
                                            pattern=[[DIAG, P // DIAG], [1, DIAG]], channel_multiplier=-1)

                @block.tensor
                def _(pe):
                    pe.wait_ge(s_const, 1)
                    pe.wait_ge(x_in, 16)
                    for t in range(NT):
                        for half in range(2):
                            for q in range(4):
                                k = 4 * half + q
                                tr = nc.tensor.transpose(bank[2 * t + half][:, q * P:(q + 1) * P],
                                                         x_tok[:, t, k * P:(k + 1) * P], ident[:])
                            tr.then_inc(turned0, 1)

                @block.vector
                def _(dve):
                    link = make_link(dve, s_chain_v)
                    dve.wait_ge(rc_seed, 1)
                    for g, w in enumerate(POOL_WINDOWS):
                        ins = nc.vector.tensor_scalar(pool_rc[:, g, :], pool_rc[:, g, :], float(w), None, ALU.min)
                    link(ins)
                    nc.vector.reciprocal(pool_rc[:], pool_rc[:])
                    dve.wait_ge(lb_in, 16)
                    link(nc.vector.tensor_copy(lb_work[:, 0, :], lbl[:, 0, :]))
                    for l in range(1, DEPTH):
                        link(nc.vector.tensor_tensor(lb_work[:, 0, :], lb_work[:, 0, :], lbl[:, l, :], ALU.max))
                    for l in range(DEPTH):
                        ins = nc.vector.tensor_tensor(lbl[:, l, :], lbl[:, l, :], lb_work[:, 0, :], ALU.subtract)
                    ins.then_inc(lb_shift, 1)
                    dve.wait_ge(lb_expd, 1)
                    link(nc.vector.tensor_copy(lb_work[:, 1, :], lb_exp[:, 0, :]))
                    for l in range(1, DEPTH):
                        link(nc.vector.tensor_tensor(lb_work[:, 1, :], lb_work[:, 1, :], lb_exp[:, l, :], ALU.add))
                    link(nc.vector.reciprocal(lb_work[:, 2, :], lb_work[:, 1, :]))
                    for l in range(DEPTH):
                        ins = nc.vector.tensor_tensor(lb_exp[:, l, :], lb_exp[:, l, :], lb_work[:, 2, :], ALU.mult)
                    link(ins)
                    link(nc.vector.tensor_copy(lb_work[:, 3, :], lb_exp[:, 0, :]))
                    for l in range(DEPTH):
                        if l:
                            link(nc.vector.tensor_tensor(lb_work[:, 3, :], lb_work[:, 3, :], lb_exp[:, l, :], ALU.add))
                        link(nc.vector.tensor_tensor(one_minus_lb[:, l, :], lb_work[:, 3, :], lb_exp[:, 0, :], ALU.subtract))
                        nc.vector.tensor_scalar(one_minus_lb[:, l, :], one_minus_lb[:, l, :], -1.0, 1.0, ALU.mult, ALU.add)
                    for n in range(2 * NT):
                        s = (slice(None), slice(4 * (n % 2), 4 * (n % 2) + 4), slice(n // 2 * P, (n // 2 + 1) * P))
                        dve.wait_ge(copied0, n + 1)
                        nc.vector.tensor_tensor(xl[s], bank[n][:].rearrange("p (q n) -> p q n", q=4), as_f32(xh[s]), ALU.subtract)

                @block.scalar
                def _(act):
                    act.wait_ge(lb_shift, 1)
                    nc.scalar.activation(lb_exp[:], lbl[:], ACT.Exp).then_inc(lb_expd, 1)
                    for n in range(2 * NT):
                        t, half = n // 2, n % 2
                        act.wait_ge(turned0, n + 1)
                        nc.scalar.activation(xh[:, 4 * half:4 * half + 4, t * P:(t + 1) * P],
                                             bank[n][:].rearrange("p (q n) -> p q n", q=4), ACT.Copy).then_inc(copied0, 1)

        clear("ln_")

        with nc.Fori(0, DEPTH) as layer:
            with ExitStack() as upper:
                with ExitStack() as mix:
                    projT = sb(mix, "projT", [P, 6, 4, SEQ])
                    with ExitStack() as ctx:
                        projN = sb(ctx, "projN", [P, 4, NT, W])
                        ffT = sb(ctx, "ffT", [WT, SEQ])
                        with ExitStack() as c2:
                            w_ff = sb(c2, "w_ff", [P, KT, WT])
                            project_stage("in", lambda n: a["w_in"][layer, n], 3, projT, 2, projN, (w_ff, a["w_ff"][layer], ffT))
                        mixer_stage(nc, a, layer, sb, sem, bank, (xh, xl), projT, projN, ffT, ident, lvl_mask, neg_mask, head_sel,
                                    pool_rc, scan_keep, one_minus_lb)
                    x_tok = upper.enter_context(nc.sbuf_tensor("x_tok", [P, NT, D_MODEL], F32, side="right"))
                    merging = ExitStack()
                    merged = merging.enter_context(nc.sbuf_tensor("merged", [P, KT, SEQ], F32, side="right"))
                    clear("mg_")
                    merge_stage(nc, a, layer, sb, sem, bank, projT, xh, xl, merged)
                norm_stage("ln1", x_tok, a["ln1_g"][layer].partition_broadcast(P), a["ln1_b"][layer].partition_broadcast(P),
                           out_proj=(a["w_out"][layer], merged))
                merging.close()
                ur = sb(upper, "u_raw", [P, EC, KT, P])

                def first_u(stage, group):
                    def load(sp):
                        for r in range(2):
                            half = slice(EC // 2 * r, EC // 2 * (r + 1))
                            sp.dma_start(ur[:, half], a["peer_u"][layer, group, :, half]).then_inc(sem(f"{stage}_u_in{r}"), 16)
                    return load

                with ExitStack() as ffn:
                    rowT = sb(ffn, "rowT", [P, SEQ])
                    colT = sb(ffn, "colT", [P, SEQ])
                    gateT = sb(ffn, "gateT", [P, SEQ])
                    with ExitStack() as ctx:
                        qT = sb(ctx, "qT", [P, 4, 4, SEQ])
                        clear("pj_")
                        project_stage("pq", lambda n: a["peer_wq"][layer, n], 2, qT, load_next=first_u("rt", NG_FULL))
                        route_stage(nc, a, layer, sb, sem, bank, qT, (xh, xl), ur, first_u("sp", NG_FULL + AHEAD_ROUTE),
                                    ident, iota_row, rowT, colT, gateT)
                        clear("hid_")
                    storing = spread_stage(nc, a, layer, sb, sem, bank, (xh, xl), ur, first_u("ex", 0), iota_row, rowT, colT, gateT)
                    clear("hid_")
                experts_stage(nc, a, layer, sb, sem, bank, xh, xl, ur, x_tok, storing)
                clear("ln_")
                norm_stage("ln2", x_tok, a["ln2_g"][layer].partition_broadcast(P), a["ln2_b"][layer].partition_broadcast(P))
            clear()


def merge_stage(nc, a, layer, sb, sem, bank, projT, xh, xl, merged):
    KW = KT + WT
    with ExitStack() as ctx:
        brh = sb(ctx, "brh", [P, 2, WT, SEQ], F32R)
        brl = sb(ctx, "brl", [P, 2, WT, SEQ], F32R)
        raw = sb(ctx, "mg_raw", [P, 2, KW, P])
        wh = sb(ctx, "mg_wh", [P, 2, KW, P], F32R)
        wl = sb(ctx, "mg_wl", [P, 2, KW, P], F32R)
        b_gate = sb(ctx, "b_gate", [P, KT, 4])
        gate = sb(ctx, "gate", [P, 2, SEQ])
        prod = sb(ctx, "prod", [P, 2, SEQ])
        loaded = [sem(f"mg_loaded{b}") for b in range(2)]
        logits_in = [sem(f"mg_logits_in{b}") for b in range(2)]
        bias_in = sem("mg_bias_in")
        br_high, br_low = sem("mg_br_high"), sem("mg_br_low")
        w_high = sem("mg_w_high")
        w_low = sem("mg_w_low")
        gate_mm = sem("mg_gate_mm")
        br_mm = sem("mg_br_mm")
        gated = sem("mg_gated")
        prods = sem("mg_prods")
        added = sem("mg_added")

        def units(eng, m, body):
            if m == 0:
                for n in range(KT):
                    body(n, n, n % 2)
                return
            with eng.Fori(0, KT // 2) as i:
                for b in range(2):
                    body(KT * m + 2 * i + b, 2 * i + b, b)

        def needed(n):
            return slice(KT if isinstance(n, int) and n < GATES_AHEAD else 0, KW)

        def round_of(n, b):
            return 16 * (n // 2) + 16 if isinstance(n, int) else 8 * (n - b) + 16

        with nc.Block() as block:

            @block.sync
            def _(sp):
                sp.dma_start(b_gate[:], a["b_gate"][layer]).then_inc(bias_in, 16)
                for m in range(4):
                    def load(n, dt, b):
                        sp.wait_ge(w_low, n + 1)
                        sp.dma_start(raw[:, b, needed(n)], a["w_merge"][layer, m, dt, :, needed(n)]).then_inc(loaded[b], 16)
                        if m == 0 and n < GATES_AHEAD:
                            sp.wait_ge(prods, n + 1)
                            sp.dma_start(gate[:, b, :], a["gate_logits"][n]).then_inc(logits_in[b], 16)
                    units(sp, m, load)

            @block.tensor
            def _(pe):
                pe.sem_inc(br_mm, 2)
                for m in range(4):
                    pe.wait_ge(br_low, m + 1)

                    def multiply(n, dt, b):
                        pe.wait_ge(w_low, n + 3)
                        if m or n >= GATES_AHEAD:
                            pe.wait_ge(gated, n + 1)
                            for k in range(KT):
                                mm = matmul_split(nc, bank[b][:], (wh[:, b, k, :], wl[:, b, k, :]), (xh[:, k, :], xl[:, k, :]),
                                                  k == 0, k == KT - 1)
                            mm.then_inc(gate_mm, 1)
                        pe.wait_ge(prods, n + 1)
                        for k in range(WT):
                            mm = matmul_split(nc, bank[2 + b][:], (wh[:, b, KT + k, :], wl[:, b, KT + k, :]),
                                              (brh[:, m % 2, k, :], brl[:, m % 2, k, :]), k == 0, k == WT - 1)
                        mm.then_inc(br_mm, 1)
                    units(pe, m, multiply)

            @block.scalar
            def _(act):
                act.sem_inc(gated, 2)

                def split_branch(m):
                    if m >= 2:
                        act.wait_ge(br_mm, KT * (m - 1) + 2)
                    nc.scalar.activation(brh[:, m % 2], projT[:, m], ACT.Copy).then_inc(br_high, 1)

                def high(n, b):
                    act.wait_ge(br_mm, n + 1)
                    act.wait_ge(loaded[b], round_of(n, b))
                    nc.scalar.activation(wh[:, b, needed(n)], raw[:, b, needed(n)], ACT.Copy).then_inc(w_high, 1)

                split_branch(0)
                act.wait_ge(bias_in, 16)
                high(0, 0)
                high(1, 1)
                for m in range(4):
                    if m < 3:
                        split_branch(m + 1)

                    def sigmoids(n, dt, b, last=False):
                        here = m == 0 and n < GATES_AHEAD
                        if here:
                            act.wait_ge(logits_in[b], round_of(n, b))
                        else:
                            act.wait_ge(gate_mm, n + 1 - GATES_AHEAD)
                            act.wait_ge(prods, n + 1)
                        nc.scalar.activation(gate[:, b, :], gate[:, b, :] if here else bank[b][:], ACT.Sigmoid, bias=b_gate[:, dt, m:m + 1] if m == 0 else b_gate[:, ds(dt, 1), m]).then_inc(gated, 1)
                        if not last:
                            high(n + 2, b)

                    if m < 3:
                        units(act, m, sigmoids)
                    else:
                        with act.Fori(0, KT // 2 - 1) as i:
                            for b in range(2):
                                sigmoids(KT * m + 2 * i + b, 2 * i + b, b)
                        for b in range(2):
                            sigmoids(KT * m + KT - 2 + b, KT - 2 + b, b, last=True)

            @block.vector
            def _(dve):
                V = nc.vector
                dve.sem_inc(w_low, 2)
                dve.sem_inc(prods, 2)
                dve.sem_inc(added, 2)

                def split_branch(m):
                    dve.wait_ge(br_high, m + 1)
                    V.tensor_tensor(brl[:, m % 2], projT[:, m], as_f32(brh[:, m % 2]), ALU.subtract).then_inc(br_low, 1)

                def low(n, b):
                    dve.wait_ge(w_high, n + 1)
                    V.tensor_tensor(wl[:, b, needed(n)], raw[:, b, needed(n)], as_f32(wh[:, b, needed(n)]),
                                    ALU.subtract).then_inc(w_low, 1)

                split_branch(0)
                low(0, 0)
                low(1, 1)
                for m in range(4):
                    if m < 3:
                        split_branch(m + 1)

                    def products(n, dt, b, last=False):
                        dve.wait_ge(gated, n + 3)
                        dve.wait_ge(br_mm, n + 3)
                        dve.wait_ge(added, n + 1)
                        if m == 0:
                            V.tensor_tensor(merged[:, dt, :], gate[:, b, :], bank[2 + b][:], ALU.mult).then_inc(prods, 1)
                            V.engine_nop().then_inc(added, 1)
                        else:
                            V.tensor_tensor(prod[:, b, :], gate[:, b, :], bank[2 + b][:], ALU.mult).then_inc(prods, 1)
                            dve.wait_ge(prods, n + 3)
                            V.tensor_tensor(merged[:, ds(dt, 1), :], merged[:, ds(dt, 1), :], prod[:, b:b + 1, :], ALU.add).then_inc(added, 1)
                        if not last:
                            low(n + 2, b)

                    if m < 3:
                        units(dve, m, products)
                    else:
                        with dve.Fori(0, KT // 2 - 1) as i:
                            for b in range(2):
                                products(KT * m + 2 * i + b, 2 * i + b, b)
                        for b in range(2):
                            products(KT * m + KT - 2 + b, KT - 2 + b, b, last=True)


class HiddenAhead:

    def __init__(self, nc, a, layer, ctx, sb, sem, bank, x, ur, load_next, stage, first):
        self.nc, self.a, self.layer, self.bank, self.x, self.first = nc, a, layer, bank, x, first
        self.ur, self.load_next = ur, load_next
        self.uh = sb(ctx, f"ahead{first}_u_high", [P, EC, KT, P], F32R)
        self.ul = sb(ctx, f"ahead{first}_u_low", [P, EC, KT, P], F32R)
        self.hid = sb(ctx, f"ahead{first}_hid", [P, EC, SEQ])
        self.u_in = [sem(f"{stage}_u_in{r}") for r in range(2)]
        self.h_out = [sem(f"ah{first}_h_out{r}") for r in range(2)]
        self.u_high = sem("hid_u_high")
        self.u_low = sem("hid_u_low")
        self.h_mm = sem("hid_h_mm")
        self.h_act = sem("hid_h_act")

    def load(self, sp, n, r):
        H = EC // 2
        sp.wait_ge(self.u_low, EC * n + H * r + H)
        sp.dma_start(self.ur[:, H * r:H * r + H],
                     self.a["peer_u"][self.layer, NG_FULL + self.first + n, :, H * r:H * r + H]).then_inc(self.u_in[r], 16)

    def store(self, sp, n, r):
        H = EC // 2
        sp.wait_ge(self.h_act, EC * n + H * r + H + 4)
        sp.dma_start(self.a["hidden"][self.first + n, :, H * r:H * r + H], self.hid[:, H * r:H * r + H]).then_inc(self.h_out[r], 16)

    def load_for_next_stage(self, sp, groups):
        sp.wait_ge(self.u_low, EC * groups + 4)
        self.load_next(sp)

    def loads_and_stores(self, sp, groups):
        with sp.Fori(0, groups - 1) as n:
            for r in range(2):
                self.load(sp, n + 1, r)
            for r in range(2):
                self.store(sp, n, r)
        self.load_for_next_stage(sp, groups)
        for r in range(2):
            self.store(sp, groups - 1, r)
        for r in range(2):
            sp.wait_ge(self.h_out[r], 16 * groups + 16)

    def high(self, act, n, c):
        act.wait_ge(self.u_in[c // (EC // 2)], 16 * n + 16)
        act.wait_ge(self.h_mm, EC * n + c + 1)
        self.nc.scalar.activation(self.uh[:, c], self.ur[:, c], ACT.Copy).then_inc(self.u_high, 1)

    def low(self, eng, n, c):
        eng.wait_ge(self.u_high, EC * n + c + 1)
        eng.tensor_tensor(self.ul[:, c], self.ur[:, c], as_f32(self.uh[:, c]), ALU.subtract).then_inc(self.u_low, 1)

    def multiply(self, pe, n, c, part=slice(0, KT)):
        xh, xl = self.x
        if part.start == 0:
            pe.wait_ge(self.h_act, EC * n + c + 1)
            pe.wait_ge(self.u_low, EC * n + c + 5)
        for k in range(part.start, part.stop):
            mm = matmul_split(self.nc, self.bank[4 + c][:], (self.uh[:, c, k, :], self.ul[:, c, k, :]), (xh[:, k, :], xl[:, k, :]),
                              k == 0, k == KT - 1)
        if part.stop == KT:
            mm.then_inc(self.h_mm, 1)

    def gelu(self, act, n, c):
        act.wait_ge(self.h_mm, EC * n + c + 5)
        act.wait_ge(self.h_out[c // (EC // 2)], 16 * n + 16)
        self.nc.scalar.activation(self.hid[:, c, :], self.bank[4 + c][:], ACT.Gelu_apprx_tanh).then_inc(self.h_act, 1)


def route_stage(nc, a, layer, sb, sem, bank, qT, x, ur, load_next, ident, iota_row, rowT, colT, gateT):
    H, K = PEER_HEADS, TOPK
    with ExitStack() as ctx:
        keys = sb(ctx, "keys", [P, N_LISTS, P])
        sc = sb(ctx, "sc", [P, N_LISTS, P])
        sc2 = sb(ctx, "sc2", [P, N_LISTS, P])
        best = sb(ctx, "best", [P, N_LISTS, K])
        best_ix = sb(ctx, "best_ix", [P, N_LISTS, K], U32)
        best_ixf = sb(ctx, "best_ixf", [P, N_LISTS, K])
        cand = sb(ctx, "cand", [P, H, K * K])
        cand2 = sb(ctx, "cand2", [P, H, K * K])
        top = sb(ctx, "top", [P, H, K])
        pos = sb(ctx, "pos", [P, H, K], U32)
        rank = sb(ctx, "rank", [P, 2, H * K], U32)
        rankf = sb(ctx, "rankf", [P, 2, H * K])
        hit = sb(ctx, "hit", [P, H * K, K])
        row = sb(ctx, "row", [P, PAIRS])
        col = sb(ctx, "col", [P, PAIRS])
        gate = sb(ctx, "pgate", [P, H, K])
        total = sb(ctx, "total", [P, H])
        keys_in = sem("rt_keys_in")
        scored = sem("rt_scored")
        sc_ready = sem("rt_sc_ready")
        sc_free = sem("rt_sc_free")
        shifted = sem("rt_shifted")
        expd = sem("rt_expd")
        routed = sem("rt_routed")
        turned = sem("rt_turned")
        taken = sem("rt_taken")
        chain = sem("rt_chain")
        ahead = HiddenAhead(nc, a, layer, ctx, sb, sem, bank, x, ur, load_next, "rt", 0)
        LEAD = 2

        PER_TILE = EC * AHEAD_ROUTE // NT

        def chunks(step, eng, t, start, stop):
            for chunk in range(PER_TILE * t + LEAD + start, min(PER_TILE * t + LEAD + stop, EC * AHEAD_ROUTE)):
                step(eng, chunk // EC, chunk % EC)

        with nc.Block() as block:

            @block.sync
            def _(sp):
                sp.dma_start(keys[:], a["peer_keys"][layer]).then_inc(keys_in, 16)
                for r in range(2):
                    sp.sem_inc(ahead.h_out[r], 16)
                ahead.loads_and_stores(sp, AHEAD_ROUTE)

            @block.gpsimd
            def _(pool):
                pool.sem_inc(ahead.u_low, 4)
                with pool.Fori(0, AHEAD_ROUTE) as n:
                    for c in range(EC):
                        ahead.low(pool, n, c)

            @block.tensor
            def _(pe):
                def score(t):
                    for j in range(4):
                        pe.wait_ge(sc_ready, 4 * t + j + 1)
                        if j == 3 and t:
                            pe.wait_ge(taken, 3 * t)
                        for q in range(4):
                            n = 4 * j + q
                            mm = nc.tensor.matmul(bank[j][:, q * P:(q + 1) * P], qT[:, n // 4, n % 4, t * P:(t + 1) * P],
                                                  keys[:, n, :], start=True, stop=True)
                        mm.then_inc(scored, 1)

                def turn(t, scores_kept):
                    pe.wait_ge(routed, t + 1)
                    pe.wait_ge(sc_ready, scores_kept)
                    for j, src in enumerate((row, col, gate)):
                        v = src[:] if j < 2 else src[:].rearrange("p h k -> p (h k)")
                        nc.tensor.transpose(bank[3][:, j * P:(j + 1) * P], v, ident[:]).then_inc(turned, 1)

                pe.sem_inc(turned, 3)
                pe.sem_inc(ahead.h_mm, 4)
                pe.wait_ge(keys_in, 16)
                score(0)
                for c in range(LEAD):
                    ahead.multiply(pe, 0, c)
                for t in range(NT - 1):
                    chunks(ahead.multiply, pe, t, 0, 2)
                    score(t + 1)
                    chunks(ahead.multiply, pe, t, 2, PER_TILE)
                    turn(t, 4 * t + 12)
                chunks(ahead.multiply, pe, NT - 1, 0, PER_TILE)
                turn(NT - 1, 4 * NT + 4)

            @block.scalar
            def _(act):
                def keep_scores(t):
                    act.wait_ge(sc_free, t + 1)
                    for j in range(4):
                        act.wait_ge(scored, 4 * t + j + 1)
                        nc.scalar.activation(sc[:, 4 * j:4 * j + 4, :].rearrange("p q n -> p (q n)"), bank[j][:],
                                             ACT.Copy).then_inc(sc_ready, 1)

                def gelu_and_next(act, n, c):
                    ahead.gelu(act, n, c)
                    if n + 1 < AHEAD_ROUTE:
                        ahead.high(act, n + 1, c)

                def exponentials(t):
                    act.wait_ge(shifted, t + 1)
                    nc.scalar.activation(gate[:], gate[:], ACT.Exp).then_inc(expd, 1)

                def keep_pairs(t):
                    act.wait_ge(turned, 3 * t + 6)
                    for j, dst in enumerate((rowT, colT, gateT)):
                        nc.scalar.activation(dst[:, ds(t * P, P)], bank[3][:, j * P:(j + 1) * P], ACT.Copy).then_inc(taken, 1)

                act.sem_inc(sc_ready, 4)
                act.sem_inc(taken, 3)
                act.sem_inc(sc_free, 1)
                act.sem_inc(ahead.h_act, 4)
                keep_scores(0)
                for c in range(EC):
                    ahead.high(act, 0, c)
                for c in range(LEAD):
                    gelu_and_next(act, 0, c)
                for t in range(NT):
                    chunks(gelu_and_next, act, t, 0, 2)
                    if t + 1 < NT:
                        keep_scores(t + 1)
                    chunks(gelu_and_next, act, t, 2, 7)
                    exponentials(t)
                    chunks(gelu_and_next, act, t, 7, PER_TILE)
                    keep_pairs(t)

            @block.vector
            def _(dve):
                V = nc.vector
                with dve.Fori(0, NT) as t:
                    dve.sem_clear(chain)
                    link = make_link(dve, chain)
                    dve.wait_ge(sc_ready, 4 * t + 8)
                    link(V.memset(total[:], 0.0))
                    for n in range(N_LISTS):
                        ins = V.max(best[:, n, 0:8], sc[:, n, :])
                    link(ins)
                    for n in range(N_LISTS):
                        V.max_index(best_ix[:, n, 0:8], best[:, n, 0:8], sc[:, n, :])
                        ins = V.match_replace(sc2[:, n, :], best[:, n, 0:8], sc[:, n, :], LOWEST)
                    link(ins)
                    V.engine_nop().then_inc(sc_free, 1)
                    for n in range(N_LISTS):
                        ins = V.max(best[:, n, 8:16], sc2[:, n, :])
                    link(ins)
                    for n in range(N_LISTS):
                        ins = V.max_index(best_ix[:, n, 8:16], best[:, n, 8:16], sc2[:, n, :])
                    link(ins)
                    V.tensor_copy(best_ixf[:], best_ix[:])
                    pairs = best[:].rearrange("p (h two) k -> p h two k", two=2)
                    link(V.tensor_tensor(cand[:].rearrange("p h (i j) -> p h i j", i=K),
                                         pairs[:, :, 0, :].unsqueeze(3).to_broadcast([P, H, K, K]),
                                         pairs[:, :, 1, :].unsqueeze(2).to_broadcast([P, H, K, K]), ALU.add))
                    for h in range(H):
                        ins = V.max(top[:, h, 0:8], cand[:, h, :])
                    link(ins)
                    for h in range(H):
                        V.max_index(pos[:, h, 0:8], top[:, h, 0:8], cand[:, h, :])
                        ins = V.match_replace(cand2[:, h, :], top[:, h, 0:8], cand[:, h, :], LOWEST)
                    link(ins)
                    for h in range(H):
                        ins = V.max(top[:, h, 8:16], cand2[:, h, :])
                    link(ins)
                    for h in range(H):
                        ins = V.max_index(pos[:, h, 8:16], top[:, h, 8:16], cand2[:, h, :])
                    link(ins)
                    dve.wait_ge(turned, 3 * t + 3)
                    V.tensor_tensor(gate[:], top[:], top[:, :, 0:1].to_broadcast([P, H, K]), ALU.subtract).then_inc(shifted, 1)
                    pf = pos[:].rearrange("p h k -> p (h k)")
                    V.tensor_scalar(rank[:, 0, :], pf, 4, None, ALU.logical_shift_right)
                    link(V.tensor_scalar(rank[:, 1, :], pf, K - 1, None, ALU.bitwise_and))
                    link(V.tensor_copy(rankf[:], rank[:]))
                    lists = best_ixf[:].rearrange("p (h two) k -> p h two k", two=2)
                    for side, dst in enumerate((row, col)):
                        link(V.tensor_tensor(hit[:], rankf[:, side, :].unsqueeze(2).to_broadcast([P, H * K, K]),
                                             iota_row[:, 0:K].unsqueeze(1).to_broadcast([P, H * K, K]), ALU.is_equal))
                        link(V.tensor_tensor(hit[:].rearrange("p (h k) j -> p h k j", h=H),
                                             hit[:].rearrange("p (h k) j -> p h k j", h=H),
                                             lists[:, :, side, :].unsqueeze(2).to_broadcast([P, H, K, K]), ALU.mult))
                        link(V.tensor_reduce(dst[:], hit[:], AX, ALU.add))
                    dve.wait_ge(expd, t + 1)
                    link(V.tensor_reduce(total[:], gate[:], AX, ALU.add))
                    link(V.reciprocal(total[:], total[:]))
                    link(V.tensor_tensor(gate[:], gate[:], total[:].unsqueeze(2).to_broadcast([P, H, K]), ALU.mult))
                    V.engine_nop().then_inc(routed, 1)


def spread_stage(nc, a, layer, sb, sem, bank, x, ur, load_next, iota_row, rowT, colT, gateT):
    STEP = 16
    with ExitStack() as ctx:
        ahead = HiddenAhead(nc, a, layer, ctx, sb, sem, bank, x, ur, load_next, "sp", AHEAD_ROUTE)
        hot_row = sb(ctx, "hot_row", [P, STEP, P])
        hot_col = sb(ctx, "hot_col", [P, STEP, P])
        cols = sb(ctx, "cols", [P, 3, STEP])
        rows = sb(ctx, "rows", [P, 2, 4])
        row_of = sb(ctx, "row_of", [P, 4])
        distance = sb(ctx, "distance", [P, 4, P])
        stage = sb(ctx, "stage", [P, 2, P, TB])
        rows_hot = sem("sp_rows_hot")
        rows_hot_a = sem("sp_rows_hot_a")
        cols_hot = sem("sp_cols_hot")
        chain_a = sem("sp_chain_a")
        spread = sem("sp_spread")
        kept = sem("sp_kept")
        stored = [sem(f"sp_stored{b}") for b in range(2)]
        chain = sem("sp_chain")
        TURNS = TB // STEP

        def unrolled(eng, body):
            def pair(m, last):
                for b in range(2):
                    for q in range(TURNS):
                        body((2 * m + b) * TURNS + q, b, q, m, last)
            with eng.Fori(0, NTB // 2 - 1) as m:
                pair(m, False)
            pair(NTB // 2 - 1, True)

        def two_ahead(step, eng, b, q, m, last, turn):
            if q % 2 == turn and not (b == 1 and last):
                step(eng, m + b, (2 * b + q // 2 + 2) % EC)

        with nc.Block() as block:

            @block.gpsimd
            def _(pool):
                def body(n):
                    for g in range(2, 4):
                        pool.wait_ge(spread, 4 * n + g + 1)
                        nc.gpsimd.tensor_copy(rows[:, g % 2, :], rowT[:, ds(n * STEP + 4 * g, 4)])
                        pool.drain()
                        for s in range(4):
                            ins = nc.gpsimd.tensor_scalar(hot_row[:, 4 * g + s, :], iota_row[:], rows[:, g % 2, s:s + 1], None, ALU.is_equal)
                        ins.then_inc(rows_hot, 1)

                with pool.Fori(0, NTB * TURNS) as n:
                    body(n)

            @block.vector
            def _(dve):
                def body(n, b, q, m, last):
                    dve.wait_ge(cols_hot, 4 * n + 4)
                    nc.vector.tensor_copy(cols[:, 0, :], colT[:, ds(n * STEP, STEP)])
                    nc.vector.tensor_copy(cols[:, 2, :], rowT[:, ds(n * STEP, STEP)])
                    nc.vector.tensor_copy(cols[:, 1, :], gateT[:, ds(n * STEP, STEP)]).then_inc(chain, 1)
                    dve.wait_ge(chain, n + 1)
                    for g in range(4):
                        dve.wait_ge(spread, 4 * n + g + 1)
                        if g == 0:
                            for s in range(4 * g, 4 * g + 4):
                                nc.vector.tensor_scalar(hot_row[:, s, :], iota_row[:], cols[:, 2, s:s + 1], None, ALU.is_equal)
                        for s in range(4 * g, 4 * g + 4):
                            ins = nc.vector.tensor_scalar(hot_col[:, s, :], iota_row[:], cols[:, 0, s:s + 1], cols[:, 1, s:s + 1],
                                                          ALU.is_equal, ALU.mult)
                        ins.then_inc(cols_hot, 1)
                        if g == 1:
                            two_ahead(ahead.low, dve, b, q, m, last, 1)

                dve.sem_inc(cols_hot, 4)
                dve.sem_inc(ahead.u_low, 4)
                for c in range(2):
                    ahead.low(dve, 0, c)
                unrolled(dve, body)

            @block.tensor
            def _(pe):
                def body(n, b, q, m, last):
                    for g in range(4):
                        pe.wait_ge(kept, 4 * n + g + 1)
                        if g == 1:
                            pe.wait_ge(rows_hot_a, n + 1)
                        if g >= 2:
                            pe.wait_ge(rows_hot, 2 * n + g - 1)
                        pe.wait_ge(cols_hot, 4 * n + g + 5)
                        for s in range(4):
                            mm = nc.tensor.matmul(bank[g][:, s * P:(s + 1) * P], hot_row[:, 4 * g + s, :], hot_col[:, 4 * g + s, :],
                                                  start=True, stop=True)
                        mm.then_inc(spread, 1)
                        if g == 1:
                            part = slice(q % 2 * KT // 2, (q % 2 + 1) * KT // 2)
                            ahead.multiply(pe, m, 2 * b + q // 2, part)

                pe.sem_inc(spread, 4)
                pe.sem_inc(ahead.h_mm, 4)
                unrolled(pe, body)

            @block.scalar
            def _(act):
                def one_hot_rows(n):
                    act.wait_ge(spread, 4 * n + 2)
                    nc.scalar.activation(row_of[:], rowT[:, ds(n * STEP + 4, 4)], ACT.Copy).then_inc(chain_a, 1)
                    act.wait_ge(chain_a, 2 * n + 1)
                    for s in range(4):
                        ins = nc.scalar.activation(distance[:, s, :], iota_row[:], ACT.Abs, scale=-1.0, bias=row_of[:, s:s + 1])
                    ins.then_inc(chain_a, 1)
                    act.wait_ge(chain_a, 2 * n + 2)
                    nc.scalar.activation(hot_row[:, 4:8, :], distance[:], ACT.Relu, scale=-1.0, bias=1.0).then_inc(rows_hot_a, 1)

                def body(n, b, q, m, last):
                    two_ahead(ahead.high, act, b, q, m, last, 0)
                    act.wait_ge(stored[b], 16 * m + 16)
                    for g in range(4):
                        act.wait_ge(spread, 4 * n + g + 5)
                        nc.scalar.activation(stage[:, b, :, q * STEP + 4 * g:q * STEP + 4 * g + 4],
                                             bank[g][:].rearrange("p (t c) -> p c t", t=4), ACT.Copy).then_inc(kept, 1)
                        if g == 1 and not (last and b == 1 and q == TURNS - 1):
                            one_hot_rows(n + 1)
                        if g == 2 and q % 2 == 1:
                            ahead.gelu(act, m, 2 * b + q // 2)

                act.sem_inc(kept, 4)
                act.sem_inc(stored[0], 16)
                act.sem_inc(stored[1], 16)
                act.sem_inc(ahead.h_act, 4)
                for c in range(2):
                    ahead.high(act, 0, c)
                one_hot_rows(0)
                unrolled(act, body)

            @block.sync
            def _(sp):
                def pair(m, last):
                    if not last:
                        for r in range(2):
                            ahead.load(sp, m + 1, r)
                    else:
                        ahead.load_for_next_stage(sp, AHEAD_SPREAD)
                    for b in range(2):
                        sp.wait_ge(kept, (2 * m + b) * 4 * TURNS + 4 * TURNS + 4)
                        sp.dma_start(a["gates"][:, 2 * m + b], stage[:, b]).then_inc(stored[b], 16)
                        ahead.store(sp, m, b)

                for r in range(2):
                    sp.sem_inc(ahead.h_out[r], 16)
                with sp.Fori(0, NTB // 2 - 1) as m:
                    pair(m, False)
                pair(NTB // 2 - 1, True)
    return [(stored[b], 16 * (NTB // 2) + 16) for b in range(2)] + [(ahead.h_out[b], 16 * AHEAD_SPREAD + 16) for b in range(2)]


def experts_stage(nc, a, layer, sb, sem, bank, xh, xl, ur, x_tok, storing):
    V, A = nc.vector, nc.scalar.activation
    H = EC // 2
    with ExitStack() as ctx:
        uh = sb(ctx, "u_high", [P, EC, KT, P], F32R)
        ul = sb(ctx, "u_low", [P, EC, KT, P], F32R)
        vr = sb(ctx, "v_raw", [P, EC, D_MODEL])
        vh = sb(ctx, "v_high", [P, EC, D_MODEL], F32R)
        vl = sb(ctx, "v_low", [P, EC, D_MODEL], F32R)
        G = sb(ctx, "G", [P, NTB, EC, TB])
        hid = sb(ctx, "hid", [P, EC, SEQ])
        wh = sb(ctx, "w_high", [P, 2, EC, SEQ], F32R)
        wl = sb(ctx, "w_low", [P, 2, EC, SEQ], F32R)
        u_in = [sem(f"ex_u_in{r}") for r in range(2)]
        v_in = [sem(f"ex_v_in{r}") for r in range(2)]
        G_in = sem("ex_G_in")
        hid_in = sem("ex_hid_in")
        u_high = sem("hid_u_high")
        u_low = sem("hid_u_low")
        v_high = sem("ex_v_high")
        v_low = sem("ex_v_low")
        h_mm = sem("hid_h_mm")
        h_act = sem("hid_h_act")
        w_mul = sem("ex_w_mul")
        w_high = sem("ex_w_high")
        w_low = sem("ex_w_low")
        y_mm = sem("ex_y_mm")
        y_add = sem("ex_y_add")
        scaled = sem("ex_scaled")

        with nc.Block() as block:

            @block.sync
            def _(sp):
                def gates_and_v(n):
                    sp.wait_ge(w_mul, EC * n + EC)
                    sp.dma_start(G[:], a["gates"][:, :, ds(n * EC, EC), :]).then_inc(G_in, 16)
                    for r in range(2):
                        cols = slice(r * 512, (r + 1) * 512)
                        sp.wait_ge(v_low, EC * n + 2 * r + 2)
                        sp.dma_start(vr[:, :, cols], a["peer_v"][layer, :, ds(n * EC, EC), cols]).then_inc(v_in[r], 16)

                def load_u(n):
                    for r in range(2):
                        sp.wait_ge(u_low, EC * n + H * r + H)
                        sp.dma_start(ur[:, H * r:H * r + H], a["peer_u"][layer, n, :, H * r:H * r + H]).then_inc(u_in[r], 16)

                for signal, value in storing:
                    sp.wait_ge(signal, value)
                gates_and_v(0)
                with sp.Fori(1, NG_FULL) as n:
                    load_u(n)
                    gates_and_v(n)
                with sp.Fori(0, NG_AHEAD) as m:
                    sp.wait_ge(w_low, EC * NG_FULL + EC * m + EC)
                    sp.dma_start(hid[:], a["hidden"][m]).then_inc(hid_in, 16)
                    gates_and_v(m + NG_FULL)

            @block.tensor
            def _(pe):
                pe.sem_inc(h_mm, 4)
                pe.sem_inc(y_mm, 16)

                def hidden(n):
                    for c in range(EC):
                        pe.wait_ge(h_act, EC * n + c + 1)
                        pe.wait_ge(u_low, EC * n + c + 5)
                        for k in range(KT):
                            mm = matmul_split(nc, bank[c][:], (uh[:, c, k, :], ul[:, c, k, :]), (xh[:, k, :], xl[:, k, :]),
                                              k == 0, k == KT - 1)
                        mm.then_inc(h_mm, 1)

                def output(n, b):
                    pe.wait_ge(w_low, EC * n + EC + 4)
                    for j in range(2 * NT):
                        tok, cols = slice(j % NT * P, (j % NT + 1) * P), slice(j // NT * 512, (j // NT + 1) * 512)
                        if j % NT == 0:
                            pe.wait_ge(v_low, EC * n + 2 * (j // NT) + 6)
                        pe.wait_ge(y_add, 8 * n + j + 5)
                        for c in range(EC):
                            mm = matmul_split(nc, bank[4 + j % 4][:], (wh[:, b, c, tok], wl[:, b, c, tok]),
                                              (vh[:, c, cols], vl[:, c, cols]), c == 0, c == EC - 1)
                        mm.then_inc(y_mm, 1)

                hidden(0)
                with pe.Fori(0, NG_FULL // 2 - 1) as i:
                    hidden(2 * i + 1)
                    output(2 * i, 0)
                    hidden(2 * i + 2)
                    output(2 * i + 1, 1)
                hidden(NG_FULL - 1)
                output(NG_FULL - 2, 0)
                output(NG_FULL - 1, 1)
                with pe.Fori(NG_FULL // 2, NG // 2) as i:
                    output(2 * i, 0)
                    output(2 * i + 1, 1)

            @block.scalar
            def _(act):
                act.sem_inc(h_act, 4)

                def split_u(n, c):
                    act.wait_ge(u_in[c // H], 16 * n + 16)
                    act.wait_ge(h_mm, EC * n + c + 1)
                    A(uh[:, c], ur[:, c], ACT.Copy).then_inc(u_high, 1)

                def group(n, b, ahead=False, last=False):
                    for c in range(EC):
                        if not ahead:
                            act.wait_ge(h_mm, EC * n + c + 5)
                            act.wait_ge(w_low, EC * n + c + 1)
                            A(hid[:, c, :], bank[c][:], ACT.Gelu_apprx_tanh).then_inc(h_act, 1)
                            if not last:
                                split_u(n + 1, c)
                        if c == 0:
                            act.wait_ge(y_mm, 8 * n + 8)
                        act.wait_ge(w_mul, EC * n + c + 5)
                        A(wh[:, b, c, :], hid[:, c, :], ACT.Copy).then_inc(w_high, 1)
                    for r in range(2):
                        act.wait_ge(v_in[r], 16 * n + 16)
                        act.wait_ge(y_mm, 8 * n + NT * r + 12)
                        for c in range(0, EC, 2):
                            A(vh[:, c:c + 2, r * 512:(r + 1) * 512], vr[:, c:c + 2, r * 512:(r + 1) * 512],
                              ACT.Copy).then_inc(v_high, 1)

                for c in range(EC):
                    split_u(0, c)
                for signal, value in storing:
                    act.wait_ge(signal, value)
                with act.Fori(0, NG_FULL // 2 - 1) as i:
                    group(2 * i, 0)
                    group(2 * i + 1, 1)
                group(NG_FULL - 2, 0)
                group(NG_FULL - 1, 1, last=True)
                with act.Fori(NG_FULL // 2, NG // 2) as i:
                    group(2 * i, 0, ahead=True)
                    group(2 * i + 1, 1, ahead=True)

            @block.vector
            def _(dve):
                dve.sem_inc(u_low, 4)
                dve.sem_inc(v_low, 4)
                dve.sem_inc(w_mul, 4)
                dve.sem_inc(w_low, 4)
                dve.sem_inc(y_add, 8)
                V.tensor_scalar(x_tok[:], x_tok[:], ALPHA, None, ALU.mult).then_inc(scaled, 1)
                dve.wait_ge(scaled, 1)

                def split_u(n, c):
                    dve.wait_ge(u_high, EC * n + c + 1)
                    V.tensor_tensor(ul[:, c], ur[:, c], as_f32(uh[:, c]), ALU.subtract).then_inc(u_low, 1)

                def times_gates(n, c):
                    h = hid[:, c, :].rearrange("p (q t) -> p q t", t=TB)
                    V.tensor_tensor(h, h, G[:, :, c, :], ALU.mult).then_inc(w_mul, 1)

                def weights_low(n, b, c):
                    dve.wait_ge(w_high, EC * n + c + 1)
                    V.tensor_tensor(wl[:, b, c, :], hid[:, c, :], as_f32(wh[:, b, c, :]), ALU.subtract).then_inc(w_low, 1)

                def weigh(n, b, last=False):
                    dve.wait_ge(G_in, 16 * n + 16)
                    for c in range(EC):
                        dve.wait_ge(h_act, EC * n + c + 5)
                        times_gates(n, c)
                        if not last:
                            split_u(n + 1, c)
                        weights_low(n, b, c)

                def add(n, j):
                    part = x_tok[:, j % NT, j // NT * 512:(j // NT + 1) * 512]
                    dve.wait_ge(y_mm, 8 * n + j + 17)
                    dve.wait_ge(y_add, 8 * n + j + 1)
                    V.tensor_tensor(part, part, bank[4 + j % 4][:], ALU.add).then_inc(y_add, 1)

                def split_v(n, r):
                    cols = slice(r * 512, (r + 1) * 512)
                    for c in range(0, EC, 2):
                        dve.wait_ge(v_high, EC * n + 2 * r + c // 2 + 1)
                        V.tensor_tensor(vl[:, c:c + 2, cols], vr[:, c:c + 2, cols], as_f32(vh[:, c:c + 2, cols]),
                                        ALU.subtract).then_inc(v_low, 1)

                def finish(n, more=True):
                    for r in range(2):
                        for j in range(NT * r, NT * r + NT):
                            add(n, j)
                        if more:
                            split_v(n + 1, r)

                def weigh_and_finish(n, b):
                    dve.wait_ge(G_in, 16 * n + 32)
                    dve.wait_ge(hid_in, 16 * (n - NG_FULL) + 32)
                    for j in range(NT):
                        times_gates(n + 1, j)
                        add(n, j)
                    split_v(n + 1, 0)
                    for j in range(NT, 2 * NT):
                        weights_low(n + 1, b, j - NT)
                        add(n, j)
                    split_v(n + 1, 1)

                for c in range(EC):
                    split_u(0, c)
                weigh(0, 0)
                for r in range(2):
                    split_v(0, r)
                with dve.Fori(0, NG_FULL // 2 - 1) as i:
                    weigh(2 * i + 1, 1)
                    finish(2 * i)
                    weigh(2 * i + 2, 0)
                    finish(2 * i + 1)
                weigh(NG_FULL - 1, 1, last=True)
                finish(NG_FULL - 2)
                with dve.Fori(NG_FULL // 2 - 1, NG // 2 - 1) as i:
                    weigh_and_finish(2 * i + 1, 0)
                    weigh_and_finish(2 * i + 2, 1)
                finish(NG - 1, more=False)


def mixer_stage(nc, a, layer, sb, sem, bank, x, projT, projN, ffT, ident, lvl_mask, neg_mask, head_sel,
                pool_rc, scan_keep, one_minus_lb):
    V = nc.vector
    NL = len(LEVELS)
    with ExitStack() as ctx:
        tmp = [sb(ctx, f"tmp{i}", [P, WT, SEQ]) for i in range(2)]
        gl_wh = sb(ctx, "gl_wh", [P, 2, KT, P], F32R)
        gl_wl = sb(ctx, "gl_wl", [P, 2, KT, P], F32R)
        gl_kept = sb(ctx, "gl_kept", [P, 2, SEQ])
        with ExitStack() as early:
            gl_raw = sb(early, "gl_raw", [P, 2, KT, P])
        att = sb(ctx, "att", [P, NT, WT, P])
        state = sb(ctx, "state", [P, WT, P])
        decay = sb(ctx, "decay", [P, WT, NT])
        ss = sb(ctx, "ss", [P, NT, WT])
        rms = sb(ctx, "rms", [P, NT, WT])
        pool_w = sb(ctx, "pool_w", [P, WT, P])
        pool_scale = sb(ctx, "pool_scale", [P, WT])
        norm_g = sb(ctx, "norm_g", [P, 1])
        ws = sb(ctx, "ws", [P, WT, P])
        bs_row = sb(ctx, "bs_row", [P, WT, P])
        lng_row = sb(ctx, "lng_row", [P, W])
        lnb_row = sb(ctx, "lnb_row", [P, W])
        gstats = sb(ctx, "gstats", [P, NT, 6])
        gmv = sb(ctx, "gmv", [P, NT, 2])
        gstd = sb(ctx, "gstd", [P, NT])
        b_fox = sb(ctx, "b_fox", [WT, 1])
        fz = sb(ctx, "fz", [WT, 2, SEQ])
        fones = sb(ctx, "fones", [WT, 1])
        cum = sb(ctx, "cum", [WT, 2, SEQ])
        fmax = sb(ctx, "fmax", [P, 16])
        fsum = sb(ctx, "fsum", [P, 16])
        prob = sb(ctx, "prob", [P, 2, SEQ])
        probT = sb(ctx, "probT", [P, 2, SEQ])

        pin, q, k, gu, fq, fk = (projT[:, j] for j in (T_POOL, T_HQ, T_HF, T_GU, T_FQ, T_FK))
        val, hg, gv, fv = (projN[:, j] for j in (N_HI, N_HG, N_GV, N_FV))
        cumb = sb(ctx, "cumb", [P, WT, SEQ])[:]

        def flat(v):
            return v.rearrange("p h t -> p (h t)")

        params_in = {n: sem(f"mx_{n}_in") for n in ("poolw", "pools", "normg", "ws", "bs", "lng", "lnb", "bfox")}
        ws_masked = sem("mx_ws_masked")
        fones_done = sem("mx_fones_done")
        q_act, hg_act, gu_act, gv_act, sig_done, logf_done = (sem(f"mx_{n}") for n in ("q_act", "hg_act", "gu_act", "gv_act", "sig_done", "logf_done"))
        diff_ready, pool_mm, pool_kept = sem("mx_diff_ready"), sem("mx_pool_mm"), sem("mx_pool_kept")
        gvar, gsqrt, gnorm, gm_mm, gm_used = (sem(f"mx_{n}") for n in ("gvar", "gsqrt", "gnorm", "gm_mm", "gm_used"))
        k_ready, lvl_d, lvl_e, lvl_x, lvl_mm, att_done = (sem(f"mx_{n}") for n in ("k_ready", "lvl_d", "lvl_e", "lvl_x", "lvl_mm", "att_done"))
        kd_d, kd_e, kd_x, qin_x, kd_turned, kd_kept = (sem(f"mx_{n}") for n in ("kd_d", "kd_e", "kd_x", "qin_x", "kd_turned", "kd_kept"))
        o_mm, o_kept, ds_mm, s_upd, ss_ready, ss_sqrt, o_normed, o_turned = (
            sem(f"mx_{n}") for n in ("o_mm", "o_kept", "ds_mm", "s_upd", "ss_ready", "ss_sqrt", "o_normed", "o_turned"))
        fz_ready, fz_exp, c_ready, fq_ready = (sem(f"mx_{n}") for n in ("fz_ready", "fz_exp", "c_ready", "fq_ready"))
        fx_mm, fx_max, fx_exp, fx_p, fx_turned, fx_pt, fx_o, fx_kept = (
            sem(f"mx_{n}") for n in ("fx_mm", "fx_max", "fx_exp", "fx_p", "fx_turned", "fx_pt", "fx_o", "fx_kept"))
        gl_in = [sem(f"mg_loaded{b}") for b in range(2)]
        gl_out = [sem(f"mx_gl_out{b}") for b in range(2)]
        gl_high, gl_low, gl_mm, gl_ready = sem("mg_w_high"), sem("mg_w_low"), sem("mg_gate_mm"), sem("mg_gated")
        chain = sem("mx_chain")
        chain_a = sem("mx_chain_a")

        UNITS = WT * NT
        PE_GMLP = 3
        after = ([(("level", i), 2) for i in range(NL + 1)] + [(("keys", 0), 1)] + [(("tile", t), 1) for t in range(NT)]
                 + [(("norm", 0), 2)])
        first_step, at = {}, 0
        for part, count in after:
            first_step[part] = range(at, at + count)
            at += count
        first_step[("end", 0)] = range(at, UNITS + 3)

        def fox_steps(step, part):
            for s in first_step[part]:
                step(s)

        def load_gate(sp, n):
            if n >= 2:
                sp.wait_ge(gl_low, n - 1)
            sp.dma_start(gl_raw[:, n % 2], a["w_merge"][layer, 0, n, :, 0:KT]).then_inc(gl_in[n % 2], 16)

        def high_gate(act, n):
            act.wait_ge(gl_in[n % 2], 16 * (n // 2) + 16)
            if n >= 2:
                act.wait_ge(gl_mm, n - 1)
            nc.scalar.activation(gl_wh[:, n % 2], gl_raw[:, n % 2], ACT.Copy).then_inc(gl_high, 1)

        def low_gate(pool, n):
            pool.wait_ge(gl_high, n + 1)
            nc.gpsimd.tensor_tensor(gl_wl[:, n % 2], gl_raw[:, n % 2], as_f32(gl_wh[:, n % 2]), ALU.subtract).then_inc(gl_low, 1)

        def multiply_gate(pe, n):
            pe.wait_ge(gl_low, n + 1)
            if n >= 2:
                pe.wait_ge(gl_ready, n - 1)
            for k_in in range(KT):
                mm = matmul_split(nc, bank[n % 2][:], (gl_wh[:, n % 2, k_in, :], gl_wl[:, n % 2, k_in, :]),
                                  (x[0][:, k_in, :], x[1][:, k_in, :]), k_in == 0, k_in == KT - 1)
            mm.then_inc(gl_mm, 1)

        def keep_gate(act, n):
            act.wait_ge(gl_mm, n + 1)
            if n >= 2:
                act.wait_ge(gl_out[n % 2], 16 * (n // 2))
            nc.scalar.activation(gl_kept[:, n % 2, :], bank[n % 2][:], ACT.Copy).then_inc(gl_ready, 1)
            if n + 2 < GATES_AHEAD:
                high_gate(act, n + 2)

        with nc.Block() as block:

            @block.sync
            def _(sp):
                load_gate(sp, 0)
                load_gate(sp, 1)
                for name, dst, src in (
                        ("bfox", b_fox, a["b_fox_f"][layer]), ("poolw", pool_w, a["pool_w"][layer]),
                        ("pools", pool_scale, a["pool_scale"][layer]),
                        ("lng", lng_row, a["gmlp_ln_g"][layer].partition_broadcast(P)),
                        ("lnb", lnb_row, a["gmlp_ln_b"][layer].partition_broadcast(P)),
                        ("ws", ws, a["gmlp_ws"][layer]), ("normg", norm_g, a["hgrn_norm_g"][layer])):
                    sp.dma_start(dst[:], src).then_inc(params_in[name], 16)
                sp.dma_start(bs_row[:].rearrange("p g t -> p (g t)"),
                             a["gmlp_bs"][layer].partition_broadcast(P)).then_inc(params_in["bs"], 16)
                for n in range(GATES_AHEAD):
                    if n + 2 < GATES_AHEAD:
                        load_gate(sp, n + 2)
                    sp.wait_ge(gl_ready, n + 1)
                    sp.dma_start(a["gate_logits"][n], gl_kept[:, n % 2, :]).then_inc(gl_out[n % 2], 16)
                for b in range(2):
                    sp.wait_ge(gl_out[b], 16 * (GATES_AHEAD // 2))

            @block.gpsimd
            def _(pool):
                nc.gpsimd.memset(fones[:], 1.0).then_inc(fones_done, 1)
                low_gate(pool, 0)
                low_gate(pool, 1)
                pool.wait_ge(params_in["ws"], 16)
                nc.gpsimd.affine_select(out=ws[:], in_=ws[:], compare_op=ALU.is_ge, fill=0.0, base=0,
                                        pattern=[[0, WT], [1, P]], channel_multiplier=-1).then_inc(ws_masked, 1)
                for n in range(2, GATES_AHEAD):
                    low_gate(pool, n)

            @block.tensor
            def _(pe):
                def logits(n):
                    h, t = divmod(n, NT)
                    cols = (t + 1) * P
                    b = bank[4 + n % 2]
                    if n >= 2:
                        pe.wait_ge(fx_exp, n - 1)
                    nc.tensor.matmul(b[:, 0:cols], fq[:, h, t * P:(t + 1) * P], fk[:, h, 0:cols], start=True, stop=False)
                    nc.tensor.matmul(b[:, 0:cols], cum[:, 0, t * P:(t + 1) * P], head_sel[:, h, 0:1].to_broadcast([WT, cols]), start=False, stop=False)
                    nc.tensor.matmul(b[:, 0:cols], head_sel[:, h, :], cum[:, 1, 0:cols], start=False, stop=False)
                    nc.tensor.matmul(b[:, t * P:cols], ident[:], neg_mask[:], start=False, stop=True).then_inc(fx_mm, 1)

                def turn(n):
                    pe.wait_ge(fx_p, n + 1)
                    if n:
                        pe.wait_ge(fx_pt, n)
                    for j in range(n % NT + 1):
                        mm = nc.tensor.transpose(bank[6][:, j * P:(j + 1) * P], prob[:, n % 2, j * P:(j + 1) * P], ident[:])
                    mm.then_inc(fx_turned, 1)

                def attend(n):
                    h, t = divmod(n, NT)
                    if t == 0 and h:
                        pe.wait_ge(fx_kept, h)
                    pe.wait_ge(fx_pt, n + 1)
                    for j in range(t + 1):
                        mm = nc.tensor.matmul(bank[7][:, t * P:(t + 1) * P], fv[:, j, h * P:(h + 1) * P],
                                              probT[:, n % 2, j * P:(j + 1) * P], start=(j == 0), stop=(j == t))
                    mm.then_inc(fx_o, 1)

                def fox(s):
                    if s + 1 < UNITS:
                        logits(s + 1)
                    if 0 <= s - 1 < UNITS:
                        turn(s - 1)
                    if 0 <= s - 2 < UNITS:
                        attend(s - 2)

                pe.wait_ge(params_in["poolw"], 16)
                for g in range(WT):
                    if g % 2 == 0:
                        multiply_gate(pe, g // 2)
                    pe.wait_ge(diff_ready, g + 1)
                    if g >= 2:
                        pe.wait_ge(pool_kept, g - 1)
                    nc.tensor.matmul(bank[6 + g % 2][:], pool_w[:, g, :], pin[:, g, :], start=True, stop=True).then_inc(pool_mm, 1)
                for n in range(2, PE_GMLP):
                    multiply_gate(pe, n)
                pe.wait_ge(ws_masked, 1)
                pe.wait_ge(gnorm, 1)
                for g in range(WT):
                    if g < 2:
                        pe.wait_ge(pool_kept, 3 + g)
                    else:
                        pe.wait_ge(gm_used, g - 1)
                    for t in range(NT):
                        mm = nc.tensor.matmul(bank[6 + g % 2][:, t * P:(t + 1) * P], gv[:, t, g * P:(g + 1) * P], ws[:, g, :],
                                              start=True, stop=True)
                    mm.then_inc(gm_mm, 1)
                    if g == 1:
                        multiply_gate(pe, PE_GMLP)
                for n in range(PE_GMLP + 1, GATES_AHEAD):
                    multiply_gate(pe, n)
                pe.wait_ge(fq_ready, 1)
                pe.wait_ge(c_ready, 2)
                pe.wait_ge(gm_used, WT)
                logits(0)
                for i in range(NL + 1):
                    pe.wait_ge(lvl_x, i + 1)
                    kk = tmp[i % 2] if i < NL else tmp[1]
                    qq = tmp[i % 2] if i < NL else tmp[0]
                    for t in range(NT):
                        if i:
                            pe.wait_ge(att_done, NT * (i - 1) + t + 1)
                        elif t == 0:
                            pe.wait_ge(gl_ready, GATES_AHEAD)
                        for h in range(WT):
                            mm = nc.tensor.matmul(bank[t][:, h * P:(h + 1) * P], kk[:, h, t * P:(t + 1) * P],
                                                  qq[:, h, t * P:(t + 1) * P], start=True, stop=True)
                        mm.then_inc(lvl_mm, 1)
                    fox_steps(fox, ("level", i))
                pe.wait_ge(kd_x, 1)
                for t in range(NT):
                    pe.wait_ge(att_done, NT * NL + t + 1)
                    for h in range(WT):
                        mm = nc.tensor.transpose(bank[t][:, h * P:(h + 1) * P], tmp[0][:, h, t * P:(t + 1) * P], ident[:])
                    mm.then_inc(kd_turned, 1)
                fox_steps(fox, ("keys", 0))
                pe.wait_ge(kd_kept, NT)
                pe.wait_ge(qin_x, 1)
                for t in range(NT):
                    if t < NT - 1:
                        if t >= 2:
                            pe.wait_ge(s_upd, t - 1)
                        for h in range(WT):
                            mm = nc.tensor.matmul(bank[2 + t % 2][:, h * P:(h + 1) * P], tmp[1][:, t, h * P:(h + 1) * P],
                                                  val[:, t, h * P:(h + 1) * P], start=True, stop=True)
                        mm.then_inc(ds_mm, 1)
                    if t >= 2:
                        pe.wait_ge(o_kept, t - 1)
                    if t:
                        pe.wait_ge(s_upd, t)
                    for h in range(WT):
                        mm = nc.tensor.matmul(bank[t % 2][:, h * P:(h + 1) * P], att[:, t, h, :], val[:, t, h * P:(h + 1) * P],
                                              start=True, stop=(t == 0))
                        if t:
                            mm = nc.tensor.matmul(bank[t % 2][:, h * P:(h + 1) * P], q[:, h, t * P:(t + 1) * P], state[:, h, :],
                                                  start=False, stop=True)
                    mm.then_inc(o_mm, 1)
                    fox_steps(fox, ("tile", t))
                fox_steps(fox, ("norm", 0))
                pe.wait_ge(o_normed, 1)
                for t in range(NT):
                    for h in range(WT):
                        mm = nc.tensor.transpose(bank[t][:, h * P:(h + 1) * P], tmp[0][:, t, h * P:(h + 1) * P], ident[:])
                    mm.then_inc(o_turned, 1)
                fox_steps(fox, ("end", 0))

            @block.scalar
            def _(act):
                A = nc.scalar.activation
                link = make_link(act, chain_a)

                def fox(s):
                    if s >= 2 and (s - 2) % NT == 0 and s > 2:
                        act.wait_ge(fx_o, s - 2)
                        A(fq[:, (s - 2) // NT - 1, :], bank[7][:], ACT.Copy).then_inc(fx_kept, 1)
                    if s < UNITS:
                        cols = (s % NT + 1) * P
                        act.wait_ge(fx_max, s + 1)
                        if s >= 2:
                            act.wait_ge(fx_turned, s - 1)
                        A(prob[:, s % 2, 0:cols], bank[4 + s % 2][:, 0:cols], ACT.Exp, bias=fmax[:, s:s + 1],
                          accum_out=fsum[:, s:s + 1]).then_inc(fx_exp, 1)
                    n = s - 1
                    if 0 <= n < UNITS:
                        cols = (n % NT + 1) * P
                        act.wait_ge(fx_turned, n + 1)
                        if n >= 2:
                            act.wait_ge(fx_o, n - 1)
                        A(probT[:, n % 2, 0:cols], bank[6][:, 0:cols], ACT.Copy).then_inc(fx_pt, 1)

                A(flat(k), flat(k), ACT.Sigmoid, scale=-1.0).then_inc(sig_done, 1)
                high_gate(act, 0)
                high_gate(act, 1)
                A(flat(gv), flat(gv), ACT.Gelu_apprx_tanh).then_inc(gv_act, 1)
                A(flat(gu), flat(gu), ACT.Gelu_apprx_tanh).then_inc(gu_act, 1)
                act.wait_ge(fz_ready, 1)
                link(A(fz[:, 1, :], fz[:, 1, :], ACT.Exp))
                keep_gate(act, 0)
                act.wait_ge(k_ready, 1)
                A(flat(tmp[0]), flat(k), ACT.Ln, bias=1.0, scale=-1.0).then_inc(logf_done, 1)
                A(fz[:, 1, :], fz[:, 1, :], ACT.Ln, bias=1.0).then_inc(fz_exp, 1)
                act.wait_ge(gvar, 1)
                A(gstd[:], gstd[:], ACT.Sqrt).then_inc(gsqrt, 1)
                A(flat(q), flat(q), ACT.Silu).then_inc(q_act, 1)
                keep_gate(act, 1)
                act.wait_ge(params_in["pools"], 16)
                for g in range(WT):
                    act.wait_ge(pool_mm, g + 1)
                    A(pin[:, g, :], bank[6 + g % 2][:], ACT.Copy, scale=pool_scale[:, g:g + 1]).then_inc(pool_kept, 1)
                A(flat(hg), flat(hg), ACT.Silu).then_inc(hg_act, 1)
                keep_gate(act, 2)
                for i in range(NL):
                    act.wait_ge(lvl_d, i + 1)
                    A(flat(tmp[i % 2]), flat(tmp[i % 2]), ACT.Exp).then_inc(lvl_e, 1)
                    if i == 1:
                        for n in range(3, GATES_AHEAD):
                            keep_gate(act, n)
                    if i:
                        fox_steps(fox, ("level", i - 1))
                act.wait_ge(lvl_d, NL + 1)
                link(A(flat(tmp[1]), flat(tmp[0]), ACT.Exp, scale=-1.0))
                A(flat(tmp[0]), flat(tmp[0]), ACT.Exp).then_inc(lvl_e, 1)
                fox_steps(fox, ("level", NL - 1))
                act.wait_ge(kd_d, 1)
                A(flat(tmp[0]), flat(tmp[0]), ACT.Exp).then_inc(kd_e, 1)
                link(A(decay[:], cumb.rearrange("p h (t n) -> p h t n", n=P)[:, :, :, P - 1], ACT.Exp))
                A(flat(cumb), flat(cumb), ACT.Exp).then_inc(kd_e, 1)
                fox_steps(fox, ("level", NL))
                for t in range(NT):
                    act.wait_ge(kd_turned, t + 1)
                    A(tmp[1][:, t, :], bank[t][:], ACT.Copy).then_inc(kd_kept, 1)
                fox_steps(fox, ("keys", 0))
                for t in range(NT):
                    act.wait_ge(o_mm, t + 1)
                    A(tmp[0][:, t, :], bank[t % 2][:], ACT.Copy).then_inc(o_kept, 1)
                    fox_steps(fox, ("tile", t))
                act.wait_ge(ss_ready, 1)
                A(rms[:], ss[:], ACT.Sqrt).then_inc(ss_sqrt, 1)
                fox_steps(fox, ("norm", 0))
                act.wait_ge(params_in["normg"], 16)
                for t in range(NT):
                    act.wait_ge(o_turned, t + 1)
                    A(q[:, :, t * P:(t + 1) * P], bank[t][:].rearrange("p (h n) -> p h n", h=WT), ACT.Copy,
                      scale=norm_g[:, 0:1])
                fox_steps(fox, ("end", 0))

            @block.vector
            def _(dve):
                link = make_link(dve, chain)

                def fox(s):
                    n = s - 1
                    if 0 <= n < UNITS:
                        cols = (n % NT + 1) * P
                        dve.wait_ge(fx_exp, n + 1)
                        link(V.reciprocal(fsum[:, n:n + 1], fsum[:, n:n + 1]))
                        V.tensor_scalar(prob[:, n % 2, 0:cols], prob[:, n % 2, 0:cols], fsum[:, n:n + 1], None,
                                        ALU.mult).then_inc(fx_p, 1)
                    if s < UNITS:
                        cols = (s % NT + 1) * P
                        dve.wait_ge(fx_mm, s + 1)
                        V.tensor_reduce(fmax[:, s:s + 1], bank[4 + s % 2][:, 0:cols], AX, ALU.max, negate=True).then_inc(fx_max, 1)

                def blocks(v, r):
                    return v.rearrange("p h (n two r) -> p (h n) two r", two=2, r=r)

                def exponents(i):
                    h = LEVELS[i]
                    n = WT * SEQ // (2 * h)
                    if i >= 2:
                        dve.wait_ge(lvl_mm, NT * (i - 1))
                    x, b = blocks(tmp[i % 2][:], h), blocks(cumb, h)
                    anchor = b[:, :, 0, h - 1:h].to_broadcast([P, n, h])
                    V.tensor_tensor(x[:, :, 0, :], anchor, b[:, :, 0, :], ALU.subtract)
                    V.tensor_tensor(x[:, :, 1, :], b[:, :, 1, :], anchor, ALU.subtract).then_inc(lvl_d, 1)

                src = pin
                for i, w in enumerate(POOL_WINDOWS):
                    dst, sh = tmp[i % 2][:], w // 2
                    V.tensor_tensor(dst[:, i:, sh:], src[:, i:, sh:], src[:, i:, 0:SEQ - sh], ALU.add)
                    link(V.tensor_copy(dst[:, i:, 0:sh], src[:, i:, 0:sh]))
                    link(V.tensor_tensor(prob[:, 0, 0:16], dst[:, i, 0:16], pool_rc[:, i, :], ALU.mult))
                    V.tensor_tensor(pin[:, i, 0:16], prob[:, 0, 0:16], pin[:, i, 0:16], ALU.subtract)
                    V.scalar_tensor_tensor(out=pin[:, i, 16:], in0=dst[:, i, 16:], scalar=1.0 / w,
                                           in1=pin[:, i, 16:], op0=ALU.mult, op1=ALU.subtract).then_inc(diff_ready, 1)
                    dve.wait_ge(diff_ready, i + 1)
                    src = dst
                dve.wait_ge(params_in["bfox"], 16)
                link(V.tensor_scalar(fz[:, 0, :], ffT[:], b_fox[:, 0:1], None, ALU.add))
                link(V.tensor_scalar(fz[:, 1, :], fz[:, 0, :], -1.0, None, ALU.mult))
                V.tensor_tensor(fz[:, 1, :], fz[:, 0, :], fz[:, 1, :], ALU.min).then_inc(fz_ready, 1)
                V.tensor_scalar(flat(fq), flat(fq), FOX_SCALE, None, ALU.mult).then_inc(fq_ready, 1)
                dve.wait_ge(sig_done, 1)
                for h in range(WT):
                    ins = V.tensor_scalar(k[:, h, :], k[:, h, :], one_minus_lb[:, ds(layer, 1), h], None, ALU.mult)
                ins.then_inc(k_ready, 1)
                dve.wait_ge(gv_act, 1)
                for t in range(NT):
                    ins = V.bn_stats(gstats[:, t, :], gv[:, t, :])
                link(ins)
                for t in range(NT):
                    ins = V.bn_aggr(gmv[:, t, :], gstats[:, t, :])
                link(ins)
                V.tensor_scalar(gstd[:], gmv[:, :, 1], LN_EPS, None, ALU.add).then_inc(gvar, 1)
                dve.wait_ge(logf_done, 1)
                for h in range(WT):
                    ins = V.tensor_tensor_scan(cumb[:, h, :], scan_keep[:], tmp[0][:, h, :], 0.0, ALU.mult, ALU.add)
                link(ins)
                exponents(0)
                exponents(1)
                dve.wait_ge(gsqrt, 1)
                link(V.reciprocal(gstd[:], gstd[:]))
                for t in range(NT):
                    ins = V.tensor_scalar(gv[:, t, :], gv[:, t, :], gmv[:, t, 0:1], gstd[:, t:t + 1], ALU.subtract, ALU.mult)
                link(ins)
                dve.wait_ge(params_in["lng"], 16)
                link(V.tensor_tensor(gv, gv, lng_row[:].unsqueeze(1).to_broadcast([P, NT, W]), ALU.mult))
                dve.wait_ge(params_in["lnb"], 16)
                V.tensor_tensor(gv, gv, lnb_row[:].unsqueeze(1).to_broadcast([P, NT, W]), ALU.add).then_inc(gnorm, 1)
                dve.wait_ge(fz_exp, 1)
                dve.wait_ge(fones_done, 1)
                link(V.tensor_scalar(fz[:, 0, :], fz[:, 0, :], 0.0, None, ALU.min))
                link(V.tensor_tensor(fz[:, 0, :], fz[:, 0, :], fz[:, 1, :], ALU.subtract))
                V.tensor_tensor_scan(cum[:, 0, :], fones[:].to_broadcast([WT, SEQ]), fz[:, 0, :], 0.0, ALU.mult, ALU.add).then_inc(c_ready, 1)
                dve.wait_ge(c_ready, 1)
                V.tensor_scalar(cum[:, 1, :], cum[:, 0, :], -1.0, None, ALU.mult).then_inc(c_ready, 1)
                dve.wait_ge(params_in["bs"], 16)
                dve.wait_ge(gu_act, 1)
                for g in range(WT):
                    dve.wait_ge(gm_mm, g + 1)
                    V.tensor_tensor(prob[:, g % 2, :].rearrange("p (t n) -> p t n", t=NT), bank[6 + g % 2][:].rearrange("p (t n) -> p t n", t=NT),
                                    bs_row[:, g:g + 1, :].to_broadcast([P, NT, P]), ALU.add).then_inc(gm_used, 1)
                    dve.wait_ge(gm_used, g + 1)
                    V.tensor_tensor(gu[:, g, :], prob[:, g % 2, :], gu[:, g, :], ALU.mult)
                dve.wait_ge(gl_low, GATES_AHEAD)
                link(V.memset(att[:], 0.0))

                def factors(i):
                    h = LEVELS[i]
                    dve.wait_ge(lvl_e, i + 1)
                    if i == 0:
                        dve.wait_ge(q_act, 1)
                    x = blocks(tmp[i % 2][:], h)
                    V.tensor_tensor(x[:, :, 0, :], x[:, :, 0, :], blocks(k, h)[:, :, 0, :], ALU.mult)
                    V.tensor_tensor(x[:, :, 1, :], x[:, :, 1, :], blocks(q, h)[:, :, 1, :], ALU.mult).then_inc(lvl_x, 1)

                def weights(i):
                    for t in range(NT):
                        dve.wait_ge(lvl_mm, NT * i + t + 1)
                        if i:
                            dve.wait_ge(att_done, NT * (i - 1) + t + 1)
                        V.copy_predicated(att[:, t], lvl_mask[:, i:i + 1, :].bitcast(U32).to_broadcast([P, WT, P]),
                                          bank[t][:].rearrange("p (h n) -> p h n", h=WT)).then_inc(att_done, 1)

                for i in range(NL):
                    if 2 <= i + 1 < NL:
                        exponents(i + 1)
                    factors(i)
                    if i:
                        fox_steps(fox, ("level", i - 1))
                    weights(i)
                dve.wait_ge(lvl_mm, NT * NL)
                d4 = "p h (n r) -> p (h n) r"
                n8 = WT * SEQ // DIAG
                b8 = cumb.rearrange(d4, r=DIAG)
                V.tensor_tensor(tmp[0][:].rearrange(d4, r=DIAG), b8,
                                b8[:, :, DIAG // 2 - 1:DIAG // 2].to_broadcast([P, n8, DIAG]), ALU.subtract).then_inc(lvl_d, 1)
                dve.wait_ge(lvl_e, NL + 1)
                V.tensor_tensor(tmp[0][:], tmp[0][:], q, ALU.mult)
                V.tensor_tensor(tmp[1][:], tmp[1][:], k, ALU.mult).then_inc(lvl_x, 1)
                fox_steps(fox, ("level", NL - 1))
                weights(NL)
                bt = cumb.rearrange("p h (t n) -> p (h t) n", n=P)
                V.tensor_tensor(tmp[0][:].rearrange("p h (t n) -> p (h t) n", n=P),
                                bt[:, :, P - 1:P].to_broadcast([P, WT * NT, P]), bt, ALU.subtract).then_inc(kd_d, 1)
                dve.wait_ge(kd_e, 1)
                V.tensor_tensor(tmp[0][:], tmp[0][:], k, ALU.mult).then_inc(kd_x, 1)
                dve.wait_ge(kd_e, 2)
                V.tensor_tensor(q, q, cumb, ALU.mult).then_inc(qin_x, 1)
                fox_steps(fox, ("level", NL))
                fox_steps(fox, ("keys", 0))
                for t in range(NT - 1):
                    dve.wait_ge(ds_mm, t + 1)
                    dve.wait_ge(o_mm, t + 1)
                    if t == 0:
                        V.tensor_copy(flat(state), bank[2][:]).then_inc(s_upd, 1)
                        fox_steps(fox, ("tile", t))
                        continue
                    dve.wait_ge(s_upd, t)
                    for h in range(WT):
                        ins = V.scalar_tensor_tensor(out=state[:, h, :], in0=state[:, h, :], scalar=decay[:, h, t:t + 1],
                                                     in1=bank[2 + t % 2][:, h * P:(h + 1) * P], op0=ALU.mult, op1=ALU.add)
                    ins.then_inc(s_upd, 1)
                    fox_steps(fox, ("tile", t))
                fox_steps(fox, ("tile", NT - 1))
                dve.wait_ge(o_kept, NT)
                sq = cumb
                link(V.tensor_tensor(sq, tmp[0][:], tmp[0][:], ALU.mult))
                link(V.tensor_reduce(ss[:], sq.rearrange("p t (h n) -> p t h n", h=WT), AX, ALU.add))
                V.tensor_scalar(ss[:], ss[:], 1.0 / P, RMS_EPS, ALU.mult, ALU.add).then_inc(ss_ready, 1)
                fox_steps(fox, ("norm", 0))
                dve.wait_ge(ss_sqrt, 1)
                link(V.reciprocal(rms[:], rms[:]))
                o4 = tmp[0][:].rearrange("p t (h n) -> p (t h) n", h=WT)
                link(V.tensor_tensor(o4, o4, rms[:].rearrange("p t h -> p (t h)").unsqueeze(2).to_broadcast([P, NT * WT, P]), ALU.mult))
                dve.wait_ge(hg_act, 1)
                V.tensor_tensor(tmp[0][:], tmp[0][:], hg, ALU.mult).then_inc(o_normed, 1)
                fox_steps(fox, ("end", 0))


def _layout(x, shape, order):
    import numpy as np
    return np.ascontiguousarray(np.asarray(x).reshape(shape).transpose(order))


def kernel(**inputs):
    import numpy as np
    import concourse.bacc as bacc
    from concourse.bass_utils import run_bass_kernel_spmd

    L = DEPTH
    i = {n: np.asarray(x) for n, x in inputs.items()}
    w_in = i["w_in"]
    blocks = w_in[:, :, :10 * W].reshape(L, KT, P, 10, W)[:, :, :, list(W_IN_ORDER), :]
    arrays = {
        "x": np.ascontiguousarray(i["x"]),
        "hgrn_lb_logits": _layout(i["hgrn_lb_logits"], (L, WT, P), (2, 0, 1)),
        "w_in": np.ascontiguousarray(blocks.transpose(0, 3, 2, 1, 4)),
        "w_ff": _layout(w_in[:, :, 10 * W:], (L, KT, P, WT), (0, 2, 1, 3)),
        "b_fox_f": _layout(i["b_fox_f"], (L, WT, 1), (0, 1, 2)),
        "pool_w": _layout(i["pool_w"], (L, WT, P, P), (0, 2, 1, 3)),
        "pool_scale": _layout(i["pool_scale"], (L, WT, P), (0, 2, 1)),
        "hgrn_norm_g": _layout(i["hgrn_norm_g"], (L, P, 1), (0, 1, 2)),
        "gmlp_ln_g": np.ascontiguousarray(i["gmlp_ln_g"]),
        "gmlp_ln_b": np.ascontiguousarray(i["gmlp_ln_b"]),
        "gmlp_ws": _layout(i["gmlp_ws"], (L, WT, P, P), (0, 3, 1, 2)),
        "gmlp_bs": _layout(i["gmlp_bs"], (L, WT * P), (0, 1)),
        "b_gate": _layout(i["b_gate"], (L, 4, KT, P), (0, 3, 2, 1)),
        "w_merge": np.ascontiguousarray(np.concatenate(
            [i["w_gate"].reshape(L, KT, P, 4, KT, P).transpose(0, 3, 4, 2, 1, 5),
             i["w_branch"].reshape(L, 4, WT, P, KT, P).transpose(0, 1, 4, 3, 2, 5)], axis=4)),
        "w_out": _layout(i["w_out"], (L, KT, P, D_MODEL), (0, 2, 1, 3)),
        "peer_wq": _layout(i["peer_wq"], (L, KT, P, 4, 512), (0, 3, 2, 1, 4)),
        "peer_keys": _layout(i["peer_keys"], (L, 2, PEER_HEADS, P, P), (0, 4, 2, 1, 3)).reshape(L, P, N_LISTS, P),
        "peer_u": _layout(i["peer_u"], (L, P, NG, EC, KT, P), (0, 2, 5, 3, 4, 1)),
        "peer_v": _layout(i["peer_v"], (L, P, P, D_MODEL), (0, 1, 2, 3)),
    }
    for n in ("ln1_g", "ln1_b", "ln2_g", "ln2_b"):
        arrays[n] = np.ascontiguousarray(i[n])

    nc = bacc.Bacc("TRN2", target_bir_lowering=False, num_devices=1)
    a = {n: nc.dram_tensor(f"{n}_dram", x.shape, mybir.dt.from_np(x.dtype), kind="ExternalInput").ap() for n, x in arrays.items()}
    a["gates"] = nc.dram_tensor("gates_scratch", (P, NTB, P, TB), F32, kind="Internal").ap()
    a["gate_logits"] = nc.dram_tensor("gate_logits_scratch", (GATES_AHEAD, P, SEQ), F32, kind="Internal").ap()
    a["hidden"] = nc.dram_tensor("hidden_scratch", (NG_AHEAD, P, EC, SEQ), F32, kind="Internal").ap()
    a["out"] = nc.dram_tensor("out_dram", (1, SEQ, D_MODEL), F32, kind="ExternalOutput").ap()
    build_program(nc, a)
    r = run_bass_kernel_spmd(nc, [{f"{n}_dram": x for n, x in arrays.items()}], core_ids=[0])
    return r.results[0]["out_dram"]
```
